# Optimizing a Trainium2 kernel written in Bass

```python
import math
import jax, jax.numpy as jnp
from jax import lax
import numpy as np

D_MODEL = 1024
BATCH = 1
SEQ = 256
DEPTH = 2

N_MIXERS = 2
N_MOBA = (DEPTH + 1) // 2
N_GDN = DEPTH // 2

MOBA_HEAD_DIM = 128
MOBA_HEADS = D_MODEL // MOBA_HEAD_DIM
MOBA_WIDTH = MOBA_HEADS * MOBA_HEAD_DIM
MOBA_BLOCK = 256
MOBA_TOP_K = 3
MOBA_Q_CHUNK = 64
MOBA_IN = 4 * MOBA_WIDTH

GDN_HEAD_DIM = 128
GDN_HEADS = D_MODEL // GDN_HEAD_DIM
GDN_WIDTH = GDN_HEADS * GDN_HEAD_DIM
GDN_CONV = 4
GDN_CHUNK = 64
GDN_IN = 4 * GDN_WIDTH + 2 * GDN_HEADS

DEEPNORM_ALPHA = (2.0 * DEPTH) ** 0.25
DEEPNORM_BETA = (8.0 * DEPTH) ** -0.25
LN_EPS = 1e-5
RMS_EPS = 1e-6
L2_EPS = 1e-6
ADA_INIT_SCALE = 0.1
NEG = -1e30


def layer_norm(x, g, b):
    xf = x.astype(jnp.float32)
    mu = jnp.mean(xf, axis=-1, keepdims=True)
    var = jnp.mean(jnp.square(xf - mu), axis=-1, keepdims=True)
    y = (xf - mu) * lax.rsqrt(var + LN_EPS)
    return (y * g.astype(jnp.float32) + b.astype(jnp.float32)).astype(x.dtype)

def l2_normalize(x):
    return x * lax.rsqrt(jnp.sum(jnp.square(x), axis=-1, keepdims=True) + L2_EPS)

def causal_depthwise_conv(u, w):
    k_w, ch = w.shape
    return lax.conv_general_dilated(
        u, w[:, None, :], window_strides=(1,), padding=[(k_w - 1, 0)],
        dimension_numbers=('NWC', 'WIO', 'NWC'), feature_group_count=ch)

def moba_attention(q, k, v):
    B, S, H, Dh = q.shape
    L = MOBA_BLOCK
    nb = -(-S // L)
    s_pad = nb * L
    pad = [(0, 0), (0, s_pad - S), (0, 0), (0, 0)]
    qh = jnp.pad(q, pad).transpose(0, 2, 1, 3)
    kb = jnp.pad(k, pad).transpose(0, 2, 1, 3).reshape(B, H, nb, L, Dh)
    vb = jnp.pad(v, pad).transpose(0, 2, 1, 3).reshape(B, H, nb, L, Dh)

    k_mean = jnp.mean(kb.astype(jnp.float32), axis=3)
    gate = jnp.einsum('bhsd,bhnd->bhsn', qh.astype(jnp.float32), k_mean)
    q_blk = jnp.arange(s_pad) // L
    cand = jnp.arange(nb)[None, :] < q_blk[:, None]
    gate = jnp.where(cand, gate, NEG)
    n_sel = max(1, min(MOBA_TOP_K, nb - 1))
    _, sel = lax.top_k(gate, n_sel)
    sel_valid = sel < q_blk[:, None]

    qc_n = MOBA_Q_CHUNK
    nqc = s_pad // qc_n
    cpb = L // qc_n

    def to_items(a):
        rest = a.shape[3:]
        a = jnp.moveaxis(a.reshape(B, H, nqc, qc_n, *rest), 2, 1)
        return a.reshape(B * nqc, H, qc_n, *rest)

    b_ids = jnp.repeat(jnp.arange(B, dtype=jnp.int32), nqc)
    c_ids = jnp.tile(jnp.arange(nqc, dtype=jnp.int32), B)
    scale = MOBA_HEAD_DIM ** -0.5
    h_idx = jnp.arange(H)[:, None, None]

    def attend(item):
        qc, selc, validc, b, ci = item
        kbb = kb[b]
        vbb = vb[b]
        kg = kbb[h_idx, selc]
        vg = vbb[h_idx, selc]
        blk = ci // cpb
        k_own = lax.dynamic_index_in_dim(kbb, blk, axis=1, keepdims=False)
        v_own = lax.dynamic_index_in_dim(vbb, blk, axis=1, keepdims=False)
        s_sel = jnp.einsum('hqd,hqnld->hqnl', qc, kg).astype(jnp.float32) * scale
        s_sel = jnp.where(validc[..., None], s_sel, NEG)
        s_own = jnp.einsum('hqd,hld->hql', qc, k_own).astype(jnp.float32) * scale
        q_pos = (ci % cpb) * qc_n + jnp.arange(qc_n)
        causal = jnp.arange(L)[None, :] <= q_pos[:, None]
        s_own = jnp.where(causal, s_own, NEG)
        s_all = jnp.concatenate([s_sel.reshape(H, qc_n, n_sel * L), s_own], axis=-1)
        p = jax.nn.softmax(s_all, axis=-1).astype(v.dtype)
        p_sel = p[..., :n_sel * L].reshape(H, qc_n, n_sel, L)
        p_own = p[..., n_sel * L:]
        return (jnp.einsum('hqnl,hqnld->hqd', p_sel, vg)
                + jnp.einsum('hql,hld->hqd', p_own, v_own))

    out = lax.map(attend, (to_items(qh), to_items(sel), to_items(sel_valid), b_ids, c_ids))
    out = out.reshape(B, nqc, H, qc_n, Dh).transpose(0, 1, 3, 2, 4).reshape(B, s_pad, H, Dh)
    return out[:, :S]

def chunk_gated_delta_rule(q, k, v, g, beta):
    B, S, H, Dk = q.shape
    Dv = v.shape[-1]
    C = GDN_CHUNK
    n = S // C

    def blk(a):
        return jnp.moveaxis(a.reshape(B, n, C, H, *a.shape[3:]), 3, 1)

    q = blk(q * (Dk ** -0.5))
    k = blk(k)
    v = blk(v)
    g = blk(g)
    beta = blk(beta)
    g_cum = jnp.cumsum(g, axis=-1)
    idx = jnp.arange(C)
    incl = idx[:, None] >= idx[None, :]
    strict = idx[:, None] > idx[None, :]
    diff = g_cum[..., :, None] - g_cum[..., None, :]
    decay_incl = jnp.exp(jnp.where(incl, diff, NEG))
    decay_strict = jnp.where(strict, decay_incl, 0.0)

    k_beta = k * beta[..., None]
    lmat = jnp.einsum('bhncd,bhnjd->bhncj', k_beta, k) * decay_strict
    a_mat = lmat + jnp.eye(C, dtype=lmat.dtype)
    rhs = jnp.concatenate([v * beta[..., None], k_beta * jnp.exp(g_cum)[..., None]], axis=-1)
    sol = lax.linalg.triangular_solve(a_mat, rhs, left_side=True, lower=True, unit_diagonal=True)
    u = sol[..., :Dv]
    w = sol[..., Dv:]
    a_qk = jnp.einsum('bhncd,bhnjd->bhncj', q, k) * decay_incl

    xs = tuple(jnp.moveaxis(t, 2, 0) for t in (q, k, u, w, g_cum, a_qk))

    def step(state, inp):
        qi, ki, ui, wi, gi, aqk = inp
        v_new = ui - jnp.einsum('bhcd,bhde->bhce', wi, state)
        o = (jnp.einsum('bhcd,bhde->bhce', qi * jnp.exp(gi)[..., None], state)
             + jnp.einsum('bhcj,bhje->bhce', aqk, v_new))
        g_last = gi[..., -1]
        k_dec = ki * jnp.exp(g_last[..., None] - gi)[..., None]
        state = state * jnp.exp(g_last)[..., None, None] + jnp.einsum('bhcd,bhce->bhde', k_dec, v_new)
        return state, o

    s0 = jnp.zeros((B, H, Dk, Dv), jnp.float32)
    _, o = lax.scan(step, s0, xs)
    o = jnp.moveaxis(o, 0, 2)
    return jnp.moveaxis(o, 1, 3).reshape(B, S, H, Dv)

def moba_branch(h, w_in, w_out):
    B, S, _ = h.shape
    proj = h @ w_in
    q, k, v, z = jnp.split(proj, [MOBA_WIDTH, 2 * MOBA_WIDTH, 3 * MOBA_WIDTH], axis=-1)
    shp = (B, S, MOBA_HEADS, MOBA_HEAD_DIM)
    o = moba_attention(q.reshape(shp), k.reshape(shp), v.reshape(shp))
    o = o.reshape(B, S, MOBA_WIDTH) * jax.nn.silu(z)
    return o @ w_out

def gdn_branch(h, w_in, conv_w, a_log, dt_bias, norm_w, w_out):
    B, S, _ = h.shape
    W = GDN_WIDTH
    proj = h @ w_in
    qkv = proj[..., :3 * W].astype(jnp.float32)
    z = proj[..., 3 * W:4 * W].astype(jnp.float32)
    a = proj[..., 4 * W:4 * W + GDN_HEADS].astype(jnp.float32)
    bt = proj[..., 4 * W + GDN_HEADS:].astype(jnp.float32)
    qkv = jax.nn.silu(causal_depthwise_conv(qkv, conv_w.astype(jnp.float32)))
    shp = (B, S, GDN_HEADS, GDN_HEAD_DIM)
    q = l2_normalize(qkv[..., :W].reshape(shp))
    k = l2_normalize(qkv[..., W:2 * W].reshape(shp))
    v = qkv[..., 2 * W:].reshape(shp)
    g = -jnp.exp(a_log.astype(jnp.float32)) * jax.nn.softplus(a + dt_bias.astype(jnp.float32))
    beta = jax.nn.sigmoid(bt)
    o = chunk_gated_delta_rule(q, k, v, g, beta)
    o = o * lax.rsqrt(jnp.mean(jnp.square(o), axis=-1, keepdims=True) + RMS_EPS)
    o = o * norm_w.astype(jnp.float32) * jax.nn.silu(z.reshape(shp))
    return o.reshape(B, S, W).astype(h.dtype) @ w_out

def first_inputs(seed: int = 0) -> dict:
    key = jax.random.key(seed)
    ks = jax.random.split(key, 16)
    f32 = jnp.float32
    x = jax.random.normal(ks[0], (BATCH, SEQ, D_MODEL), f32)
    c = jax.random.normal(ks[1], (BATCH, D_MODEL), f32)
    ada_w = jax.random.normal(ks[2], (DEPTH, D_MODEL, 3 * D_MODEL), f32) * (ADA_INIT_SCALE * D_MODEL ** -0.5)
    ada_base = jnp.concatenate([jnp.zeros((2 * D_MODEL,), f32), jnp.ones((D_MODEL,), f32)])
    ada_b = ada_base[None, :] + 0.01 * jax.random.normal(ks[3], (DEPTH, 3 * D_MODEL), f32)
    ln_g = 1.0 + 0.01 * jax.random.normal(ks[4], (DEPTH, D_MODEL), f32)
    ln_b = 0.01 * jax.random.normal(ks[5], (DEPTH, D_MODEL), f32)
    moba_w_in = jax.random.normal(ks[6], (N_MOBA, D_MODEL, MOBA_IN), f32) * D_MODEL ** -0.5
    moba_w_out = jax.random.normal(ks[7], (N_MOBA, MOBA_WIDTH, D_MODEL), f32) * (MOBA_WIDTH ** -0.5 * DEEPNORM_BETA)
    gdn_w_in = jax.random.normal(ks[8], (N_GDN, D_MODEL, GDN_IN), f32) * D_MODEL ** -0.5
    gdn_conv_w = jax.random.normal(ks[9], (N_GDN, GDN_CONV, 3 * GDN_WIDTH), f32) * GDN_CONV ** -0.5
    gdn_a_log = jnp.log(jax.random.uniform(ks[10], (N_GDN, GDN_HEADS), f32, 1.0, 16.0))
    dt = jnp.exp(jax.random.uniform(ks[11], (N_GDN, GDN_HEADS), f32, math.log(1e-3), math.log(1e-1)))
    gdn_dt_bias = dt + jnp.log(-jnp.expm1(-dt))
    gdn_norm_w = 1.0 + 0.01 * jax.random.normal(ks[12], (N_GDN, GDN_HEAD_DIM), f32)
    gdn_w_out = jax.random.normal(ks[13], (N_GDN, GDN_WIDTH, D_MODEL), f32) * (GDN_WIDTH ** -0.5 * DEEPNORM_BETA)
    return {"x": x, "c": c, "ada_w": ada_w, "ada_b": ada_b, "ln_g": ln_g, "ln_b": ln_b,
            "moba_w_in": moba_w_in, "moba_w_out": moba_w_out,
            "gdn_w_in": gdn_w_in, "gdn_conv_w": gdn_conv_w, "gdn_a_log": gdn_a_log,
            "gdn_dt_bias": gdn_dt_bias, "gdn_norm_w": gdn_norm_w, "gdn_w_out": gdn_w_out}

def first_block(x, c, ada_w, ada_b, ln_g, ln_b, moba_w_in, moba_w_out,
              gdn_w_in, gdn_conv_w, gdn_a_log, gdn_dt_bias, gdn_norm_w, gdn_w_out):
    cs = jax.nn.silu(c)
    for i in range(DEPTH):
        mod = cs @ ada_w[i] + ada_b[i]
        shift, scale, gate = jnp.split(mod, 3, axis=-1)
        h = x * (1.0 + scale[:, None, :]) + shift[:, None, :]
        j = i // N_MIXERS
        if i % N_MIXERS == 0:
            y = moba_branch(h, moba_w_in[j], moba_w_out[j])
        else:
            y = gdn_branch(h, gdn_w_in[j], gdn_conv_w[j], gdn_a_log[j], gdn_dt_bias[j],
                           gdn_norm_w[j], gdn_w_out[j])
        x = layer_norm(DEEPNORM_ALPHA * x + gate[:, None, :] * y, ln_g[i], ln_b[i])
    return x


DEPTH_2 = 1

F32 = jnp.float32
EPS = 1e-6
MEM_LEN = 256
GRID_W = 64
CONV_W = 3
ML_HEADS = 4
ML_HEAD_DIM = 128
ML_WIDTH = ML_HEADS * ML_HEAD_DIM
ML_CHUNK = 64
NA_HEADS = 8
NA_HEAD_DIM = 64
NA_WIDTH = NA_HEADS * NA_HEAD_DIM
NA_WIN_ROWS_MAX = 8
NA_WIN_COLS = 16
XA_HEADS = 4
XA_HEAD_DIM = 128
XA_WIDTH = XA_HEADS * XA_HEAD_DIM
N_BRANCHES = 3
D_FF = 2816
IN_SPLITS = (ML_WIDTH, ML_WIDTH, ML_WIDTH, ML_WIDTH, 4 * ML_HEADS, 3 * NA_WIDTH, XA_WIDTH, N_BRANCHES * D_MODEL)
IN_WIDTH = sum(IN_SPLITS)
NEG_INIT = -1e30


def rms_norm(x, g):
    xf = x.astype(F32)
    y = xf * lax.rsqrt(jnp.mean(xf * xf, axis=-1, keepdims=True) + EPS)
    return (y * g.astype(F32)).astype(x.dtype)

def dwconv3(x, w, b):
    xp = jnp.pad(x, ((0, 0), (1, 1), (0, 0)))
    return xp[:, :-2] * w[0] + xp[:, 1:-1] * w[1] + xp[:, 2:] * w[2] + b

def mlstm_chunkwise(q, k, v, i_pre, f_pre):
    B, H, S, Dh = q.shape
    L = ML_CHUNK
    NC = S // L
    q = q.astype(F32).reshape(B, H, NC, L, Dh) * (Dh ** -0.5)
    k = k.astype(F32).reshape(B, H, NC, L, Dh)
    v = v.astype(F32).reshape(B, H, NC, L, Dh)
    log_f = jax.nn.log_sigmoid(f_pre.astype(F32)).reshape(B, H, NC, L)
    log_i = i_pre.astype(F32).reshape(B, H, NC, L)
    a = jnp.cumsum(log_f, axis=-1)
    g = a[..., -1]
    w_end = g[..., None] - a + log_i
    m_end = jnp.max(w_end, axis=-1)

    def step(carry, xs):
        C, n, m = carry
        k_c, v_c, w_c, mw_c, g_c = xs
        m_new = jnp.maximum(g_c + m, mw_c)
        decay = jnp.exp(g_c + m - m_new)
        wt = jnp.exp(w_c - m_new[..., None])
        C_new = decay[..., None, None] * C + jnp.einsum('bhl,bhld,bhle->bhde', wt, v_c, k_c)
        n_new = decay[..., None] * n + jnp.einsum('bhl,bhle->bhe', wt, k_c)
        return (C_new, n_new, m_new), (C, n, m)

    init = (jnp.zeros((B, H, Dh, Dh), F32), jnp.zeros((B, H, Dh), F32), jnp.full((B, H), NEG_INIT, F32))
    xs = (jnp.moveaxis(k, 2, 0), jnp.moveaxis(v, 2, 0), jnp.moveaxis(w_end, 2, 0),
          jnp.moveaxis(m_end, 2, 0), jnp.moveaxis(g, 2, 0))
    _, (C_prev, n_prev, m_prev) = lax.scan(step, init, xs)
    C_prev = jnp.moveaxis(C_prev, 0, 2)
    n_prev = jnp.moveaxis(n_prev, 0, 2)
    m_prev = jnp.moveaxis(m_prev, 0, 2)

    causal = jnp.tril(jnp.ones((L, L), dtype=bool))
    D = a[..., :, None] - a[..., None, :] + log_i[..., None, :]
    D = jnp.where(causal, D, -jnp.inf)
    inter_log = a + m_prev[..., None]
    m_j = jnp.maximum(inter_log, jnp.max(D, axis=-1))
    qk = jnp.einsum('bhcjd,bhcsd->bhcjs', q, k)
    P = jnp.exp(D - m_j[..., None]) * qk
    inter_w = jnp.exp(inter_log - m_j)
    num = jnp.einsum('bhcjs,bhcsd->bhcjd', P, v) + inter_w[..., None] * jnp.einsum('bhcde,bhcje->bhcjd', C_prev, q)
    den = jnp.sum(P, axis=-1) + inter_w * jnp.einsum('bhce,bhcje->bhcj', n_prev, q)
    h = num / jnp.maximum(jnp.abs(den), jnp.exp(-m_j))[..., None]
    return h.reshape(B, H, S, Dh)

def mlstm_branch(q_pre, k_pre, v, o_pre, gates, w_conv, b_conv, b_ig, b_fg, norm_g):
    B, S, _ = q_pre.shape
    qk = jax.nn.silu(dwconv3(jnp.concatenate([q_pre, k_pre], axis=-1), w_conv, b_conv))
    q, k = jnp.split(qk, 2, axis=-1)
    heads = lambda t: t.reshape(B, S, ML_HEADS, ML_HEAD_DIM).transpose(0, 2, 1, 3)
    qh, kh, vh = heads(q), heads(k), heads(v)
    gt = gates.astype(F32).reshape(B, S, 4, ML_HEADS).transpose(2, 0, 3, 1)
    b_ig = b_ig.astype(F32)
    b_fg = b_fg.astype(F32)
    i_fw = gt[0] + b_ig[0][None, :, None]
    f_fw = gt[1] + b_fg[0][None, :, None]
    i_bw = gt[2] + b_ig[1][None, :, None]
    f_bw = gt[3] + b_fg[1][None, :, None]
    h_fw = mlstm_chunkwise(qh, kh, vh, i_fw, f_fw)
    flip = lambda t: jnp.flip(t, axis=2)
    h_bw = flip(mlstm_chunkwise(flip(qh), flip(kh), flip(vh), flip(i_bw), flip(f_bw)))
    h = h_fw + h_bw
    h = h * lax.rsqrt(jnp.mean(h * h, axis=-1, keepdims=True) + EPS)
    h = h * norm_g.astype(F32).reshape(ML_HEADS, 1, ML_HEAD_DIM)
    h = h.transpose(0, 2, 1, 3).reshape(B, S, ML_WIDTH)
    return (jax.nn.sigmoid(o_pre.astype(F32)) * h).astype(q_pre.dtype)

def neighbourhood_attention(q, k, v, rpb):
    B, S, _ = q.shape
    rows = S // GRID_W
    kr = min(NA_WIN_ROWS_MAX, rows)
    grid = lambda t: t.reshape(B, rows, GRID_W, NA_HEADS, NA_HEAD_DIM).transpose(0, 3, 1, 2, 4)
    qg, kg, vg = grid(q).astype(F32), grid(k), grid(v)
    r = jnp.arange(rows)
    row_start = jnp.clip(r - kr // 2, 0, rows - kr)
    row_idx = row_start[:, None] + jnp.arange(kr)[None, :]
    k_band = kg[:, :, row_idx].astype(F32)
    v_band = vg[:, :, row_idx].astype(F32)
    c = jnp.arange(GRID_W)
    col_start = jnp.clip(c - NA_WIN_COLS // 2, 0, GRID_W - NA_WIN_COLS)
    col_ok = (c[None, :] >= col_start[:, None]) & (c[None, :] < col_start[:, None] + NA_WIN_COLS)
    dr = row_idx - r[:, None] + (NA_WIN_ROWS_MAX - 1)
    dc = jnp.clip(c[None, :] - c[:, None] + (NA_WIN_COLS - 1), 0, 2 * NA_WIN_COLS - 2)
    bias = rpb.astype(F32)[:, dr[:, None, :, None], dc[None, :, None, :]]
    s = jnp.einsum('bhrcd,bhrkjd->bhrckj', qg, k_band) * (NA_HEAD_DIM ** -0.5) + bias[None]
    s = jnp.where(col_ok[None, None, None, :, None, :], s, -jnp.inf)
    p = jax.nn.softmax(s.reshape(B, NA_HEADS, rows, GRID_W, kr * GRID_W), axis=-1).reshape(s.shape)
    o = jnp.einsum('bhrckj,bhrkjd->bhrcd', p, v_band)
    return o.transpose(0, 2, 3, 1, 4).reshape(B, S, NA_WIDTH).astype(q.dtype)

def memory_cross_attention(q, mem_k, mem_v):
    B, S, _ = q.shape
    M = mem_k.shape[1]
    qh = q.reshape(B, S, XA_HEADS, XA_HEAD_DIM).astype(F32)
    kh = mem_k.reshape(B, M, XA_HEADS, XA_HEAD_DIM).astype(F32)
    vh = mem_v.reshape(B, M, XA_HEADS, XA_HEAD_DIM).astype(F32)
    s = jnp.einsum('bshd,bmhd->bhsm', qh, kh) * (XA_HEAD_DIM ** -0.5)
    p = jax.nn.softmax(s, axis=-1)
    o = jnp.einsum('bhsm,bmhd->bshd', p, vh)
    return o.reshape(B, S, XA_WIDTH).astype(q.dtype)

def conv_glu_ffn(h, w_up, w_conv, b_conv, w_down):
    a, u = jnp.split(h @ w_up, 2, axis=-1)
    return (jax.nn.gelu(dwconv3(a, w_conv, b_conv)) * u) @ w_down

def second_inputs(seed: int = 0) -> dict:
    key = jax.random.key(seed)
    ks = jax.random.split(key, 24)

    def dense(k, shape, fan_in):
        return jax.random.normal(k, shape, F32) * (fan_in ** -0.5)

    def gain(k, shape):
        return 1.0 + 0.05 * jax.random.normal(k, shape, F32)

    def small(k, shape, scale):
        return scale * jax.random.normal(k, shape, F32)

    L = DEPTH_2
    return {
        "x": jax.random.normal(ks[0], (BATCH, SEQ, D_MODEL), F32),
        "mem": jax.random.normal(ks[1], (BATCH, MEM_LEN, D_MODEL), F32),
        "mix_norm_g": gain(ks[2], (L, D_MODEL)),
        "w_in": dense(ks[3], (L, D_MODEL, IN_WIDTH), D_MODEL),
        "b_ml_igate": small(ks[4], (L, 2, ML_HEADS), 0.1),
        "b_ml_fgate": jnp.linspace(3.0, 6.0, ML_HEADS, dtype=F32) + small(ks[5], (L, 2, ML_HEADS), 0.1),
        "w_ml_conv": dense(ks[6], (L, CONV_W, 2 * ML_WIDTH), CONV_W),
        "b_ml_conv": small(ks[7], (L, 2 * ML_WIDTH), 0.02),
        "ml_norm_g": gain(ks[8], (L, ML_WIDTH)),
        "na_rpb": small(ks[9], (L, NA_HEADS, 2 * NA_WIN_ROWS_MAX - 1, 2 * NA_WIN_COLS - 1), 0.1),
        "mem_norm_g": gain(ks[10], (L, D_MODEL)),
        "w_mem_kv": dense(ks[11], (L, D_MODEL, 2 * XA_WIDTH), D_MODEL),
        "b_merge_gate": small(ks[12], (L, N_BRANCHES * D_MODEL), 0.02),
        "w_br_ml": dense(ks[13], (L, ML_WIDTH, D_MODEL), ML_WIDTH),
        "w_br_na": dense(ks[14], (L, NA_WIDTH, D_MODEL), NA_WIDTH),
        "w_br_xa": dense(ks[15], (L, XA_WIDTH, D_MODEL), XA_WIDTH),
        "w_out": dense(ks[16], (L, D_MODEL, D_MODEL), D_MODEL),
        "ffn_norm_g": gain(ks[17], (L, D_MODEL)),
        "w_ffn_up": dense(ks[18], (L, D_MODEL, 2 * D_FF), D_MODEL),
        "w_ffn_conv": dense(ks[19], (L, CONV_W, D_FF), CONV_W),
        "b_ffn_conv": small(ks[20], (L, D_FF), 0.02),
        "w_ffn_down": dense(ks[21], (L, D_FF, D_MODEL), D_FF),
        "final_norm_g": gain(ks[22], (D_MODEL,)),
    }

def second_block(x, mem, mix_norm_g, w_in, b_ml_igate, b_ml_fgate, w_ml_conv, b_ml_conv, ml_norm_g,
              na_rpb, mem_norm_g, w_mem_kv, b_merge_gate, w_br_ml, w_br_na, w_br_xa, w_out,
              ffn_norm_g, w_ffn_up, w_ffn_conv, b_ffn_conv, w_ffn_down, final_norm_g):
    split_points = [int(p) for p in np.cumsum(IN_SPLITS)[:-1]]
    for l in range(DEPTH_2):
        h = rms_norm(x, mix_norm_g[l])
        proj = h @ w_in[l]
        ml_q, ml_k, ml_v, ml_o, ml_gates, na_qkv, xa_q, merge_pre = jnp.split(proj, split_points, axis=-1)
        y_ml = mlstm_branch(ml_q, ml_k, ml_v, ml_o, ml_gates, w_ml_conv[l], b_ml_conv[l],
                            b_ml_igate[l], b_ml_fgate[l], ml_norm_g[l])
        na_q, na_k, na_v = jnp.split(na_qkv, 3, axis=-1)
        y_na = neighbourhood_attention(na_q, na_k, na_v, na_rpb[l])
        mem_k, mem_v = jnp.split(rms_norm(mem, mem_norm_g[l]) @ w_mem_kv[l], 2, axis=-1)
        y_xa = memory_cross_attention(xa_q, mem_k, mem_v)
        gates = jax.nn.sigmoid((merge_pre + b_merge_gate[l]).astype(F32)).astype(x.dtype)
        g_ml, g_na, g_xa = jnp.split(gates, N_BRANCHES, axis=-1)
        merged = g_ml * (y_ml @ w_br_ml[l]) + g_na * (y_na @ w_br_na[l]) + g_xa * (y_xa @ w_br_xa[l])
        x = x + merged @ w_out[l]
        x = x + conv_glu_ffn(rms_norm(x, ffn_norm_g[l]), w_ffn_up[l], w_ffn_conv[l], b_ffn_conv[l], w_ffn_down[l])
    return rms_norm(x, final_norm_g)


def setup_inputs(seed=0):
    out = dict(first_inputs(seed))
    for name, value in second_inputs(seed + 1).items():
        if name != "x":
            out[name + "_2"] = value
    return out


def reference(
    x, c, ada_w, ada_b, ln_g, ln_b, moba_w_in, moba_w_out, gdn_w_in, gdn_conv_w, gdn_a_log,
    gdn_dt_bias, gdn_norm_w, gdn_w_out, mem_2, mix_norm_g_2, w_in_2, b_ml_igate_2, b_ml_fgate_2,
    w_ml_conv_2, b_ml_conv_2, ml_norm_g_2, na_rpb_2, mem_norm_g_2, w_mem_kv_2, b_merge_gate_2,
    w_br_ml_2, w_br_na_2, w_br_xa_2, w_out_2, ffn_norm_g_2, w_ffn_up_2, w_ffn_conv_2,
    b_ffn_conv_2, w_ffn_down_2, final_norm_g_2,
):
    x = first_block(
        x, c, ada_w, ada_b, ln_g, ln_b, moba_w_in, moba_w_out, gdn_w_in, gdn_conv_w, gdn_a_log,
        gdn_dt_bias, gdn_norm_w, gdn_w_out,
    )
    return second_block(
        x, mem_2, mix_norm_g_2, w_in_2, b_ml_igate_2, b_ml_fgate_2, w_ml_conv_2, b_ml_conv_2,
        ml_norm_g_2, na_rpb_2, mem_norm_g_2, w_mem_kv_2, b_merge_gate_2, w_br_ml_2, w_br_na_2,
        w_br_xa_2, w_out_2, ffn_norm_g_2, w_ffn_up_2, w_ffn_conv_2, b_ffn_conv_2, w_ffn_down_2,
        final_norm_g_2,
    )


_drawn_inputs = setup_inputs


def setup_inputs(seed=0):
    import zlib

    import numpy as np

    out = dict(_drawn_inputs(seed))
    spreads = {}
    factors = {'ln_g': 3.083,
     'gdn_norm_w': 25.836,
     'b_ml_igate_2': 64.0,
     'b_ml_conv_2': 21.582,
     'ml_norm_g_2': 19.131,
     'na_rpb_2': 28.637,
     'mem_norm_g_2': 8.0,
     'b_merge_gate_2': 8.0,
     'b_ffn_conv_2': 20.674,
     'ln_b': 4.091,
     'ffn_norm_g_2': 5.72}
    for name, (base, spread) in spreads.items():
        noise = np.random.default_rng([zlib.crc32(name.encode()), seed]).standard_normal(out[name].shape)
        drawn = base * np.exp(spread * noise) if base else spread * noise
        out[name] = __import__('jax').numpy.asarray(drawn.astype(out[name].dtype))
    for name, factor in factors.items():
        out[name] = (out[name] * factor).astype(out[name].dtype)
    return out
```

```python
from contextlib import ExitStack

import numpy as np
import concourse.bass as bass
from concourse import mybir

F32 = mybir.dt.float32
F32R = mybir.dt.float32r
ALU = mybir.AluOpType
ACT = mybir.ActivationFunctionType
X = mybir.AxisListType.X

P = 128
D = 1024
KT = D // P
S = 256
NEG = -1e30
DEPTH = 2
ALPHA = (2.0 * DEPTH) ** 0.25
LN_EPS = 1e-5
EPS = 1e-6
FF = 2816
FT = FF // P
UNIT = 8
GROUP = 4
RAW = 2
LEVELS = 7

STAGES = [("ada0", 24), ("moba_in", 32), ("ada1", 24), ("moba_out", 8), ("gdn_in", 32), ("gdn_out", 8),
          ("mem_kv", 8), ("w_in", 32), ("merge", 24), ("branch", 12), ("w_out", 8), ("ffn_up", 44),
          ("ffn_down", 24)]
FIRST = {}
_n = 0
for _name, _count in STAGES:
    FIRST[_name] = _n
    _n += _count
UNITS = _n
COUNT = dict(STAGES)

PARAMS = [("c", 8), ("ada_b", 48), ("ln_g", 16), ("ln_b", 16), ("gdn_conv", 96), ("gdn_norm", 1),
          ("ml_conv", 24), ("ml_conv_b", 8), ("ml_norm", 4), ("mix_norm", 8), ("mem_norm", 8),
          ("merge_b", 24), ("ffn_norm", 8), ("ffn_conv", 66), ("ffn_conv_b", 22), ("final_norm", 8),
          ("a_log", 1), ("dt_bias", 1), ("b_ig", 1), ("b_fg", 1)]
PCOL = {}
_n = 0
for _name, _count in PARAMS:
    PCOL[_name] = _n
    _n += _count
NPARAM = _n

CONSTS = [("ident", P), ("fw", 3 * P), ("bw", 3 * P), ("neg", 3 * P), ("level", LEVELS * P), ("colmask", S)]
CCOL = {}
_n = 0
for _name, _count in CONSTS:
    CCOL[_name] = _n
    _n += _count
NCONST = _n
ML_ROWS = 36


def build(nc, io):
    ctx = ExitStack()
    with ctx:
        _program(nc, io, ctx)


def _program(nc, io, ctx):
    def sb(name, shape, dt=F32):
        return ctx.enter_context(nc.sbuf_tensor(name, shape, dt))

    turns = {
        ("_res",): [("ln0", KT), ("ln1", KT), ("ffn", KT), ("final", KT)],
        ("_sum",): [("ln0", 1), ("ln1", 1)],
        ("_root", "_sumsq"): [("ln0", 1), ("ln1", 1), ("mem", 1), ("mix", 1), ("ffn", 1), ("final", 1)],
        ("_sq",): [(n, KT) for n in ("ln0", "ln1", "mem", "mix", "ffn", "final")],
        ("_centred", "_scaled", "_x"): [("ln0", KT), ("ln1", KT)],
        ("_scores", "_logits", "_max", "_probs", "_turned_p", "_pt", "_pv", "_out"):
            [("moba", 8), ("na", 8), ("xa", 4)],
        ("_exp",): [("moba", 16), ("na", 16), ("xa", 8)],
        ("_high",): [("na", 8), ("xa", 4)],
        ("_turned", "_natural"): [("moba_v", 4), ("mem_v", 2), ("ml_v", 2), ("na_v", 2)],
        ("_hi", "_lo"): [(f"in{n}", KT) for n in range(6)] + [("in6m", 4), ("in7", KT), ("in8", KT), ("in9", FT)],
    }
    shared, start = {}, {}
    for kinds, order in turns.items():
        for kind in kinds:
            at = 0
            for tag, n in order:
                shared[tag + kind], start[tag + kind] = "turn" + kind, at
                at += n

    sems = {}

    def sem(name):
        name = shared.get(name, name)
        if name not in sems:
            sems[name] = ctx.enter_context(nc.semaphore(name))
        return sems[name]

    def after(name, n):
        return sem(name), n + start.get(name, 0)

    raw = sb("raw", [P, RAW, GROUP * UNIT * P])
    w_hi = sb("w_hi", [P, GROUP, UNIT * P], F32R)
    w_lo = sb("w_lo", [P, GROUP, UNIT * P], F32R)
    in_hi = sb("in_hi", [P, FT, S], F32R)
    in_lo = sb("in_lo", [P, FT, S], F32R)
    x_t = sb("x_t", [P, KT, S])
    proj = sb("proj", [P, 32, S])
    params = sb("params", [P, NPARAM])
    consts = sb("consts", [P, NCONST])
    gdn_wg = sb("gdn_wg", [P, KT, 16])
    ml_wg = sb("ml_wg", [P, KT, 2 * ML_ROWS])
    cs = sb("cs", [P, KT])
    cs_hi = sb("cs_hi", [P, KT, 2], F32R)
    cs_lo = sb("cs_lo", [P, KT, 2], F32R)
    mod2 = sb("mod2", [P, 24, 2])
    mod = sb("mod", [P, 2, 24])
    stat = sb("stat", [P, 2, S])
    rows = sb("rows", [ML_ROWS, 6, S])
    gcol = sb("gcol", [P, 2, 2, 8])
    gexp = sb("gexp", [P, 3, 8])
    mcol = sb("mcol", [P, 2, 2, ML_ROWS])
    small = sb("small", [P, 2, 16])
    work = sb("work", [P, 5 * 1024])
    memkv = sb("memkv", [P, 8, S])
    mem_vnat = sb("mem_vnat", [P, 2, 4 * P])

    ps = ctx.enter_context(nc.psum_tensor("ps", [P, 8, 512], F32))

    def area(at, *shape, of=work):
        v = of[:, at:at + int(np.prod(shape))]
        return v.rearrange("p (a b) -> p a b", a=shape[0]) if len(shape) == 2 else v

    sq = area(0, KT, S)
    h_t = area(2048, KT, S)
    vnat = area(0, 2, D)
    lg = [area(2048, 2, S), area(2560, 2, S)]
    pt = area(3072, 2, S)
    gated = [area(3584, S), area(3840, S)]
    bias = [area(4096, 2, S), area(4608, 2, S)]
    cin = [area((S + 3) * u, S + 3) for u in range(GROUP)]
    fbuf = [area(2048 + 512 * u, 2, S) for u in range(2)]
    eb = area(2048, 4, S)
    wsum = area(3584, 2, S)
    gsq = area(4096, 4, S)
    rb = area(1024, 4, S)
    ctm, pm, lt, aqk = (area(512 * n, 4, P) for n in range(4))
    dec, kdg, vb = (area(2048 + 512 * n, 4, P) for n in range(3))
    kb = area(3584, 2, S)
    qg = area(4096, 2, P)
    u0, s1, wn, v1 = (area(4352 + P * n, P) for n in range(4))
    tm, ttm = (memkv[:, 2 * n:2 * n + 2, :].rearrange("p a (c b) -> p (a c) b", c=2) for n in range(2))

    ident = consts[:, CCOL["ident"]:CCOL["ident"] + P]
    ones = consts[:, CCOL["fw"]:CCOL["fw"] + P]

    def param(name, k=0, n=1, rows_=P):
        return params[0:rows_, PCOL[name] + k:PCOL[name] + k + n]

    def strip(name, qt):
        a = CCOL[name] + P * (1 - qt)
        return consts[:, a:a + S]

    def half(bank, k):
        return ps[:, bank, k * S:(k + 1) * S]

    def flat(t):
        return t.rearrange("p a b -> p (a b)")

    loaded, hi_done, lo_done, unit_done, taken = (sem(n) for n in
        ("group_loaded", "unit_hi", "unit_lo", "unit_multiplied", "bank_taken"))

    def all_taken(name, n=None):
        return GROUP + FIRST[name] + (COUNT[name] if n is None else n)

    block = ctx.enter_context(nc.Block())

    @block.sync
    def _(sp):
        sp.dma_start(params[:], io["params"]).then_inc(sem("params_in"), 16)
        sp.dma_start(consts[:], io["consts"]).then_inc(sem("consts_in"), 16)
        sp.dma_start(x_t[:], io["x_t"]).then_inc(sem("x_in"), 16)
        sp.dma_start(gdn_wg[:], io["gdn_wg"]).then_inc(sem("gate_w_in"), 16)
        sp.dma_start(ml_wg[:], io["ml_wg"]).then_inc(sem("gate_w_in"), 16)
        g = 0
        for name, units in STAGES:
            for j in range(units // GROUP):
                if g >= RAW:
                    sp.wait_ge(lo_done, GROUP * (g - RAW + 1))
                sp.dma_start(raw[:, g % RAW, :], io[name][j]).then_inc(sem(f"slot_in{g % RAW}"), 16)
                if g >= 1:
                    sp.wait_ge(*after(f"slot_in{(g - 1) % RAW}", 16 * ((g - 1) // RAW + 1)))
                    sp.sem_inc(loaded, 1)
                g += 1
        sp.wait_ge(*after(f"slot_in{(g - 1) % RAW}", 16 * ((g - 1) // RAW + 1)))
        sp.sem_inc(loaded, 1)
        sp.wait_ge(*after("final_done", KT))
        sp.dma_start(io["out"], proj[:, 0:KT, :]).then_inc(sem("out_stored"), 16)
        sp.wait_ge(*after("out_stored", 16))

    @block.tensor
    def _(pe):
        def project(name, a_hi, a_lo, first_in=0, width=S):
            first = FIRST[name]
            with pe.Fori(0, COUNT[name] // GROUP) as i:
                for u in range(GROUP):
                    pe.wait_ge(lo_done, i * GROUP + (first + u + 1))
                    pe.wait_ge(taken, i * GROUP + (first + u + 1))
                    out = ps[:, u, 0:width]
                    for n, (w, a) in enumerate(((w_hi, a_hi), (w_hi, a_lo), (w_lo, a_hi))):
                        for k in range(UNIT):
                            mm = pe.matmul(out, w[:, u, k * P:(k + 1) * P], a[:, first_in + k, :],
                                           start=(n == 0 and k == 0), stop=(n == 2 and k == UNIT - 1))
                    mm.then_inc(unit_done, 1)

        def split_mm(out, u, blocks, start, stop):
            last = len(blocks) - 1
            for n, (w, a) in enumerate(((w_hi, in_hi), (w_hi, in_lo), (w_lo, in_hi))):
                for m, (b, k) in enumerate(blocks):
                    mm = pe.matmul(out, w[:, u, b * P:(b + 1) * P], a[:, k, :],
                                   start=start and n == 0 and m == 0, stop=stop and n == 2 and m == last)
            return mm

        def sum_tiles(out, src, ready, name, tiles=KT):
            for k in range(tiles):
                pe.wait_ge(*after(ready, k + 1))
                mm = pe.matmul(out, ones, src[:, k, :], start=(k == 0), stop=(k == tiles - 1))
            mm.then_inc(sem(name), 1)

        def transposes(src, tiles, banks, name, per_bank=2):
            for t in range(tiles):
                bank = banks[(t // 2) % len(banks)]
                if t % 2 == 0 and t // 2 >= len(banks):
                    pe.wait_ge(*after(f"{name}_natural", t // 2 - len(banks) + 1))
                for c in range(2):
                    mm = pe.transpose(ps[:, bank, (t % 2) * S + c * P:(t % 2) * S + (c + 1) * P],
                                      src[:, t, c * P:(c + 1) * P], ident)
                if t % 2 == 1:
                    mm.then_inc(sem(f"{name}_turned"), 1)

        def attention(name, heads, q, k, v):
            def scores(h):
                if h >= 2:
                    pe.wait_ge(*after(f"{name}_logits", h - 1))
                for qt in range(2):
                    qh = q(h)
                    mm = pe.matmul(half(4 + h % 2, qt), qh[:, qt * P:(qt + 1) * P], k(h), start=True, stop=True)
                mm.then_inc(sem(f"{name}_scores"), 1)

            scores(0)
            for h in range(heads):
                if h + 1 < heads:
                    scores(h + 1)
                pe.wait_ge(*after(f"{name}_probs", h + 1))
                if h >= 1:
                    pe.wait_ge(*after(f"{name}_pt", h))
                for qt in range(2):
                    for kt in range(2):
                        mm = pe.transpose(ps[:, 6, kt * S + qt * P:kt * S + (qt + 1) * P],
                                          lg[h % 2][:, qt, kt * P:(kt + 1) * P], ident)
                mm.then_inc(sem(f"{name}_turned_p"), 1)
                pe.wait_ge(*after(f"{name}_pt", h + 1))
                if h >= 1:
                    pe.wait_ge(*after(f"{name}_out", h))
                for kt in range(2):
                    vh = v(h, kt)
                    m = vh.shape[-1]
                    p0 = 64 * (h % 2) if m == 64 else 0
                    mm = pe.matmul(ps[p0:p0 + m, 7, 0:S], vh, pt[:, kt, :], start=(kt == 0), stop=(kt == 1))
                mm.then_inc(sem(f"{name}_pv"), 1)

        pe.wait_ge(*after("cs_split", 2))
        project("ada0", cs_hi, cs_lo, 0, 2)
        pe.wait_ge(*after("in0_lo", KT))
        project("moba_in", in_hi, in_lo)

        pe.wait_ge(taken, all_taken("moba_in"))
        transposes(proj[:, 16:24, :], 8, (4, 5, 6, 7), "moba_v")
        pe.wait_ge(*after("moba_v_natural", 4))
        attention("moba", 8, lambda h: proj[:, h, :], lambda h: proj[:, 8 + h, :],
                  lambda h, kt: vnat[:, kt, h * P:(h + 1) * P])
        project("ada1", cs_hi, cs_lo, 0, 2)
        pe.wait_ge(*after("in1_lo", KT))
        project("moba_out", in_hi, in_lo)

        def norm_sums(tag, centred):
            if centred:
                sum_tiles(half(4, 0), x_t, f"{tag}_res", f"{tag}_sum")
            sum_tiles(half(5, 0), sq, f"{tag}_sq", f"{tag}_sumsq")

        norm_sums("ln0", True)

        pe.wait_ge(*after("in2_lo", KT))
        for r in range(2):
            for k in range(KT):
                mm = pe.matmul(ps[0:8, 6 + r, 0:S], gdn_wg[:, k, 8 * r:8 * r + 8], h_t[:, k, :],
                               start=(k == 0), stop=(k == KT - 1))
        mm.then_inc(sem("gdn_gates"), 1)
        project("gdn_in", in_hi, in_lo)
        pe.wait_ge(*after("gdn_rows", 2))
        for n, r in enumerate((2, 3)):
            for c in range(2):
                mm = pe.transpose(ps[:, 6, (2 * n + c) * 8:(2 * n + c) * 8 + 8], rows[0:8, r, c * P:(c + 1) * P],
                                  ident[0:8, 0:8])
        mm.then_inc(sem("gdn_cols"), 1)
        for t in range(16):
            pe.wait_ge(*after("gdn_sq", t + 1))
            if t >= 4:
                pe.wait_ge(*after("gdn_len", t - 3))
            pe.matmul(half(t % 4, 0), ones, gsq[:, t % 4, :], start=True, stop=True).then_inc(sem("gdn_sum"), 1)
        pe.wait_ge(*after("gdn_unit", 16))
        for g in range(4):
            if g >= 1:
                pe.wait_ge(*after("gdn_o", 2 * g))
            for m in range(2):
                h = 2 * g + m
                sel = ident[0:8, h:h + 1].to_broadcast([8, P])
                pe.matmul(half(m, 0), sel, rows[0:8, 2, :], start=True, stop=True)
                mm = pe.matmul(half(m, 1), sel, rows[0:8, 3, :], start=True, stop=True)
            mm.then_inc(sem("gdn_bc"), 1)
            for m in range(2):
                h = 2 * g + m
                for c in range(2):
                    pe.transpose(ps[:, 2, (2 * m + c) * P:(2 * m + c + 1) * P], proj[:, 8 + h, c * P:(c + 1) * P], ident)
                    mm = pe.transpose(ps[:, 3, (2 * m + c) * P:(2 * m + c + 1) * P], proj[:, 16 + h, c * P:(c + 1) * P],
                                      ident)
            mm.then_inc(sem("gdn_nat"), 1)
            pe.wait_ge(*after("gdn_kb", 2 * (g + 1)))
            for m in range(2):
                h = 2 * g + m
                for c in range(2):
                    kk = proj[:, 8 + h, c * P:(c + 1) * P]
                    j = 2 * m + c
                    pe.matmul(ps[:, 4, j * P:(j + 1) * P], kk, kb[:, m, c * P:(c + 1) * P], start=True, stop=True)
                    mm = pe.matmul(ps[:, 5, j * P:(j + 1) * P], kk, proj[:, h, c * P:(c + 1) * P], start=True, stop=True)
            mm.then_inc(sem("gdn_gram"), 1)
            for lv in range(LEVELS):
                n = g * LEVELS + lv
                pe.wait_ge(*after("gdn_ct", n + 1))
                pe.wait_ge(*after("gdn_t", n + g + 1))
                for j in range(4):
                    pe_out = ps[:, 6, j * P:(j + 1) * P]
                    mm = pe.matmul(pe_out, ctm[:, j, :], tm[:, j, :], start=True, stop=True)
                mm.then_inc(sem("gdn_p"), 1)
                pe.wait_ge(*after("gdn_ps", n + 1))
                for j in range(4):
                    pe.matmul(ps[:, 7, j * P:(j + 1) * P], ttm[:, j, :], pm[:, j, :], start=True, stop=True)
                for j in range(4):
                    mm = pe.matmul(ps[:, 4, j * P:(j + 1) * P], pm[:, j, :], ttm[:, j, :], start=True, stop=True)
                mm.then_inc(sem("gdn_d"), 1)
            pe.wait_ge(*after("gdn_t", (g + 1) * (LEVELS + 1)))
            pe.wait_ge(*after("gdn_kdg", 4 * (g + 1)))
            pe.wait_ge(*after("gdn_vb", 4 * (g + 1)))
            pe.wait_ge(*after("gdn_aqk", g + 1))
            pe.wait_ge(*after("gdn_qg", g + 1))
            for m in range(2):
                h = 2 * g + m
                T0, T1 = ttm[:, 2 * m, :], ttm[:, 2 * m + 1, :]
                pe.matmul(ps[:, 6, 0:P], T0, vb[:, 2 * m, :], start=True, stop=True).then_inc(sem("gdn_u0"), 1)
                pe.matmul(ps[:, 7, 0:P], kdg[:, 2 * m + 1, :], T1, start=True, stop=True).then_inc(sem("gdn_w"), 1)
                pe.wait_ge(*after("gdn_u0s", h + 1))
                pe.matmul(ps[:, 5, 0:P], kdg[:, 2 * m, :], u0, start=True, stop=True).then_inc(sem("gdn_s1"), 1)
                pe.wait_ge(*after("gdn_s1s", h + 1))
                pe.wait_ge(*after("gdn_ws", h + 1))
                pe.matmul(ps[:, 4, 0:P], T1, vb[:, 2 * m + 1, :], start=True, stop=False)
                pe.matmul(ps[:, 4, 0:P], wn, s1, start=False, stop=True).then_inc(sem("gdn_v1"), 1)
                pe.matmul(ps[:, 3, 0:P], u0, aqk[:, 2 * m, :], start=True, stop=True)
                pe.wait_ge(*after("gdn_v1s", h + 1))
                pe.matmul(ps[:, 3, P:S], v1, aqk[:, 2 * m + 1, :], start=True, stop=False)
                pe.matmul(ps[:, 3, P:S], s1, qg[:, m, :], start=False, stop=True).then_inc(sem("gdn_ot"), 1)
                if m == 0:
                    pe.wait_ge(*after("gdn_o", h + 1))
        for h in range(8):
            pe.wait_ge(*after("gdn_osq", h + 1))
            if h >= 4:
                pe.wait_ge(*after("gdn_rms", h - 3))
            pe.matmul(half(h % 4, 0), ones, gsq[:, h % 4, :], start=True, stop=True).then_inc(sem("gdn_osum"), 1)
        pe.wait_ge(*after("in3_lo", KT))
        project("gdn_out", in_hi, in_lo)
        norm_sums("ln1", True)

        norm_sums("mem", False)
        pe.wait_ge(*after("in4_lo", KT))
        project("mem_kv", in_hi, in_lo)
        norm_sums("mix", False)
        pe.wait_ge(*after("in5_lo", KT))
        for r in range(2):
            for k in range(KT):
                mm = pe.matmul(ps[0:ML_ROWS, 6 + r, 0:S], ml_wg[:, k, ML_ROWS * r:ML_ROWS * (r + 1)], h_t[:, k, :],
                               start=(k == 0), stop=(k == KT - 1))
        mm.then_inc(sem("ml_gates"), 1)
        pe.wait_ge(taken, all_taken("mem_kv"))
        transposes(memkv[:, 4:8, :], 4, (4, 5), "mem_v")
        project("w_in", in_hi, in_lo)
        pe.wait_ge(taken, all_taken("w_in"))

        pe.wait_ge(*after("mem_v_natural", 2))
        pe.wait_ge(*after("ml_gate_rows", 1))
        for n in range(2):
            for c in range(2):
                a = (2 * n + c) * 40
                mm = pe.transpose(ps[:, 4, a:a + ML_ROWS], rows[0:ML_ROWS, 4 + n, c * P:(c + 1) * P],
                                  ident[0:ML_ROWS, 0:ML_ROWS])
        mm.then_inc(sem("ml_cols"), 1)
        transposes(proj[:, 8:12, :], 4, (5, 6), "ml_v")
        pe.wait_ge(*after("ml_v_natural", 2))
        pe.wait_ge(*after("ml_qk", 8))
        pe.wait_ge(*after("ml_cols_taken", 3))
        for h in range(4):
            if h >= 1:
                pe.wait_ge(*after("ml_w", 2 * h))
            for qt in range(2):
                mm = pe.matmul(half(4, qt), proj[:, h, qt * P:(qt + 1) * P], proj[:, 4 + h, :], start=True, stop=True)
            for d in range(2):
                r = h + 32 * d
                sel = ident[0:ML_ROWS, r:r + 1].to_broadcast([ML_ROWS, P])
                mm = pe.matmul(half(5, d), sel, rows[0:ML_ROWS, 3, :], start=True, stop=True)
            mm.then_inc(sem("ml_scores"), 1)
            pe.wait_ge(*after("ml_w", 2 * (h + 1)))
            if h >= 1:
                pe.wait_ge(*after("ml_pt", h))
            for qt in range(2):
                for kt in range(2):
                    mm = pe.transpose(ps[:, 6, kt * S + qt * P:kt * S + (qt + 1) * P],
                                      wsum[:, qt, kt * P:(kt + 1) * P], ident)
            mm.then_inc(sem("ml_turned_p"), 1)
            pe.wait_ge(*after("ml_pt", h + 1))
            if h >= 1:
                pe.wait_ge(*after("ml_h", h))
            for kt in range(2):
                mm = pe.matmul(half(7, 0), vnat[:, kt, h * P:(h + 1) * P], pt[:, kt, :],
                               start=(kt == 0), stop=(kt == 1))
            mm.then_inc(sem("ml_pv"), 1)
        for h in range(4):
            pe.wait_ge(*after("ml_hsq", h + 1))
            pe.matmul(half(h, 0), ones, gsq[:, h, :], start=True, stop=True).then_inc(sem("ml_hsum"), 1)

        pe.wait_ge(*after("ml_h", 4))
        transposes(proj[:, 24:28, :], 4, (4, 5), "na_v")
        pe.wait_ge(*after("na_v_natural", 2))
        attention("na", 8, lambda h: proj[64 * (h % 2):64 * (h % 2) + 64, 16 + h // 2, :],
                  lambda h: proj[64 * (h % 2):64 * (h % 2) + 64, 20 + h // 2, :],
                  lambda h, kt: vnat[:, kt, h * 64:(h + 1) * 64])
        pe.wait_ge(*after("na_out", 8))
        attention("xa", 4, lambda h: proj[:, 28 + h, :], lambda h: memkv[:, h, :],
                  lambda h, kt: mem_vnat[:, kt, h * P:(h + 1) * P])

        pe.wait_ge(*after("ml_rms", 4))
        project("merge", in_hi, in_lo)
        pe.wait_ge(*after("in6m_lo", 4))
        pe.wait_ge(*after("na_out", 8))
        pe.wait_ge(*after("xa_out", 4))
        first = FIRST["branch"]
        for i in range(3):
            for u in range(GROUP):
                n = first + GROUP * i + u
                pe.wait_ge(lo_done, n + 1)
                pe.wait_ge(taken, n + 1)
                for t in range(2):
                    mm = split_mm(half(u, t), u, [(4 * t + k, 8 + 4 * i + k) for k in range(4)], True, True)
                mm.then_inc(unit_done, 1)
        pe.wait_ge(*after("in7_lo", KT))
        project("w_out", in_hi, in_lo)
        norm_sums("ffn", False)
        pe.wait_ge(*after("in8_lo", KT))
        project("ffn_up", in_hi, in_lo)
        pe.wait_ge(*after("in9_lo", FT))
        first = FIRST["ffn_down"]
        with pe.Fori(0, 2) as i:
            for u in range(12):
                pe.wait_ge(lo_done, i * 12 + (first + u + 1))
                if u % 3 == 0:
                    pe.wait_ge(taken, i * 4 + (first + u // 3 + 1))
                blocks = [(b, 8 * (u % 3) + b) for b in range(UNIT if u % 3 < 2 else FT - 2 * UNIT)]
                split_mm(ps[:, u // 3, 0:S], u % GROUP, blocks, u % 3 == 0, u % 3 == 2).then_inc(unit_done, 1)
        norm_sums("final", False)

    @block.scalar
    def _(act):
        act_in = [0]

        def link(ins):
            act_in[0] += 1
            ins.then_inc(sem("act_chain"), 1)
            act.wait_ge(*after("act_chain", act_in[0]))

        def high(n, u):
            act.wait_ge(loaded, n // GROUP + 1)
            if not isinstance(n, int) or n >= GROUP:
                act.wait_ge(unit_done, n - (GROUP - 1))
            slot = (n // GROUP) % RAW
            act.copy(w_hi[:, u, :], raw[:, slot, u * UNIT * P:(u + 1) * UNIT * P]).then_inc(hi_done, 1)

        def project(name, evac, per=1, first_group=0, groups=None):
            first = FIRST[name]
            groups = COUNT[name] // GROUP if groups is None else groups
            with act.Fori(first_group, first_group + groups) as i:
                for u in range(GROUP):
                    act.wait_ge(unit_done, i * GROUP + (first + u + 1))
                    evac(i, u)
                    act.wait_ge(loaded, i + (first // GROUP + 2))
                    slot = (i + (first // GROUP + 1)) % RAW
                    act.copy(w_hi[:, u, :], raw[:, bass.ds(slot, 1), u * UNIT * P:(u + 1) * UNIT * P]
                             .rearrange("p a b -> p (a b)")).then_inc(hi_done, 1)

        def plain(dst):
            def evac(i, u):
                act.copy(dst[:, bass.ds(i * GROUP + u, 1), :], ps[:, u:u + 1, 0:S]).then_inc(taken, 1)
            return evac

        def split(tag, tiles, src, ready, ready_at, base=0):
            for k in range(tiles):
                act.wait_ge(*after(ready, ready_at(k)))
                act.copy(in_hi[:, base + k, :], src(k)).then_inc(sem(f"{tag}_hi"), 1)

        def squares(tag, src, ready=None):
            for k in range(KT):
                if ready:
                    act.wait_ge(*after(ready, k + 1))
                act.activation(sq[:, k, :], src[:, k, :], ACT.Square).then_inc(sem(f"{tag}_sq"), 1)

        def root(tag, eps):
            act.wait_ge(*after(f"{tag}_sumsq", 1))
            act.activation(stat[:, 1, :], half(5, 0), ACT.Sqrt, bias=eps_col(eps), scale=1.0 / D
                           ).then_inc(sem(f"{tag}_root"), 1)

        def eps_col(eps):
            return small[:, 1, 15:16] if eps == LN_EPS else small[:, 1, 14:15]

        def gdn_root(act, t):
            act.wait_ge(*after("gdn_sum", t + 1))
            if t >= 4:
                act.wait_ge(*after("gdn_unit", t - 3))
            act.activation(rb[:, t % 4, :], half(t % 4, 0), ACT.Sqrt, bias=eps_col(EPS)).then_inc(sem("gdn_len"), 1)

        def gdn_out_root(act, h):
            act.wait_ge(*after("gdn_osum", h + 1))
            if h >= 4:
                act.wait_ge(*after("gdn_gated", h - 3))
            act.activation(rb[:, h % 4, :], half(h % 4, 0), ACT.Sqrt, bias=eps_col(EPS), scale=1.0 / P
                           ).then_inc(sem("gdn_rms"), 1)

        act.sem_inc(taken, GROUP)
        act.wait_ge(*after("params_in", 16))
        act.activation(cs[:], param("c", 0, 8), ACT.Silu).then_inc(sem("cs_ready"), 1)
        act.wait_ge(*after("cs_ready", 1))
        for r in range(2):
            act.copy(cs_hi[:, :, r:r + 1], cs[:].rearrange("p (k a) -> p k a", a=1)).then_inc(sem("cs_high"), 1)
        for n in range(GROUP):
            high(n, n)

        def evac_mod(i, u):
            act.copy(mod2[:, bass.ds(i * GROUP + u, 1), :], ps[:, u:u + 1, 0:2]).then_inc(taken, 1)

        project("ada0", evac_mod)
        split("in0", KT, lambda k: h_t[:, k, :], "h0", lambda k: k + 1)
        project("moba_in", plain(proj))

        def natural(name, tiles, banks, dst):
            for g in range(tiles // 2):
                act.wait_ge(*after(f"{name}_turned", g + 1))
                act.copy(dst[:, :, 2 * g * P:2 * (g + 1) * P].rearrange("p c (t d) -> p t c d", t=2),
                         ps[:, banks[g % len(banks)], :].rearrange("p (t c d) -> p t c d", t=2, c=2)
                         ).then_inc(sem(f"{name}_natural"), 1)

        def attention(name, heads, finish):
            for h in range(heads + 1):
                if h < heads:
                    act.wait_ge(*after(f"{name}_max", h + 1))
                    for qt in range(2):
                        act.activation(lg[h % 2][:, qt, :], lg[h % 2][:, qt, :], ACT.Exp,
                                       bias=small[:, 0, 4 * (h % 2) + qt:4 * (h % 2) + qt + 1],
                                       accum_out=small[:, 0, 4 * (h % 2) + 2 + qt:4 * (h % 2) + 3 + qt]
                                       ).then_inc(sem(f"{name}_exp"), 1)
                if h >= 1:
                    finish(h - 1)
                if h < heads:
                    act.wait_ge(*after(f"{name}_turned_p", h + 1))
                    if h >= 1:
                        act.wait_ge(*after(f"{name}_pv", h))
                    act.copy(flat(pt), ps[:, 6, :]).then_inc(sem(f"{name}_pt"), 1)

        act.wait_ge(taken, all_taken("moba_in"))
        act.activation(proj[:, 24:32, :], proj[:, 24:32, :], ACT.Silu).then_inc(sem("moba_z"), 1)
        natural("moba_v", 8, (4, 5, 6, 7), vnat)

        def moba_finish(h):
            act.wait_ge(*after("moba_out", h + 1))
            act.copy(in_hi[:, h, :], gated[h % 2]).then_inc(sem("in1_hi"), 1)

        attention("moba", 8, moba_finish)
        project("ada1", evac_mod)
        project("moba_out", plain(proj))

        def layer_norm(tag, layer, out_h):
            squares(tag, x_t, f"{tag}_centred")
            root(tag, LN_EPS)
            for k in range(KT):
                act.wait_ge(*after(f"{tag}_scaled", k + 1))
                act.activation(x_t[:, k, :], sq[:, k, :], ACT.Identity, bias=param("ln_b", 8 * layer + k)
                               ).then_inc(sem(f"{tag}_x"), 1)
            if out_h:
                for k in range(KT):
                    act.wait_ge(*after(f"{tag}_x", k + 1))
                    act.activation(h_t[:, k, :], x_t[:, k, :], ACT.Identity, bias=mod[:, 1, k:k + 1],
                                   scale=mod[:, 1, 8 + k:9 + k]).then_inc(sem("h1"), 1)

        layer_norm("ln0", 0, True)
        split("in2", KT, lambda k: h_t[:, k, :], "h1", lambda k: k + 1)

        act.activation(gexp[0:8, 2, 0:1], param("a_log", 0, 1, 8), ACT.Exp).then_inc(sem("gdn_a"), 1)
        act.wait_ge(*after("gdn_gates", 1))
        act.activation(rows[0:8, 3, :], ps[0:8, 7, 0:S], ACT.Sigmoid).then_inc(sem("gdn_rows"), 1)
        act.wait_ge(*after("gdn_z", 1))
        link(act.activation(rows[0:8, 1, :], rows[0:8, 0, :], ACT.Abs))
        link(act.activation(rows[0:8, 1, :], rows[0:8, 1, :], ACT.Exp, scale=-1.0))
        act.activation(rows[0:8, 1, :], rows[0:8, 1, :], ACT.Ln, bias=1.0).then_inc(sem("gdn_ln"), 1)

        def evac_conv(i, u):
            act.wait_ge(*after("conv_free", i * GROUP + (u + 1)))
            act.copy(cin[u][:, 3:3 + S], ps[:, u, 0:S])
            act.activation(proj[:, bass.ds(i * GROUP + u, 1), :], ps[:, u:u + 1, 0:S], ACT.Copy,
                           scale=params[:, bass.ds(i * GROUP + (PCOL["gdn_conv"] + 72 + u), 1)]).then_inc(taken, 1)

        project("gdn_in", evac_conv, groups=6)
        project("gdn_in", plain(proj), first_group=6, groups=2)
        act.wait_ge(taken, all_taken("gdn_in"))
        act.wait_ge(*after("conv_free", GROUP + 24))
        for n in range(8):
            act.activation(proj[:, 4 * n:4 * n + 4, :], proj[:, 4 * n:4 * n + 4, :], ACT.Silu
                           ).then_inc(sem("gdn_silu"), 1)
        act.wait_ge(*after("gdn_cols", 1))
        act.copy(gcol[:].rearrange("p a b c -> p (a b c)"), ps[:, 6, 0:32]).then_inc(sem("gdn_col_done"), 1)
        for t in range(16):
            act.wait_ge(*after("gdn_silu", t // 4 + 1))
            if t >= 4:
                act.wait_ge(*after("gdn_sum", t - 3))
            act.activation(gsq[:, t % 4, :], proj[:, t, :], ACT.Square).then_inc(sem("gdn_sq"), 1)
            if t >= 3:
                gdn_root(act, t - 3)
        for t in range(13, 16):
            gdn_root(act, t)
        act.wait_ge(*after("gdn_col_done", 1))
        act.activation(gexp[:, 1, :], gcol[:, 0, 1, :], ACT.Exp).then_inc(sem("gdn_e1"), 1)
        for g in range(4):
            act.wait_ge(*after("gdn_bc", g + 1))
            if g >= 1:
                act.wait_ge(*after("gdn_ot", 2 * g))
            for m in range(2):
                act.activation(qg[:, m, :], ps[:, m, P:S], ACT.Exp).then_inc(sem("gdn_qe"), 1)
            act.wait_ge(*after("gdn_diff", g + 1))
            act.activation(flat(dec), flat(dec), ACT.Exp).then_inc(sem("gdn_dec"), 1)
            act.wait_ge(*after("gdn_nat", g + 1))
            act.wait_ge(*after("gdn_e0", 2 * (g + 1)))
            act.wait_ge(*after("gdn_e1", 2))
            link(act.activation(gexp[:, 0, 2 * g:2 * g + 2], gexp[:, 2, 2 * g:2 * g + 2], ACT.Exp))
            for m in range(2):
                h = 2 * g + m
                for c in range(2):
                    j = 2 * m + c
                    act.activation(kdg[:, j, :], ps[:, 2, j * P:(j + 1) * P], ACT.Copy,
                                   scale=gexp[:, c, h:h + 1]).then_inc(sem("gdn_kdg"), 1)
            for lv in range(LEVELS):
                act.wait_ge(*after("gdn_p", g * LEVELS + lv + 1))
                act.copy(flat(pm), ps[:, 6, :]).then_inc(sem("gdn_ps"), 1)
            for m in range(2):
                h = 2 * g + m
                act.wait_ge(*after("gdn_u0", h + 1))
                if h >= 1:
                    act.wait_ge(*after("gdn_ot", h))
                act.copy(u0, ps[:, 6, 0:P]).then_inc(sem("gdn_u0s"), 1)
                act.wait_ge(*after("gdn_w", h + 1))
                act.mul(wn, ps[:, 7, 0:P], -1.0).then_inc(sem("gdn_ws"), 1)
                act.wait_ge(*after("gdn_ot", h + 1))
                act.copy(proj[:, h, :], ps[:, 3, 0:S]).then_inc(sem("gdn_o"), 1)
        for h in range(8):
            act.wait_ge(*after("gdn_o", h + 1))
            if h >= 4:
                act.wait_ge(*after("gdn_osum", h - 3))
            act.activation(gsq[:, h % 4, :], proj[:, h, :], ACT.Square).then_inc(sem("gdn_osq"), 1)
            if h >= 3:
                gdn_out_root(act, h - 3)
        for h in range(5, 8):
            gdn_out_root(act, h)
        split("in3", KT, lambda k: proj[:, k, :], "gdn_gated", lambda k: k + 1)
        project("gdn_out", plain(proj))
        layer_norm("ln1", 1, False)

        act.wait_ge(*after("mem_in", 16))
        act.wait_ge(*after("ln1_x", KT))
        squares("mem", proj[:, 8:16, :])
        root("mem", EPS)
        split("in4", KT, lambda k: h_t[:, k, :], "mem_h", lambda k: k + 1)
        project("mem_kv", plain(memkv))
        act.wait_ge(*after("ln1_x", KT))
        squares("mix", x_t)
        root("mix", EPS)
        split("in5", KT, lambda k: h_t[:, k, :], "mix_h", lambda k: k + 1)
        natural("mem_v", 4, (4, 5), mem_vnat)
        act.wait_ge(*after("ml_pre", 2))
        link(act.activation(rows[:, 2, :], rows[:, 1, :], ACT.Abs))
        link(act.activation(rows[:, 2, :], rows[:, 2, :], ACT.Exp, scale=-1.0))
        act.activation(rows[:, 2, :], rows[:, 2, :], ACT.Ln, bias=1.0).then_inc(sem("ml_ln"), 1)
        project("w_in", plain(proj))
        act.wait_ge(taken, all_taken("w_in"))
        act.activation(proj[:, 12:16, :], proj[:, 12:16, :], ACT.Sigmoid).then_inc(sem("ml_o"), 1)
        for t in range(8):
            act.wait_ge(*after("ml_conv", t + 1))
            act.activation(proj[:, t, :], gsq[:, t % 4, :], ACT.Silu, bias=param("ml_conv_b", t)
                           ).then_inc(sem("ml_qk"), 1)
        act.wait_ge(*after("ml_cols", 1))
        for c in range(2):
            act.activation(mcol[:, 1, c, :], ps[:, 4, (2 + c) * 40:(2 + c) * 40 + ML_ROWS], ACT.Exp, scale=-1.0
                           ).then_inc(sem("ml_cols_taken"), 1)
        natural("ml_v", 4, (5, 6), vnat)
        for h in range(4):
            act.wait_ge(*after("ml_diff", h + 1))
            act.activation(flat(eb), flat(eb), ACT.Exp).then_inc(sem("ml_exp"), 1)
            act.wait_ge(*after("ml_turned_p", h + 1))
            if h >= 1:
                act.wait_ge(*after("ml_pv", h))
            act.copy(flat(pt), ps[:, 6, :]).then_inc(sem("ml_pt"), 1)
            act.wait_ge(*after("ml_pv", h + 1))
            act.copy(proj[:, h, :], half(7, 0)).then_inc(sem("ml_h"), 1)
            act.wait_ge(*after("ml_h", h + 1))
            act.activation(gsq[:, h, :], proj[:, h, :], ACT.Square).then_inc(sem("ml_hsq"), 1)
        for h in range(4):
            act.wait_ge(*after("ml_hsum", h + 1))
            act.activation(eb[:, h, :], half(h, 0), ACT.Sqrt, bias=eps_col(EPS), scale=1.0 / P
                           ).then_inc(sem("ml_root"), 1)
        split("in6m", 4, lambda k: proj[:, k, :], "ml_rms", lambda k: k + 1, base=8)

        def high_of(name, base, h, rows_):
            act.wait_ge(*after(f"{name}_pv", h + 1))
            p0 = rows_ * (h % 2) if rows_ == 64 else 0
            t = h // 2 if rows_ == 64 else h
            act.copy(in_hi[p0:p0 + rows_, base + t, :], ps[p0:p0 + rows_, 7, 0:S]).then_inc(sem(f"{name}_high"), 1)

        natural("na_v", 4, (4, 5), vnat)
        attention("na", 8, lambda h: high_of("na", 12, h, 64))
        attention("xa", 4, lambda h: high_of("xa", 16, h, P))

        def evac_gate(i, u):
            act.activation(proj[:, bass.ds(i * GROUP + u, 1), :], ps[:, u:u + 1, 0:S], ACT.Sigmoid,
                           bias=params[:, bass.ds(i * GROUP + (PCOL["merge_b"] + u), 1)]).then_inc(taken, 1)

        act.wait_ge(*after("in6m_lo", 4))
        project("merge", evac_gate)
        act.wait_ge(taken, all_taken("merge"))
        for n in range(COUNT["branch"]):
            high(FIRST["branch"] + n + GROUP, n % GROUP)
        split("in7", KT, lambda k: h_t[:, k, :], "merged", lambda k: 9 + k // 2)
        project("w_out", plain(proj))
        squares("ffn", x_t, "ffn_res")
        root("ffn", EPS)
        split("in8", KT, lambda k: h_t[:, k, :], "ffn_h", lambda k: k + 1)

        first = FIRST["ffn_up"]
        with act.Fori(0, COUNT["ffn_up"] // GROUP) as i:
            for m in range(2):
                act.wait_ge(unit_done, i * GROUP + (first + 2 * m + 1))
                act.wait_ge(*after("ffn_pair_free", i * 2 + (m + 1)))
                act.copy(cin[m][:, 1:1 + S], ps[:, 2 * m, 0:S]).then_inc(taken, 1)
                act.wait_ge(unit_done, i * GROUP + (first + 2 * m + 2))
                act.copy(fbuf[m][:, 1, :], ps[:, 2 * m + 1, 0:S]).then_inc(taken, 1)
                for u in (2 * m, 2 * m + 1):
                    act.wait_ge(loaded, i + (first // GROUP + 2))
                    slot = (i + (first // GROUP + 1)) % RAW
                    act.copy(w_hi[:, u, :], raw[:, bass.ds(slot, 1), u * UNIT * P:(u + 1) * UNIT * P]
                             .rearrange("p a b -> p (a b)")).then_inc(hi_done, 1)
                act.wait_ge(*after("ffn_conv", i * 6 + (3 * m + 3)))
                act.activation(fbuf[m][:, 0, :], fbuf[m][:, 0, :], ACT.Gelu_apprx_tanh,
                               bias=params[:, bass.ds(i * 2 + (PCOL["ffn_conv_b"] + m), 1)]).then_inc(sem("ffn_gelu"), 1)
        split("in9", FT, lambda k: proj[:, k, :], "ffn_pair_free", lambda k: 2 + k + 1)
        first = FIRST["ffn_down"]
        for n in range(COUNT["ffn_down"]):
            if n % 3 == 2:
                act.wait_ge(unit_done, first + n + 1)
                act.copy(proj[:, 22 + n // 3, :], ps[:, (n // 3) % 4, 0:S]).then_inc(taken, 1)
            if first + n + GROUP < UNITS:
                high(first + n + GROUP, n % GROUP)
        squares("final", x_t, "final_res")
        root("final", EPS)

    @block.vector
    def _(dve):
        count = [0]

        def link(ins):
            count[0] += 1
            ins.then_inc(sem("dve_chain"), 1)
            dve.wait_ge(*after("dve_chain", count[0]))

        def low_copy(u, slot):
            src = raw[:, slot, u * UNIT * P:(u + 1) * UNIT * P]
            if len(src.shape) == 3:
                src = src.rearrange("p a b -> p (a b)")
            dve.tensor_tensor(w_lo[:, u, :], src, w_hi[:, u, :].bitcast(F32), ALU.subtract).then_inc(lo_done, 1)

        def low(n):
            dve.wait_ge(hi_done, n + 1)
            low_copy(n % GROUP, (n // GROUP) % RAW)

        def low_in_loop(first, i, u):
            dve.wait_ge(hi_done, i * GROUP + (first + u + GROUP + 1))
            low_copy(u, bass.ds((i + (first // GROUP + 1)) % RAW, 1))

        def project(name, before=None, first_group=0, groups=None):
            first = FIRST[name]
            groups = COUNT[name] // GROUP if groups is None else groups
            with dve.Fori(first_group, first_group + groups) as i:
                for u in range(GROUP):
                    if before:
                        before(i, u)
                    low_in_loop(first, i, u)

        def split(tag, tiles, src, base=0):
            for k in range(tiles):
                dve.wait_ge(*after(f"{tag}_hi", k + 1))
                dve.tensor_tensor(in_lo[:, base + k, :], src(k), in_hi[:, base + k, :].bitcast(F32), ALU.subtract
                                  ).then_inc(sem(f"{tag}_lo"), 1)

        def h_tile(k):
            return h_t[:, k, :]

        for m in range(GROUP):
            link(dve.memset(cin[m], 0.0))
        link(dve.memset(small[:, 1, 14:15], EPS))
        link(dve.memset(small[:, 1, 15:16], LN_EPS))
        dve.memset(rows[:], 0.0).then_inc(sem("rows_zero"), 1)
        dve.sem_inc(sem("conv_free"), GROUP)
        dve.wait_ge(*after("cs_high", 2))
        for r in range(2):
            dve.tensor_tensor(cs_lo[:, :, r:r + 1], cs[:].rearrange("p (k a) -> p k a", a=1),
                              cs_hi[:, :, r:r + 1].bitcast(F32), ALU.subtract).then_inc(sem("cs_split"), 1)
        for n in range(GROUP):
            low(n)

        def modulation(layer, name):
            dve.wait_ge(taken, all_taken(name))
            link(dve.tensor_tensor(mod[:, layer:layer + 1, :].rearrange("p a b -> p b a"), mod2[:, :, 0:1],
                                   param("ada_b", 24 * layer, 24).rearrange("p (b a) -> p b a", a=1), ALU.add))
            link(dve.tensor_scalar(mod[:, layer, 8:16], mod[:, layer, 8:16], 1.0, None, ALU.add))

        project("ada0")
        modulation(0, "ada0")
        dve.wait_ge(*after("x_in", 16))
        for k in range(KT):
            dve.tensor_scalar(h_t[:, k, :], x_t[:, k, :], mod[:, 0, 8 + k:9 + k], mod[:, 0, k:k + 1], ALU.mult, ALU.add
                              ).then_inc(sem("h0"), 1)
        split("in0", KT, h_tile)
        dve.tensor_scalar(x_t[:], x_t[:], ALPHA, None, ALU.mult).then_inc(sem("x_alpha"), 1)
        project("moba_in")

        def attention(name, heads, logits, finish):
            for h in range(heads + 1):
                if h < heads:
                    dve.wait_ge(*after(f"{name}_scores", h + 1))
                    if h >= 2:
                        dve.wait_ge(*after(f"{name}_turned_p", h - 1))
                    logits(h)
                    dve.wait_ge(*after(f"{name}_logits", h + 1))
                    dve.tensor_reduce(small[:, 0, 4 * (h % 2):4 * (h % 2) + 2], lg[h % 2], X, ALU.max, negate=True
                                      ).then_inc(sem(f"{name}_max"), 1)
                    dve.wait_ge(*after(f"{name}_exp", 2 * h + 2))
                    a = small[:, 0, 4 * (h % 2) + 2:4 * (h % 2) + 4]
                    link(dve.reciprocal(a, a))
                    for qt in range(2):
                        ins = dve.tensor_scalar(lg[h % 2][:, qt, :], lg[h % 2][:, qt, :], a[:, qt:qt + 1], None, ALU.mult)
                    ins.then_inc(sem(f"{name}_probs"), 1)
                if h >= 1:
                    finish(h - 1)

        def low_of(name, base, h, rows_):
            dve.wait_ge(*after(f"{name}_high", h + 1))
            p0 = rows_ * (h % 2) if rows_ == 64 else 0
            t = h // 2 if rows_ == 64 else h
            dve.tensor_tensor(in_lo[p0:p0 + rows_, base + t, :], ps[p0:p0 + rows_, 7, 0:S],
                              in_hi[p0:p0 + rows_, base + t, :].bitcast(F32), ALU.subtract).then_inc(sem(f"{name}_out"), 1)

        def moba_logits(h):
            for qt in range(2):
                ins = dve.scalar_tensor_tensor(lg[h % 2][:, qt, :], half(4 + h % 2, qt), float(P) ** -0.5,
                                               strip("neg", qt), ALU.mult, ALU.add)
            ins.then_inc(sem("moba_logits"), 1)

        def moba_finish(h):
            dve.wait_ge(*after("moba_pv", h + 1))
            if h >= 2:
                dve.wait_ge(*after("in1_hi", h - 1))
            dve.tensor_tensor(gated[h % 2], half(7, 0), proj[:, 24 + h, :], ALU.mult).then_inc(sem("moba_out"), 1)
            dve.wait_ge(*after("in1_hi", h + 1))
            dve.tensor_tensor(in_lo[:, h, :], gated[h % 2], in_hi[:, h, :].bitcast(F32), ALU.subtract
                              ).then_inc(sem("in1_lo"), 1)

        dve.wait_ge(*after("moba_z", 1))
        attention("moba", 8, moba_logits, moba_finish)
        project("ada1")
        modulation(1, "ada1")
        project("moba_out")

        def layer_norm(tag, layer, name):
            dve.wait_ge(taken, all_taken(name))
            for k in range(KT):
                dve.scalar_tensor_tensor(x_t[:, k, :], proj[:, k, :], mod[:, layer, 16 + k:17 + k], x_t[:, k, :],
                                         ALU.mult, ALU.add).then_inc(sem(f"{tag}_res"), 1)
            dve.wait_ge(*after(f"{tag}_sum", 1))
            link(dve.tensor_scalar(stat[:, 0, :], half(4, 0), 1.0 / D, None, ALU.mult))
            for k in range(KT):
                dve.tensor_tensor(x_t[:, k, :], x_t[:, k, :], stat[:, 0, :], ALU.subtract
                                  ).then_inc(sem(f"{tag}_centred"), 1)
            dve.wait_ge(*after(f"{tag}_root", 1))
            link(dve.reciprocal(stat[:, 1, :], stat[:, 1, :]))
            for k in range(KT):
                dve.scalar_tensor_tensor(sq[:, k, :], x_t[:, k, :], param("ln_g", 8 * layer + k), stat[:, 1, :],
                                         ALU.mult, ALU.mult).then_inc(sem(f"{tag}_scaled"), 1)

        def rms(tag, src, dst, gain, done):
            dve.wait_ge(*after(f"{tag}_root", 1))
            link(dve.reciprocal(stat[:, 1, :], stat[:, 1, :]))
            for k in range(KT):
                dve.scalar_tensor_tensor(dst[:, k, :], src[:, k, :], param(gain, k), stat[:, 1, :],
                                         ALU.mult, ALU.mult).then_inc(sem(done), 1)

        layer_norm("ln0", 0, "moba_out")
        split("in2", KT, h_tile)

        dve.wait_ge(*after("h1", KT))
        dve.tensor_scalar(x_t[:], x_t[:], ALPHA, None, ALU.mult).then_inc(sem("x_alpha"), 1)
        for m in range(GROUP):
            dve.memset(cin[m][:, 0:3], 0.0).then_inc(sem("edges"), 1)
        dve.wait_ge(*after("gdn_gates", 1))
        dve.tensor_scalar(rows[0:8, 0, :], ps[0:8, 6, 0:S], param("dt_bias", 0, 1, 8), None, ALU.add
                          ).then_inc(sem("gdn_z"), 1)
        dve.wait_ge(*after("gdn_ln", 1))
        link(dve.scalar_tensor_tensor(rows[0:8, 0, :], rows[0:8, 0, :], 0.0, rows[0:8, 1, :], ALU.max, ALU.add))
        dve.wait_ge(*after("gdn_a", 1))
        link(dve.tensor_scalar(rows[0:8, 0, :], rows[0:8, 0, :], gexp[0:8, 2, 0:1], -1.0, ALU.mult, ALU.mult))
        for c in range(2):
            ins = dve.tensor_tensor_scan(rows[0:8, 2, c * P:(c + 1) * P], rows[0:8, 4, c * P:(c + 1) * P],
                                         rows[0:8, 0, c * P:(c + 1) * P], 0.0, ALU.add, ALU.add)
        ins.then_inc(sem("gdn_rows"), 1)

        def conv(i, u):
            first = FIRST["gdn_in"]
            dve.wait_ge(taken, i * GROUP + (GROUP + first + u + 1))
            tile = proj[:, bass.ds(i * GROUP + u, 1), :]
            for n, tap in enumerate((2, 1, 0)):
                if n:
                    dve.wait_ge(*after("conv_tap", i * 8 + (2 * u + n)))
                ins = dve.scalar_tensor_tensor(tile, cin[u][:, tap:tap + S].rearrange("p (a b) -> p a b", a=1),
                                               params[:, bass.ds(i * GROUP + (PCOL["gdn_conv"] + 24 * tap + u), 1)],
                                               tile, ALU.mult, ALU.add)
                ins.then_inc(sem("conv_tap") if n < 2 else sem("conv_free"), 1)

        dve.wait_ge(*after("edges", GROUP))
        project("gdn_in", conv, groups=6)
        project("gdn_in", first_group=6, groups=2)
        for t in range(16):
            dve.wait_ge(*after("gdn_len", t + 1))
            link(dve.reciprocal(rb[:, t % 4, :], rb[:, t % 4, :]))
            dve.scalar_tensor_tensor(proj[:, t, :], proj[:, t, :], float(P) ** -0.5 if t < 8 else 1.0, rb[:, t % 4, :],
                                     ALU.mult, ALU.mult).then_inc(sem("gdn_unit"), 1)
        dve.wait_ge(*after("gdn_e1", 1))
        dve.tensor_tensor(gexp[:, 1, :], gexp[:, 1, :], gcol[:, 1, 1, :], ALU.mult).then_inc(sem("gdn_e1"), 1)
        dve.wait_ge(*after("gdn_unit", 16))
        for g in range(4):
            dve.wait_ge(*after("gdn_bc", g + 1))
            dve.wait_ge(*after("gdn_qe", 2 * (g + 1)))
            for m in range(2):
                h = 2 * g + m
                dve.tensor_tensor(kb[:, m, :], half(m, 1), proj[:, 8 + h, :], ALU.mult).then_inc(sem("gdn_kb"), 1)
                dve.tensor_scalar(gexp[:, 2, h:h + 1], ps[:, m, P - 1:P], gcol[:, 0, 0, h:h + 1], None, ALU.subtract
                                  ).then_inc(sem("gdn_e0"), 1)
                for c in range(2):
                    ins = dve.tensor_scalar(dec[:, 2 * m + c, :], ps[:, m, c * P:(c + 1) * P], gcol[:, 0, c, h:h + 1],
                                            0.0, ALU.subtract, ALU.min)
            ins.then_inc(sem("gdn_diff"), 1)
            dve.wait_ge(*after("gdn_nat", g + 1))
            for m in range(2):
                for c in range(2):
                    j = 2 * m + c
                    dve.tensor_scalar(vb[:, j, :], ps[:, 3, j * P:(j + 1) * P], gcol[:, 1, c, 2 * g + m:2 * g + m + 1],
                                      None, ALU.mult).then_inc(sem("gdn_vb"), 1)
            dve.wait_ge(*after("gdn_gram", g + 1))
            dve.wait_ge(*after("gdn_dec", g + 1))
            dve.tensor_tensor(flat(lt), ps[:, 4, :], flat(dec), ALU.mult).then_inc(sem("gdn_lt"), 1)
            dve.tensor_tensor(flat(aqk), ps[:, 5, :], flat(dec), ALU.mult).then_inc(sem("gdn_a0"), 1)
            for lv in range(LEVELS):
                n = g * LEVELS + lv
                if lv == 0:
                    dve.wait_ge(*after("gdn_tinit", 2 * (g + 1)))
                dve.wait_ge(*after("gdn_d", n + 1))
                dve.tensor_tensor(tm, tm, ps[:, 7, :].rearrange("p (a b) -> p a b", a=4), ALU.subtract)
                dve.tensor_tensor(ttm, ttm, ps[:, 4, :].rearrange("p (a b) -> p a b", a=4), ALU.subtract
                                  ).then_inc(sem("gdn_t"), 1)
                dve.wait_ge(*after("gdn_t", n + g + 2))
            for m in range(2):
                h = 2 * g + m
                dve.wait_ge(*after("gdn_s1", h + 1))
                dve.tensor_copy(s1, ps[:, 5, 0:P]).then_inc(sem("gdn_s1s"), 1)
                dve.wait_ge(*after("gdn_v1", h + 1))
                dve.tensor_copy(v1, ps[:, 4, 0:P]).then_inc(sem("gdn_v1s"), 1)
        for h in range(8):
            dve.wait_ge(*after("gdn_rms", h + 1))
            link(dve.reciprocal(rb[:, h % 4, :], rb[:, h % 4, :]))
            link(dve.scalar_tensor_tensor(proj[:, h, :], proj[:, h, :], param("gdn_norm"), rb[:, h % 4, :],
                                          ALU.mult, ALU.mult))
            dve.tensor_tensor(proj[:, h, :], proj[:, h, :], proj[:, 24 + h, :], ALU.mult).then_inc(sem("gdn_gated"), 1)
        split("in3", KT, lambda k: proj[:, k, :])
        project("gdn_out")
        layer_norm("ln1", 1, "gdn_out")

        rms("mem", proj[:, 8:16, :], h_t, "mem_norm", "mem_h")
        split("in4", KT, h_tile)
        project("mem_kv")
        rms("mix", x_t, h_t, "mix_norm", "mix_h")
        split("in5", KT, h_tile)
        dve.wait_ge(*after("ml_gates", 1))
        dve.tensor_scalar(rows[:, 0, :], ps[0:ML_ROWS, 6, 0:S], param("b_ig", 0, 1, ML_ROWS), None, ALU.add
                          ).then_inc(sem("ml_pre"), 1)
        dve.tensor_scalar(rows[:, 1, :], ps[0:ML_ROWS, 7, 0:S], param("b_fg", 0, 1, ML_ROWS), None, ALU.add
                          ).then_inc(sem("ml_pre"), 1)
        dve.wait_ge(*after("ml_ln", 1))
        link(dve.scalar_tensor_tensor(rows[:, 1, :], rows[:, 1, :], 0.0, rows[:, 2, :], ALU.min, ALU.subtract))
        link(dve.memset(rows[:, 4, :], 0.0))
        link(dve.tensor_tensor_scan(rows[:, 2, :], rows[:, 4, :], rows[:, 1, :], 0.0, ALU.add, ALU.add))
        link(dve.tensor_tensor(rows[32:36, 2, :], rows[32:36, 1, :], rows[32:36, 2, :], ALU.subtract))
        link(dve.tensor_tensor(rows[:, 3, :], rows[:, 0, :], rows[:, 2, :], ALU.subtract))
        link(dve.tensor_tensor_scan(rows[0:4, 4, :], rows[0:4, 3, :], rows[0:4, 3, :], NEG, ALU.max, ALU.max))
        link(dve.tensor_tensor_scan(rows[32:36, 4, ::-1], rows[32:36, 3, ::-1], rows[32:36, 3, ::-1], NEG, ALU.max, ALU.max))
        link(dve.tensor_tensor(rows[:, 5, :], rows[:, 2, :], rows[:, 4, :], ALU.add))
        dve.tensor_scalar(rows[:, 5, :], rows[:, 5, :], -88.0, None, ALU.max).then_inc(sem("ml_gate_rows"), 1)
        project("w_in")
        dve.wait_ge(taken, all_taken("w_in"))
        for t in range(8):
            if t >= 4:
                dve.wait_ge(*after("ml_qk", t - 3))
            out, src = gsq[:, t % 4, :], proj[:, t, :]
            link(dve.tensor_scalar(out, src, param("ml_conv", 8 + t), None, ALU.mult))
            link(dve.scalar_tensor_tensor(out[:, 1:S], src[:, 0:S - 1], param("ml_conv", t), out[:, 1:S], ALU.mult, ALU.add))
            dve.scalar_tensor_tensor(out[:, 0:S - 1], src[:, 1:S], param("ml_conv", 16 + t), out[:, 0:S - 1],
                                     ALU.mult, ALU.add).then_inc(sem("ml_conv"), 1)
        dve.wait_ge(*after("ml_cols", 1))
        dve.wait_ge(*after("ml_cols_taken", 2))
        for c in range(2):
            link(dve.tensor_copy(mcol[:, 0, c, :], ps[:, 4, c * 40:c * 40 + ML_ROWS]))
        dve.sem_inc(sem("ml_cols_taken"), 1)
        for h in range(4):
            dve.wait_ge(*after("ml_scores", h + 1))
            for d in range(2):
                for qt in range(2):
                    r = h + 32 * d
                    ins = dve.tensor_scalar(eb[:, 2 * d + qt, :], half(5, d), mcol[:, 0, qt, r:r + 1], 0.0,
                                            ALU.subtract, ALU.min)
            ins.then_inc(sem("ml_diff"), 1)
            dve.wait_ge(*after("ml_masked", 4 * (h + 1)))
            den = small[:, 1, 0:4]
            for d in range(2):
                for qt in range(2):
                    j = 2 * d + qt
                    link(dve.tensor_tensor_reduce(eb[:, j, :], eb[:, j, :], half(4, qt), float(P) ** -0.5, 0.0, ALU.mult,
                                                  ALU.add, den[:, j:j + 1]))
            link(dve.scalar_tensor_tensor(den, den, -1.0, den, ALU.mult, ALU.max))
            for d in range(2):
                r = h + 32 * d
                link(dve.tensor_tensor(den[:, 2 * d:2 * d + 2].rearrange("p (a b) -> p a b", b=1),
                                       den[:, 2 * d:2 * d + 2].rearrange("p (a b) -> p a b", b=1),
                                       mcol[:, 1, :, r:r + 1], ALU.max))
            link(dve.reciprocal(den, den))
            if h >= 1:
                dve.wait_ge(*after("ml_turned_p", h))
            for qt in range(2):
                link(dve.tensor_scalar(wsum[:, qt, :], eb[:, qt, :], den[:, qt:qt + 1], None, ALU.mult))
                dve.scalar_tensor_tensor(wsum[:, qt, :], eb[:, 2 + qt, :], den[:, 2 + qt:3 + qt], wsum[:, qt, :],
                                         ALU.mult, ALU.add).then_inc(sem("ml_w"), 1)
        dve.wait_ge(*after("ml_o", 1))
        for h in range(4):
            dve.wait_ge(*after("ml_root", h + 1))
            link(dve.reciprocal(eb[:, h, :], eb[:, h, :]))
            link(dve.scalar_tensor_tensor(proj[:, h, :], proj[:, h, :], param("ml_norm", h), eb[:, h, :],
                                          ALU.mult, ALU.mult))
            dve.tensor_tensor(proj[:, h, :], proj[:, h, :], proj[:, 12 + h, :], ALU.mult).then_inc(sem("ml_rms"), 1)
        split("in6m", 4, lambda k: proj[:, k, :], base=8)

        def na_logits(h):
            dve.wait_ge(*after("na_bias", h + 1))
            dve.scalar_tensor_tensor(flat(lg[h % 2]), ps[:, 4 + h % 2, :], 64.0 ** -0.5, flat(bias[h % 2]),
                                     ALU.mult, ALU.add).then_inc(sem("na_logits"), 1)

        def xa_logits(h):
            dve.tensor_scalar(flat(lg[h % 2]), ps[:, 4 + h % 2, :], float(P) ** -0.5, None, ALU.mult
                              ).then_inc(sem("xa_logits"), 1)

        attention("na", 8, na_logits, lambda h: low_of("na", 12, h, 64))
        attention("xa", 4, xa_logits, lambda h: low_of("xa", 16, h, P))
        project("merge")
        dve.wait_ge(taken, all_taken("merge"))
        first = FIRST["branch"]
        for n in range(COUNT["branch"]):
            b, u = divmod(n, GROUP)
            dve.wait_ge(unit_done, first + n + 1)
            out = ps[:, u, :].rearrange("p (a b) -> p a b", a=2)
            gate = proj[:, 8 * b + 2 * u:8 * b + 2 * u + 2, :]
            dst = h_t[:, 2 * u:2 * u + 2, :]
            if b == 0:
                ins = dve.tensor_tensor(dst, gate, out, ALU.mult)
            else:
                ins = dve.tensor_tensor(gate, gate, out, ALU.mult)
            ins.then_inc(taken, 1)
            if b:
                dve.wait_ge(taken, all_taken("branch", n + 1))
                ins = dve.tensor_tensor(dst, dst, gate, ALU.add).then_inc(sem("merged"), 1)
            else:
                dve.sem_inc(sem("merged"), 1)
            low(first + n + GROUP)
        split("in7", KT, h_tile)
        project("w_out")
        dve.wait_ge(taken, all_taken("w_out"))
        for k in range(KT):
            dve.tensor_tensor(x_t[:, k, :], x_t[:, k, :], proj[:, k, :], ALU.add).then_inc(sem("ffn_res"), 1)
        rms("ffn", x_t, h_t, "ffn_norm", "ffn_h")
        split("in8", KT, h_tile)
        dve.wait_ge(*after("in8_lo", KT))
        for m in range(2):
            dve.memset(cin[m][:, 0:1], 0.0).then_inc(sem("edges"), 1)
            dve.memset(cin[m][:, 1 + S:2 + S], 0.0).then_inc(sem("edges"), 1)
        dve.wait_ge(*after("edges", GROUP + 4))
        dve.sem_inc(sem("ffn_pair_free"), 2)
        first = FIRST["ffn_up"]
        with dve.Fori(0, COUNT["ffn_up"] // GROUP) as i:
            for m in range(2):
                dve.wait_ge(taken, i * GROUP + (GROUP + first + 2 * m + 1))
                acc = fbuf[m][:, 0, :]

                def tap(t):
                    return params[:, bass.ds(i * 2 + (PCOL["ffn_conv"] + FT * t + m), 1)]

                dve.tensor_scalar(acc, cin[m][:, 0:S], tap(0), None, ALU.mult).then_inc(sem("ffn_conv"), 1)
                for t in (1, 2):
                    dve.wait_ge(*after("ffn_conv", i * 6 + (3 * m + t)))
                    dve.scalar_tensor_tensor(acc, cin[m][:, t:t + S], tap(t), acc, ALU.mult, ALU.add
                                             ).then_inc(sem("ffn_conv"), 1)
                for u in (2 * m, 2 * m + 1):
                    low_in_loop(first, i, u)
                dve.wait_ge(*after("ffn_gelu", i * 2 + (m + 1)))
                dve.wait_ge(taken, i * GROUP + (GROUP + first + 2 * m + 2))
                dve.tensor_tensor(proj[:, bass.ds(i * 2 + m, 1), :], fbuf[m][:, 0:1, :], fbuf[m][:, 1:2, :], ALU.mult
                                  ).then_inc(sem("ffn_pair_free"), 1)
        split("in9", FT, lambda k: proj[:, k, :])
        first = FIRST["ffn_down"]
        for n in range(COUNT["ffn_down"] - GROUP):
            low(first + n + GROUP)
        for k in range(KT):
            dve.wait_ge(taken, GROUP + first + k + 1)
            dve.tensor_tensor(x_t[:, k, :], x_t[:, k, :], proj[:, 22 + k, :], ALU.add).then_inc(sem("final_res"), 1)
        rms("final", x_t, proj, "final_norm", "final_done")

    @block.gpsimd
    def _(pool):
        pool.wait_ge(*after("consts_in", 16))
        pool.wait_ge(*after("gdn_unit", 16))
        for g in range(4):
            for m in range(2):
                pool.wait_ge(*after("gdn_qe", 2 * g + m + 1))
                ins = pool.tensor_tensor(qg[:, m, :], qg[:, m, :], proj[:, 2 * g + m, P:S], ALU.mult)
            ins.then_inc(sem("gdn_qg"), 1)
            if g >= 1:
                pool.wait_ge(*after("gdn_ot", 2 * g))
            one = ident.rearrange("p (a b) -> p a b", a=1).to_broadcast([P, 4, P])
            pool.tensor_copy(tm, one).then_inc(sem("gdn_tinit"), 1)
            pool.tensor_copy(ttm, one).then_inc(sem("gdn_tinit"), 1)
            pool.wait_ge(*after("gdn_tinit", 2 * (g + 1)))
            pool.sem_inc(sem("gdn_t"), 1)
            pool.wait_ge(*after("gdn_a0", g + 1))
            incl = consts[:, CCOL["bw"] + P:CCOL["bw"] + 2 * P].rearrange("p (a b) -> p a b", a=1).to_broadcast([P, 4, P])
            pool.tensor_tensor(aqk, aqk, incl, ALU.mult).then_inc(sem("gdn_aqk"), 1)
            pool.wait_ge(*after("gdn_lt", g + 1))
            for lv in range(LEVELS):
                n = g * LEVELS + lv
                if n >= 1:
                    pool.wait_ge(*after("gdn_p", n))
                a = CCOL["level"] + lv * P
                mask = consts[:, a:a + P].rearrange("p (a b) -> p a b", a=1).to_broadcast([P, 4, P])
                pool.tensor_tensor(ctm, lt, mask, ALU.mult).then_inc(sem("gdn_ct"), 1)
        pool.wait_ge(*after("in3_lo", KT))
        pool.dma_start(proj[:, 8:16, :], io["mem_t"]).then_inc(sem("mem_in"), 16)
        for h in range(4):
            pool.wait_ge(*after("ml_exp", h + 1))
            for d, name in enumerate(("fw", "bw")):
                for qt in range(2):
                    pool.tensor_tensor(eb[:, 2 * d + qt, :], eb[:, 2 * d + qt, :], strip(name, qt), ALU.mult
                                       ).then_inc(sem("ml_masked"), 1)
        pool.wait_ge(*after("ml_hsum", 4))
        for h in range(8):
            if h >= 2:
                pool.wait_ge(*after("na_logits", h - 1))
            pool.dma_start(bias[h % 2], io["na_bias"][h]).then_inc(sem("na_bias_in"), 16)
            pool.wait_ge(*after("na_bias_in", 16 * (h + 1)))
            mask = consts[:, CCOL["colmask"]:CCOL["colmask"] + S].rearrange("p (a b) -> p a b", a=1).to_broadcast([P, 2, S])
            pool.tensor_tensor(bias[h % 2], bias[h % 2], mask, ALU.add).then_inc(sem("na_bias"), 1)


def _constants():
    i, j = np.meshgrid(np.arange(P), np.arange(P), indexing="ij")
    one, zero = np.ones((P, P)), np.zeros((P, P))
    out = {
        "ident": np.eye(P),
        "fw": np.hstack([one, j <= i, zero]),
        "bw": np.hstack([zero, j >= i, one]),
        "neg": np.hstack([zero, np.where(j <= i, 0.0, NEG), NEG * one]),
        "level": np.hstack([(i // (2 * s) == j // (2 * s)) & ((i // s) % 2 == 0) & ((j // s) % 2 == 1)
                            for s in (2 ** n for n in range(LEVELS))]),
    }
    c, w = np.arange(64), 16
    start = np.clip(c - w // 2, 0, 64 - w)
    ok = (c[None, :] >= start[:, None]) & (c[None, :] < start[:, None] + w)
    out["colmask"] = np.tile(np.where(ok, 0.0, NEG), (2, 4))
    return np.ascontiguousarray(np.hstack([out[n] for n, _ in CONSTS]).astype(np.float32))


def _groups(blocks):
    u = blocks.shape[0]
    return np.ascontiguousarray(blocks.reshape(u // GROUP, GROUP * UNIT, P, P).transpose(0, 2, 1, 3)
                                .reshape(u // GROUP, P, GROUP * UNIT * P))


def _by_output(w):
    n = w.shape[1] // P
    return w.reshape(KT, P, n, P).transpose(2, 0, 1, 3)


def _tiles(a):
    return np.ascontiguousarray(a.T.reshape(-1, P, S).transpose(1, 0, 2))


def _columns(v):
    return np.asarray(v).reshape(-1, P).T


def _rows(v, at):
    out = np.zeros((P, 1), np.float32)
    for part, a in zip(v, at):
        out[a:a + len(part), 0] = part
    return out


def kernel(**inputs):
    import concourse.bacc as bacc
    from concourse.bass_utils import run_bass_kernel_spmd

    t = {k: np.asarray(v) for k, v in inputs.items()}
    a = {}
    w_in = t["w_in_2"][0]
    gdn = t["gdn_w_in"][0]
    a["ada0"], a["ada1"] = (_groups(_by_output(t["ada_w"][n])) for n in range(2))
    a["moba_in"] = _groups(_by_output(t["moba_w_in"][0]))
    a["moba_out"] = _groups(_by_output(t["moba_w_out"][0]))
    a["gdn_in"] = _groups(_by_output(gdn[:, :4096]))
    a["gdn_out"] = _groups(_by_output(t["gdn_w_out"][0]))
    a["mem_kv"] = _groups(_by_output(t["w_mem_kv_2"][0]))
    a["w_in"] = _groups(_by_output(np.concatenate([w_in[:, :2048], w_in[:, 2064:4112]], 1)))
    a["merge"] = _groups(_by_output(w_in[:, 4112:]))
    a["branch"] = _groups(np.concatenate([
        t[n][0].reshape(4, P, 8, P).transpose(2, 0, 1, 3).reshape(4, 8, P, P)
        for n in ("w_br_ml_2", "w_br_na_2", "w_br_xa_2")]))
    a["w_out"] = _groups(_by_output(t["w_out_2"][0]))
    up = _by_output(t["w_ffn_up_2"][0])
    a["ffn_up"] = _groups(np.stack([up[:FT], up[FT:]], 1).reshape(2 * FT, KT, P, P))
    down = t["w_ffn_down_2"][0].reshape(FT, P, KT, P).transpose(2, 0, 1, 3)
    a["ffn_down"] = _groups(np.concatenate([down, np.zeros((KT, 2, P, P), np.float32)], 1).reshape(24, UNIT, P, P))
    a["x_t"] = _tiles(t["x"][0])
    a["mem_t"] = _tiles(t["mem_2"][0])
    a["gdn_wg"] = np.ascontiguousarray(gdn[:, 4096:].reshape(KT, P, 16).transpose(1, 0, 2))
    gates = w_in[:, 2048:2064]
    wide = np.zeros((D, 2 * ML_ROWS), np.float32)
    wide[:, 0:4], wide[:, 32:36] = gates[:, 0:4], gates[:, 8:12]
    wide[:, ML_ROWS:ML_ROWS + 4], wide[:, ML_ROWS + 32:ML_ROWS + 36] = gates[:, 4:8], gates[:, 12:16]
    a["ml_wg"] = np.ascontiguousarray(wide.reshape(KT, P, 2 * ML_ROWS).transpose(1, 0, 2))
    rpb = t["na_rpb_2"][0]
    q = np.arange(S)
    r, c = q // 64, q % 64
    dr = r[None, :] - r[:, None] + 7
    dc = np.clip(c[None, :] - c[:, None] + 15, 0, 30)
    a["na_bias"] = np.ascontiguousarray(rpb[:, dr, dc].reshape(8, 2, P, S).transpose(0, 2, 1, 3))
    named = {
        "c": t["c"], "ada_b": t["ada_b"], "ln_g": t["ln_g"], "ln_b": t["ln_b"], "gdn_conv": t["gdn_conv_w"][0],
        "gdn_norm": t["gdn_norm_w"], "ml_conv": t["w_ml_conv_2"][0], "ml_conv_b": t["b_ml_conv_2"],
        "ml_norm": t["ml_norm_g_2"], "mix_norm": t["mix_norm_g_2"], "mem_norm": t["mem_norm_g_2"],
        "merge_b": t["b_merge_gate_2"], "ffn_norm": t["ffn_norm_g_2"], "ffn_conv": t["w_ffn_conv_2"][0],
        "ffn_conv_b": t["b_ffn_conv_2"], "final_norm": t["final_norm_g_2"],
    }
    rows_ = {"a_log": _rows([t["gdn_a_log"][0]], [0]), "dt_bias": _rows([t["gdn_dt_bias"][0]], [0]),
             "b_ig": _rows(t["b_ml_igate_2"][0], [0, 32]), "b_fg": _rows(t["b_ml_fgate_2"][0], [0, 32])}
    a["params"] = np.ascontiguousarray(np.hstack([_columns(named[n]) if n in named else rows_[n] for n, _ in PARAMS]))
    a["consts"] = _constants()

    nc = bacc.Bacc("TRN2", target_bir_lowering=False, num_devices=1)
    io = {n: nc.dram_tensor(f"in_{n}", v.shape, F32, kind="ExternalInput").ap() for n, v in a.items()}
    io["out"] = nc.dram_tensor("out_t", (P, KT, S), F32, kind="ExternalOutput").ap()
    build(nc, io)
    r = run_bass_kernel_spmd(nc, [{f"in_{n}": v for n, v in a.items()}], core_ids=[0])
    out = r.results[0]["out_t"]
    return np.ascontiguousarray(out.transpose(1, 0, 2).reshape(D, S).T)[None]
```

```python
from contextlib import ExitStack

import numpy as np
import concourse.bass as bass
from concourse import mybir

F32 = mybir.dt.float32
F32R = mybir.dt.float32r
ALU = mybir.AluOpType
ACT = mybir.ActivationFunctionType
X = mybir.AxisListType.X

P = 128
D = 1024
KT = D // P
S = 256
NEG = -1e30
DEPTH = 2
ALPHA = (2.0 * DEPTH) ** 0.25
LN_EPS = 1e-5
EPS = 1e-6
FF = 2816
FT = FF // P
UNIT = 8
GROUP = 4
PAIR = 2
RAW = 4
ADA = 48
LEVELS = 7

STAGES = [("moba_in", 32), ("moba_out", 8), ("gdn_in", 32), ("gdn_out", 8),
          ("mem_kv", 8), ("w_in", 32), ("merge", 24), ("branch", 12), ("w_out", 8), ("ffn_up", 44),
          ("ffn_down", 24)]
FIRST = {}
_n = 0
for _name, _count in STAGES:
    FIRST[_name] = _n
    _n += _count
UNITS = _n
LOADED = {n: 16 + f + (32 if f else 0) for n, f in FIRST.items()}
STRIDE = {n: 8 if n == "moba_in" else 4 for n in FIRST}
COUNT = dict(STAGES)

PARAMS = [("c", 8), ("ada_b", 48), ("ln_g", 16), ("ln_b", 16), ("gdn_conv", 96), ("gdn_norm", 1),
          ("ml_conv", 24), ("ml_conv_b", 8), ("ml_norm", 4), ("mix_norm", 8), ("mem_norm", 8),
          ("merge_b", 24), ("ffn_norm", 8), ("ffn_conv", 66), ("ffn_conv_b", 22), ("final_norm", 8),
          ("a_log", 1), ("dt_bias", 1), ("b_ig", 1), ("b_fg", 1)]
PCOL = {}
_n = 0
for _name, _count in PARAMS:
    PCOL[_name] = _n
    _n += _count
NPARAM = _n

CONSTS = [("ident", P), ("fw", 3 * P), ("bw", 3 * P), ("neg", 3 * P), ("level", LEVELS * P), ("colmask", S)]
CCOL = {}
_n = 0
for _name, _count in CONSTS:
    CCOL[_name] = _n
    _n += _count
NCONST = _n
ML_ROWS = 36


def build(nc, io):
    ctx = ExitStack()
    with ctx:
        _program(nc, io, ctx)


def _program(nc, io, ctx):
    def sb(name, shape, dt=F32):
        return ctx.enter_context(nc.sbuf_tensor(name, shape, dt))

    turns = {
        ("_res",): [("ln0", KT), ("ln1", KT), ("ffn", KT), ("final", KT)],
        ("_sum",): [("ln0", 1), ("ln1", 1)],
        ("_root", "_sumsq"): [("ln0", 1), ("ln1", 1), ("mem", 1), ("mix", 1), ("ffn", 1), ("final", 1)],
        ("_sq",): [(n, KT) for n in ("ln0", "ln1", "mem", "mix", "ffn", "final")],
        ("_centred", "_scaled", "_x"): [("ln0", KT), ("ln1", KT)],
        ("_scores", "_logits", "_max", "_probs", "_turned_p", "_pt", "_pv", "_out"):
            [("moba", 8), ("na", 8), ("xa", 4)],
        ("_exp",): [("moba", 16), ("na", 16), ("xa", 8)],
        ("_high",): [("na", 8), ("xa", 4)],
        ("_turned", "_natural"): [("moba_v", 4), ("mem_v", 2), ("ml_v", 2), ("na_v", 2)],
        ("_hi", "_lo"): [(f"in{n}", KT) for n in range(6)] + [("in6m", 4), ("in7", KT), ("in8", KT), ("in9", FT)],
    }
    shared, start = {}, {}
    for kinds, order in turns.items():
        for kind in kinds:
            at = 0
            for tag, n in order:
                shared[tag + kind], start[tag + kind] = "turn" + kind, at
                at += n

    sems = {}

    def sem(name):
        name = shared.get(name, name)
        if name not in sems:
            sems[name] = ctx.enter_context(nc.semaphore(name))
        return sems[name]

    def after(name, n):
        return sem(name), n + start.get(name, 0)

    raw = sb("raw", [P, RAW, PAIR * UNIT * P])
    w_hi = sb("w_hi", [P, GROUP, UNIT * P], F32R)
    w_lo = sb("w_lo", [P, GROUP, UNIT * P], F32R)
    in_hi = sb("in_hi", [P, FT, S], F32R)
    in_lo = sb("in_lo", [P, FT, S], F32R)
    x_t = sb("x_t", [P, KT, S])
    proj = sb("proj", [P, 32, S])
    params = sb("params", [P, NPARAM])
    consts = sb("consts", [P, NCONST])
    gdn_wg = sb("gdn_wg", [P, KT, 16])
    ml_wg = sb("ml_wg", [P, KT, 2 * ML_ROWS])
    cs = sb("cs", [P, KT])
    mod = sb("mod", [P, 2, 24])
    stat = sb("stat", [P, 2, S])
    rows = sb("rows", [ML_ROWS, 6, S])
    gcol = sb("gcol", [P, 2, 2, 8])
    gexp = sb("gexp", [P, 3, 8])
    mcol = sb("mcol", [P, 2, 2, ML_ROWS])
    small = sb("small", [P, 2, 16])
    work = sb("work", [P, 5 * 1024])
    memkv = sb("memkv", [P, 8, S])
    mem_vnat = sb("mem_vnat", [P, 2, 4 * P])

    ps = ctx.enter_context(nc.psum_tensor("ps", [P, 8, 512], F32))

    def area(at, *shape, of=work):
        v = of[:, at:at + int(np.prod(shape))]
        return v.rearrange("p (a b) -> p a b", a=shape[0]) if len(shape) == 2 else v

    acc = area(0, 4, D)
    sq = area(0, KT, S)
    h_t = area(2048, KT, S)
    vnat = area(0, 2, D)
    lg = [area(2048, 2, S), area(2560, 2, S)]
    pt = area(3072, 2, S)
    gated = [area(3584, S), area(3840, S)]
    bias = [area(4096, 2, S), area(4608, 2, S)]
    cin = [area((S + 3) * u, S + 3) for u in range(GROUP)]
    fbuf = [area(2048 + 512 * u, 2, S) for u in range(2)]
    eb = area(2048, 4, S)
    wsum = area(3584, 2, S)
    gsq = area(4096, 4, S)
    rb = area(1024, 4, S)
    ctm, pm, lt, aqk = ([area(1024 * n + 512 * p, 4, P) for p in range(2)] for n in range(4))
    dec, kb = area(4096, 4, P), area(4608, 2, S)
    kv_flat = memkv[:].rearrange("p a b -> p (a b)")
    kdg, vb = ([area(1024 * n + 512 * p, 4, P, of=kv_flat) for p in range(2)] for n in range(2))
    qg = area(0, 4, P, of=mem_vnat[:].rearrange("p a b -> p (a b)"))
    u0, wn, s1, v1 = area(4096, 4, P), area(4608, 4, P), ctm[0], ctm[1]

    def tri(base, gg):
        return proj[:, base + 2 * gg:base + 2 * gg + 2, :].rearrange("p a (c b) -> p (a c) b", c=2)


    ident = consts[:, CCOL["ident"]:CCOL["ident"] + P]
    ones = consts[:, CCOL["fw"]:CCOL["fw"] + P]

    def param(name, k=0, n=1, rows_=P):
        return params[0:rows_, PCOL[name] + k:PCOL[name] + k + n]

    def strip(name, qt):
        a = CCOL[name] + P * (1 - qt)
        return consts[:, a:a + S]

    def half(bank, k):
        return ps[:, bank, k * S:(k + 1) * S]

    def flat(t):
        return t.rearrange("p a b -> p (a b)")

    loaded, hi_done, lo_done, unit_done, taken = (sem(n) for n in
        ("pair_loaded", "unit_hi", "unit_lo", "unit_multiplied", "bank_taken"))

    def all_taken(name, n=None):
        return GROUP + FIRST[name] + (COUNT[name] if n is None else n)

    block = ctx.enter_context(nc.Block())

    @block.sync
    def _(sp):
        sp.dma_start(params[:], io["params"]).then_inc(sem("params_in"), 16)
        sp.dma_start(consts[:], io["consts"]).then_inc(sem("consts_in"), 16)
        sp.dma_start(x_t[:], io["x_t"]).then_inc(sem("x_in"), 16)
        sp.dma_start(gdn_wg[:], io["gdn_wg"]).then_inc(sem("gate_w_in"), 16)
        sp.dma_start(ml_wg[:], io["ml_wg"]).then_inc(sem("gate_w_in"), 16)

        def load(g, src, i=None):
            at = 0 if i is None else i
            if i is not None or g >= RAW:
                sp.wait_ge(lo_done, at * RAW * PAIR + PAIR * (g - RAW + 1))
            sp.dma_start(raw[:, g % RAW, :], src).then_inc(sem(f"slot_in{g % RAW}"), 16)
            if i is not None or g >= 2:
                sp.wait_ge(sem(f"slot_in{(g - 2) % RAW}"), at * 16 + 16 * ((g - 2) // RAW + 1))
                sp.sem_inc(loaded, 1)

        def load_stage(name, first, count):
            g = LOADED[name] // PAIR + first
            if count % RAW == 0 and g % RAW == 0 and count > RAW:
                with sp.Fori(0, count // RAW) as i:
                    for c in range(RAW):
                        load(g + c, io[name][bass.ds(i * RAW + (first + c), 1)].rearrange("a p n -> (a p) n"), i)
            else:
                for c in range(count):
                    load(g + c, io[name][first + c])

        for g in range(8):
            load(g, io["ada"][g])
        with sp.Fori(0, 8) as i:
            for c in range(RAW):
                src, first = (io["moba_in"], c) if c < 2 else (io["ada"], 6 + c)
                load(8 + c, src[bass.ds(i * 2 + first, 1)].rearrange("a p n -> (a p) n"), i)
        for name, units in STAGES[1:]:
            pairs = units // PAIR
            head = -(LOADED[name] // PAIR) % RAW if pairs > 2 * RAW else 0
            load_stage(name, 0, head)
            load_stage(name, head, (pairs - head) // RAW * RAW)
            done = head + (pairs - head) // RAW * RAW
            load_stage(name, done, pairs - done)
        for g in (138, 139):
            sp.wait_ge(sem(f"slot_in{g % RAW}"), 16 * (g // RAW + 1))
            sp.sem_inc(loaded, 1)
        sp.wait_ge(*after("final_done", KT))
        sp.dma_start(io["out"], proj[:, 0:KT, :]).then_inc(sem("out_stored"), 16)
        sp.wait_ge(*after("out_stored", 16))

    @block.tensor
    def _(pe):
        def project(name, a_hi, a_lo, first_in=0, width=S):
            first = FIRST[name]
            with pe.Fori(0, COUNT[name] // GROUP) as i:
                for u in range(GROUP):
                    pe.wait_ge(lo_done, i * STRIDE[name] + (LOADED[name] + u + 1))
                    pe.wait_ge(taken, i * GROUP + (first + u + 1))
                    out = ps[:, u, 0:width]
                    for n, (w, a) in enumerate(((w_hi, a_hi), (w_hi, a_lo), (w_lo, a_hi))):
                        for k in range(UNIT):
                            mm = pe.matmul(out, w[:, u, k * P:(k + 1) * P], a[:, first_in + k, :],
                                           start=(n == 0 and k == 0), stop=(n == 2 and k == UNIT - 1))
                    mm.then_inc(unit_done, 1)

        def split_mm(out, u, blocks, start, stop):
            last = len(blocks) - 1
            for n, (w, a) in enumerate(((w_hi, in_hi), (w_hi, in_lo), (w_lo, in_hi))):
                for m, (b, k) in enumerate(blocks):
                    mm = pe.matmul(out, w[:, u, b * P:(b + 1) * P], a[:, k, :],
                                   start=start and n == 0 and m == 0, stop=stop and n == 2 and m == last)
            return mm

        def sum_tiles(out, src, ready, name, tiles=KT):
            for k in range(tiles):
                pe.wait_ge(*after(ready, k + 1))
                mm = pe.matmul(out, ones, src[:, k, :], start=(k == 0), stop=(k == tiles - 1))
            mm.then_inc(sem(name), 1)

        def transposes(src, tiles, banks, name, per_bank=2):
            for t in range(tiles):
                bank = banks[(t // 2) % len(banks)]
                if t % 2 == 0 and t // 2 >= len(banks):
                    pe.wait_ge(*after(f"{name}_natural", t // 2 - len(banks) + 1))
                for c in range(2):
                    mm = pe.transpose(ps[:, bank, (t % 2) * S + c * P:(t % 2) * S + (c + 1) * P],
                                      src[:, t, c * P:(c + 1) * P], ident)
                if t % 2 == 1:
                    mm.then_inc(sem(f"{name}_turned"), 1)

        def attention(name, heads, q, k, v):
            def scores(h):
                if h >= 2:
                    pe.wait_ge(*after(f"{name}_logits", h - 1))
                for qt in range(2):
                    qh = q(h)
                    mm = pe.matmul(half(4 + h % 2, qt), qh[:, qt * P:(qt + 1) * P], k(h), start=True, stop=True)
                mm.then_inc(sem(f"{name}_scores"), 1)

            scores(0)
            for h in range(heads):
                if h + 1 < heads:
                    scores(h + 1)
                pe.wait_ge(*after(f"{name}_probs", h + 1))
                if h >= 1:
                    pe.wait_ge(*after(f"{name}_pt", h))
                for qt in range(2):
                    for kt in range(2):
                        mm = pe.transpose(ps[:, 6, kt * S + qt * P:kt * S + (qt + 1) * P],
                                          lg[h % 2][:, qt, kt * P:(kt + 1) * P], ident)
                mm.then_inc(sem(f"{name}_turned_p"), 1)
                pe.wait_ge(*after(f"{name}_pt", h + 1))
                if h >= 1:
                    pe.wait_ge(*after(f"{name}_out", h))
                for kt in range(2):
                    vh = v(h, kt)
                    m = vh.shape[-1]
                    p0 = 64 * (h % 2) if m == 64 else 0
                    mm = pe.matmul(ps[p0:p0 + m, 7, 0:S], vh, pt[:, kt, :], start=(kt == 0), stop=(kt == 1))
                mm.then_inc(sem(f"{name}_pv"), 1)

        def add_partitions(chunks, name):
            for c in range(chunks):
                for n in range(KT):
                    mm = pe.matmul(ps[:, 7, c * KT + n:c * KT + n + 1], acc[:, c, n * P:(n + 1) * P], ones[:, 0:1],
                                   start=True, stop=True)
            mm.then_inc(sem(name), 1)

        pe.wait_ge(*after("consts_in", 16))
        pe.wait_ge(lo_done, 16)
        add_partitions(2, "mod_first")
        pe.wait_ge(*after("in0_lo", KT))
        project("moba_in", in_hi, in_lo)

        pe.wait_ge(lo_done, LOADED["moba_out"])
        add_partitions(4, "mod_rest")
        pe.wait_ge(taken, all_taken("moba_in"))
        transposes(proj[:, 16:24, :], 8, (4, 5, 6), "moba_v")
        pe.wait_ge(*after("moba_v_natural", 4))
        pe.wait_ge(*after("mod_read", 1))
        attention("moba", 8, lambda h: proj[:, h, :], lambda h: proj[:, 8 + h, :],
                  lambda h, kt: vnat[:, kt, h * P:(h + 1) * P])
        pe.wait_ge(*after("in1_lo", KT))
        project("moba_out", in_hi, in_lo)

        def norm_sums(tag, centred):
            if centred:
                sum_tiles(half(4, 0), x_t, f"{tag}_res", f"{tag}_sum")
            sum_tiles(half(5, 0), sq, f"{tag}_sq", f"{tag}_sumsq")

        norm_sums("ln0", True)

        pe.wait_ge(*after("in2_lo", KT))
        for r in range(2):
            for k in range(KT):
                mm = pe.matmul(ps[0:8, 6 + r, 0:S], gdn_wg[:, k, 8 * r:8 * r + 8], h_t[:, k, :],
                               start=(k == 0), stop=(k == KT - 1))
        mm.then_inc(sem("gdn_gates"), 1)
        project("gdn_in", in_hi, in_lo)
        pe.wait_ge(*after("gdn_rows", 2))
        for n, r in enumerate((2, 3)):
            for c in range(2):
                mm = pe.transpose(ps[:, 6, (2 * n + c) * 8:(2 * n + c) * 8 + 8], rows[0:8, r, c * P:(c + 1) * P],
                                  ident[0:8, 0:8])
        mm.then_inc(sem("gdn_cols"), 1)
        for t in range(16):
            pe.wait_ge(*after("gdn_sq", t + 1))
            if t >= 4:
                pe.wait_ge(*after("gdn_len", t - 3))
            pe.matmul(half(t % 4, 0), ones, gsq[:, t % 4, :], start=True, stop=True).then_inc(sem("gdn_sum"), 1)
        pe.wait_ge(*after("gdn_unit", 16))
        for sg in range(2):
            for p in range(2):
                g = 2 * sg + p
                if g >= 1:
                    pe.wait_ge(*after("gdn_a0", g))
                    pe.wait_ge(*after("gdn_kdg", 4 * g))
                if sg and not p:
                    pe.wait_ge(*after("gdn_o", 2 * sg))
                for m in range(2):
                    h = 2 * g + m
                    sel = ident[0:8, h:h + 1].to_broadcast([8, P])
                    pe.matmul(half(m, 0), sel, rows[0:8, 2, :], start=True, stop=True)
                    mm = pe.matmul(half(m, 1), sel, rows[0:8, 3, :], start=True, stop=True)
                mm.then_inc(sem("gdn_bc"), 1)
                for m in range(2):
                    h = 2 * g + m
                    for c in range(2):
                        j = 2 * m + c
                        pe.transpose(ps[:, 2, j * P:(j + 1) * P], proj[:, 8 + h, c * P:(c + 1) * P], ident)
                        mm = pe.transpose(ps[:, 3, j * P:(j + 1) * P], proj[:, 16 + h, c * P:(c + 1) * P], ident)
                mm.then_inc(sem("gdn_nat"), 1)
                pe.wait_ge(*after("gdn_kb", 2 * (g + 1)))
                for m in range(2):
                    h = 2 * g + m
                    for c in range(2):
                        kk = proj[:, 8 + h, c * P:(c + 1) * P]
                        j = 2 * m + c
                        pe.matmul(ps[:, 4, j * P:(j + 1) * P], kk, kb[:, m, c * P:(c + 1) * P], start=True, stop=True)
                        mm = pe.matmul(ps[:, 5, j * P:(j + 1) * P], kk, proj[:, h, c * P:(c + 1) * P], start=True, stop=True)
                mm.then_inc(sem("gdn_gram"), 1)
            for lv in range(LEVELS):
                for p in range(2):
                    n = (sg * LEVELS + lv) * 2 + p
                    t, tt = tri(8, 2 * sg + p), tri(16, 2 * sg + p)
                    pe.wait_ge(*after("gdn_ct", n + 1))
                    if lv == 0:
                        for j in range(4):
                            mm = pe.matmul(ps[:, 6 + p, j * P:(j + 1) * P], ctm[p][:, j, :], ident, start=True, stop=True)
                        mm.then_inc(sem("gdn_p"), 1)
                        continue
                    pe.wait_ge(*after("gdn_t", n - 1))
                    for j in range(4):
                        mm = pe.matmul(ps[:, 6 + p, j * P:(j + 1) * P], ctm[p][:, j, :], t[:, j, :], start=True, stop=True)
                    mm.then_inc(sem("gdn_p"), 1)
                for p in range(2):
                    if lv == 0:
                        continue
                    n = (sg * (LEVELS - 1) + lv - 1) * 2 + p
                    t, tt = tri(8, 2 * sg + p), tri(16, 2 * sg + p)
                    pe.wait_ge(*after("gdn_ps", n + 1))
                    if lv < LEVELS - 1:
                        for j in range(4):
                            pe.matmul(ps[:, 2 * p, j * P:(j + 1) * P], tt[:, j, :], pm[p][:, j, :], start=True, stop=True)
                    for j in range(4):
                        mm = pe.matmul(ps[:, 2 * p + 1, j * P:(j + 1) * P], pm[p][:, j, :], tt[:, j, :], start=True, stop=True)
                    mm.then_inc(sem("gdn_d"), 1)
            pe.wait_ge(*after("gdn_t", 2 * (sg + 1) * LEVELS))
            pe.wait_ge(*after("gdn_kdg", 8 * (sg + 1)))
            pe.wait_ge(*after("gdn_vb", 8 * (sg + 1)))
            pe.wait_ge(*after("gdn_aqk", 2 * (sg + 1)))
            pe.wait_ge(*after("gdn_qg", 2 * (sg + 1)))

            def each():
                for q in range(4):
                    p, m = divmod(q, 2)
                    tt = tri(16, 2 * sg + p)
                    yield q, slice(q * P, (q + 1) * P), p, 2 * m, tt[:, 2 * m, :], tt[:, 2 * m + 1, :]

            for q, c, p, j, t0, t1 in each():
                mm = pe.matmul(ps[:, 6, c], t0, vb[p][:, j, :], start=True, stop=True)
            mm.then_inc(sem("gdn_u0"), 1)
            for q, c, p, j, t0, t1 in each():
                mm = pe.matmul(ps[:, 7, c], kdg[p][:, j + 1, :], t1, start=True, stop=True)
            mm.then_inc(sem("gdn_w"), 1)
            pe.wait_ge(*after("gdn_u0s", sg + 1))
            for q, c, p, j, t0, t1 in each():
                mm = pe.matmul(ps[:, 5, c], kdg[p][:, j, :], u0[:, q, :], start=True, stop=True)
            mm.then_inc(sem("gdn_s1"), 1)
            pe.wait_ge(*after("gdn_s1s", sg + 1))
            pe.wait_ge(*after("gdn_ws", sg + 1))
            for q, c, p, j, t0, t1 in each():
                pe.matmul(ps[:, 4, c], t1, vb[p][:, j + 1, :], start=True, stop=False)
                mm = pe.matmul(ps[:, 4, c], wn[:, q, :], s1[:, q, :], start=False, stop=True)
            mm.then_inc(sem("gdn_v1"), 1)
            pe.wait_ge(*after("gdn_v1s", sg + 1))
            for q, c, p, j, t0, t1 in each():
                out = half(2 + q // 2, q % 2)
                pe.matmul(out[:, 0:P], u0[:, q, :], aqk[p][:, j, :], start=True, stop=True)
                pe.matmul(out[:, P:S], v1[:, q, :], aqk[p][:, j + 1, :], start=True, stop=False)
                mm = pe.matmul(out[:, P:S], s1[:, q, :], qg[:, q, :], start=False, stop=True)
                if q % 2:
                    mm.then_inc(sem("gdn_ot"), 1)
        for h in range(8):
            pe.wait_ge(*after("gdn_osq", h + 1))
            if h >= 4:
                pe.wait_ge(*after("gdn_rms", h - 3))
            pe.matmul(half(h % 4, 0), ones, gsq[:, h % 4, :], start=True, stop=True).then_inc(sem("gdn_osum"), 1)
        pe.wait_ge(*after("in3_lo", KT))
        project("gdn_out", in_hi, in_lo)
        norm_sums("ln1", True)

        norm_sums("mem", False)
        pe.wait_ge(*after("in4_lo", KT))
        project("mem_kv", in_hi, in_lo)
        norm_sums("mix", False)
        pe.wait_ge(*after("in5_lo", KT))
        for r in range(2):
            for k in range(KT):
                mm = pe.matmul(ps[0:ML_ROWS, 6 + r, 0:S], ml_wg[:, k, ML_ROWS * r:ML_ROWS * (r + 1)], h_t[:, k, :],
                               start=(k == 0), stop=(k == KT - 1))
        mm.then_inc(sem("ml_gates"), 1)
        pe.wait_ge(taken, all_taken("mem_kv"))
        transposes(memkv[:, 4:8, :], 4, (4, 5), "mem_v")
        project("w_in", in_hi, in_lo)
        pe.wait_ge(taken, all_taken("w_in"))

        pe.wait_ge(*after("mem_v_natural", 2))
        pe.wait_ge(*after("ml_gate_rows", 1))
        for n in range(2):
            for c in range(2):
                a = (2 * n + c) * 40
                mm = pe.transpose(ps[:, 4, a:a + ML_ROWS], rows[0:ML_ROWS, 4 + n, c * P:(c + 1) * P],
                                  ident[0:ML_ROWS, 0:ML_ROWS])
        mm.then_inc(sem("ml_cols"), 1)
        transposes(proj[:, 8:12, :], 4, (5, 6), "ml_v")
        pe.wait_ge(*after("ml_v_natural", 2))
        pe.wait_ge(*after("ml_qk", 8))
        pe.wait_ge(*after("ml_cols_taken", 3))
        for h in range(4):
            if h >= 1:
                pe.wait_ge(*after("ml_w", 2 * h))
            for qt in range(2):
                mm = pe.matmul(half(4, qt), proj[:, h, qt * P:(qt + 1) * P], proj[:, 4 + h, :], start=True, stop=True)
            for d in range(2):
                r = h + 32 * d
                sel = ident[0:ML_ROWS, r:r + 1].to_broadcast([ML_ROWS, P])
                mm = pe.matmul(half(5, d), sel, rows[0:ML_ROWS, 3, :], start=True, stop=True)
            mm.then_inc(sem("ml_scores"), 1)
            pe.wait_ge(*after("ml_w", 2 * (h + 1)))
            if h >= 1:
                pe.wait_ge(*after("ml_pt", h))
            for qt in range(2):
                for kt in range(2):
                    mm = pe.transpose(ps[:, 6, kt * S + qt * P:kt * S + (qt + 1) * P],
                                      wsum[:, qt, kt * P:(kt + 1) * P], ident)
            mm.then_inc(sem("ml_turned_p"), 1)
            pe.wait_ge(*after("ml_pt", h + 1))
            if h >= 1:
                pe.wait_ge(*after("ml_h", h))
            for kt in range(2):
                mm = pe.matmul(half(7, 0), vnat[:, kt, h * P:(h + 1) * P], pt[:, kt, :],
                               start=(kt == 0), stop=(kt == 1))
            mm.then_inc(sem("ml_pv"), 1)
        for h in range(4):
            pe.wait_ge(*after("ml_hsq", h + 1))
            pe.matmul(half(h, 0), ones, gsq[:, h, :], start=True, stop=True).then_inc(sem("ml_hsum"), 1)

        pe.wait_ge(*after("ml_h", 4))
        transposes(proj[:, 24:28, :], 4, (4, 5), "na_v")
        pe.wait_ge(*after("na_v_natural", 2))
        attention("na", 8, lambda h: proj[64 * (h % 2):64 * (h % 2) + 64, 16 + h // 2, :],
                  lambda h: proj[64 * (h % 2):64 * (h % 2) + 64, 20 + h // 2, :],
                  lambda h, kt: vnat[:, kt, h * 64:(h + 1) * 64])
        pe.wait_ge(*after("na_out", 8))
        attention("xa", 4, lambda h: proj[:, 28 + h, :], lambda h: memkv[:, h, :],
                  lambda h, kt: mem_vnat[:, kt, h * P:(h + 1) * P])

        pe.wait_ge(*after("ml_rms", 4))
        project("merge", in_hi, in_lo)
        pe.wait_ge(*after("in6m_lo", 4))
        pe.wait_ge(*after("na_out", 8))
        pe.wait_ge(*after("xa_out", 4))
        first = FIRST["branch"]
        for i in range(3):
            for u in range(GROUP):
                n = first + GROUP * i + u
                pe.wait_ge(lo_done, LOADED["branch"] + GROUP * i + u + 1)
                pe.wait_ge(taken, n + 1)
                for t in range(2):
                    mm = split_mm(half(u, t), u, [(4 * t + k, 8 + 4 * i + k) for k in range(4)], True, True)
                mm.then_inc(unit_done, 1)
        pe.wait_ge(*after("in7_lo", KT))
        project("w_out", in_hi, in_lo)
        norm_sums("ffn", False)
        pe.wait_ge(*after("in8_lo", KT))
        project("ffn_up", in_hi, in_lo)
        pe.wait_ge(*after("in9_lo", FT))
        first = FIRST["ffn_down"]
        with pe.Fori(0, 2) as i:
            for u in range(12):
                pe.wait_ge(lo_done, i * 12 + (LOADED["ffn_down"] + u + 1))
                if u % 3 == 0:
                    pe.wait_ge(taken, i * 4 + (first + u // 3 + 1))
                blocks = [(b, 8 * (u % 3) + b) for b in range(UNIT if u % 3 < 2 else FT - 2 * UNIT)]
                split_mm(ps[:, u // 3, 0:S], u % GROUP, blocks, u % 3 == 0, u % 3 == 2).then_inc(unit_done, 1)
        norm_sums("final", False)

    @block.scalar
    def _(act):
        act_in = [0]

        def link(ins):
            act_in[0] += 1
            ins.then_inc(sem("act_chain"), 1)
            act.wait_ge(*after("act_chain", act_in[0]))

        def high_part(r, u, i=None, stride=0):
            c = slice((r % PAIR) * UNIT * P, (r % PAIR + 1) * UNIT * P)
            if i is None:
                act.wait_ge(loaded, r // PAIR + 1)
                src = raw[:, (r // PAIR) % RAW, c]
            else:
                act.wait_ge(loaded, i * (stride // PAIR) + (r // PAIR + 1))
                slot = (i * (stride // PAIR) + r // PAIR) % RAW
                src = raw[:, bass.ds(slot, 1), c].rearrange("p a b -> p (a b)")
            act.copy(w_hi[:, u, :], src).then_inc(hi_done, 1)

        def high(name, n):
            if FIRST[name] + n >= GROUP:
                act.wait_ge(unit_done, FIRST[name] + n - GROUP + 1)
            high_part(LOADED[name] + n, n % GROUP)

        def project(name, evac, first_group=0, groups=None):
            first = FIRST[name]
            groups = COUNT[name] // GROUP if groups is None else groups
            with act.Fori(first_group, first_group + groups) as i:
                for u in range(GROUP):
                    act.wait_ge(unit_done, i * GROUP + (first + u + 1))
                    evac(i, u)
                    high_part(LOADED[name] + STRIDE[name] + u, u, i, STRIDE[name])

        def plain(dst):
            def evac(i, u):
                act.copy(dst[:, bass.ds(i * GROUP + u, 1), :], ps[:, u:u + 1, 0:S]).then_inc(taken, 1)
            return evac

        def split(tag, tiles, src, ready, ready_at, base=0):
            for k in range(tiles):
                act.wait_ge(*after(ready, ready_at(k)))
                act.copy(in_hi[:, base + k, :], src(k)).then_inc(sem(f"{tag}_hi"), 1)

        def squares(tag, src, ready=None):
            for k in range(KT):
                if ready:
                    act.wait_ge(*after(ready, k + 1))
                act.activation(sq[:, k, :], src[:, k, :], ACT.Square).then_inc(sem(f"{tag}_sq"), 1)

        def root(tag, eps):
            act.wait_ge(*after(f"{tag}_sumsq", 1))
            act.activation(stat[:, 1, :], half(5, 0), ACT.Sqrt, bias=eps_col(eps), scale=1.0 / D
                           ).then_inc(sem(f"{tag}_root"), 1)

        def eps_col(eps):
            return small[:, 1, 15:16] if eps == LN_EPS else small[:, 1, 14:15]

        def gdn_root(act, t):
            act.wait_ge(*after("gdn_sum", t + 1))
            if t >= 4:
                act.wait_ge(*after("gdn_unit", t - 3))
            act.activation(rb[:, t % 4, :], half(t % 4, 0), ACT.Sqrt, bias=eps_col(EPS)).then_inc(sem("gdn_len"), 1)

        def gdn_out_root(act, h):
            act.wait_ge(*after("gdn_osum", h + 1))
            if h >= 4:
                act.wait_ge(*after("gdn_gated", h - 3))
            act.activation(rb[:, h % 4, :], half(h % 4, 0), ACT.Sqrt, bias=eps_col(EPS), scale=1.0 / P
                           ).then_inc(sem("gdn_rms"), 1)

        act.sem_inc(taken, GROUP)
        act.wait_ge(*after("params_in", 16))
        act.activation(cs[:], param("c", 0, 8), ACT.Silu).then_inc(sem("cs_ready"), 1)
        act.wait_ge(*after("cs_ready", 1))
        for n in range(GROUP):
            high("moba_in", n)
        split("in0", KT, lambda k: h_t[:, k, :], "h0", lambda k: k + 1)
        project("moba_in", plain(proj))

        def natural(name, tiles, banks, dst):
            for g in range(tiles // 2):
                act.wait_ge(*after(f"{name}_turned", g + 1))
                act.copy(dst[:, :, 2 * g * P:2 * (g + 1) * P].rearrange("p c (t d) -> p t c d", t=2),
                         ps[:, banks[g % len(banks)], :].rearrange("p (t c d) -> p t c d", t=2, c=2)
                         ).then_inc(sem(f"{name}_natural"), 1)

        def attention(name, heads, finish):
            for h in range(heads + 1):
                if h < heads:
                    act.wait_ge(*after(f"{name}_max", h + 1))
                    for qt in range(2):
                        act.activation(lg[h % 2][:, qt, :], lg[h % 2][:, qt, :], ACT.Exp,
                                       bias=small[:, 0, 4 * (h % 2) + qt:4 * (h % 2) + qt + 1],
                                       accum_out=small[:, 0, 4 * (h % 2) + 2 + qt:4 * (h % 2) + 3 + qt]
                                       ).then_inc(sem(f"{name}_exp"), 1)
                if h >= 1:
                    finish(h - 1)
                if h < heads:
                    act.wait_ge(*after(f"{name}_turned_p", h + 1))
                    if h >= 1:
                        act.wait_ge(*after(f"{name}_pv", h))
                    act.copy(flat(pt), ps[:, 6, :]).then_inc(sem(f"{name}_pt"), 1)

        act.wait_ge(taken, all_taken("moba_in"))
        act.activation(proj[:, 24:32, :], proj[:, 24:32, :], ACT.Silu).then_inc(sem("moba_z"), 1)
        natural("moba_v", 8, (4, 5, 6), vnat)

        def moba_finish(h):
            act.wait_ge(*after("moba_out", h + 1))
            act.copy(in_hi[:, h, :], gated[h % 2]).then_inc(sem("in1_hi"), 1)

        attention("moba", 8, moba_finish)
        project("moba_out", plain(proj))

        def layer_norm(tag, layer, out_h):
            squares(tag, x_t, f"{tag}_centred")
            root(tag, LN_EPS)
            for k in range(KT):
                act.wait_ge(*after(f"{tag}_scaled", k + 1))
                act.activation(x_t[:, k, :], sq[:, k, :], ACT.Identity, bias=param("ln_b", 8 * layer + k)
                               ).then_inc(sem(f"{tag}_x"), 1)
            if out_h:
                for k in range(KT):
                    act.wait_ge(*after(f"{tag}_x", k + 1))
                    act.activation(h_t[:, k, :], x_t[:, k, :], ACT.Identity, bias=mod[:, 1, k:k + 1],
                                   scale=mod[:, 1, 8 + k:9 + k]).then_inc(sem("h1"), 1)

        layer_norm("ln0", 0, True)
        split("in2", KT, lambda k: h_t[:, k, :], "h1", lambda k: k + 1)

        act.activation(gexp[0:8, 2, 0:1], param("a_log", 0, 1, 8), ACT.Exp).then_inc(sem("gdn_a"), 1)
        act.wait_ge(*after("gdn_gates", 1))
        act.activation(rows[0:8, 3, :], ps[0:8, 7, 0:S], ACT.Sigmoid).then_inc(sem("gdn_rows"), 1)
        act.wait_ge(*after("gdn_z", 1))
        link(act.activation(rows[0:8, 1, :], rows[0:8, 0, :], ACT.Abs))
        link(act.activation(rows[0:8, 1, :], rows[0:8, 1, :], ACT.Exp, scale=-1.0))
        act.activation(rows[0:8, 1, :], rows[0:8, 1, :], ACT.Ln, bias=1.0).then_inc(sem("gdn_ln"), 1)

        def evac_conv(i, u):
            act.wait_ge(*after("conv_free", i * GROUP + (u + 1)))
            act.copy(cin[u][:, 3:3 + S], ps[:, u, 0:S])
            act.activation(proj[:, bass.ds(i * GROUP + u, 1), :], ps[:, u:u + 1, 0:S], ACT.Copy,
                           scale=params[:, bass.ds(i * GROUP + (PCOL["gdn_conv"] + 72 + u), 1)]).then_inc(taken, 1)

        project("gdn_in", evac_conv, groups=6)
        project("gdn_in", plain(proj), first_group=6, groups=2)
        act.wait_ge(taken, all_taken("gdn_in"))
        act.wait_ge(*after("conv_free", GROUP + 24))
        for n in range(8):
            act.activation(proj[:, 4 * n:4 * n + 4, :], proj[:, 4 * n:4 * n + 4, :], ACT.Silu
                           ).then_inc(sem("gdn_silu"), 1)
        act.wait_ge(*after("gdn_cols", 1))
        act.copy(gcol[:].rearrange("p a b c -> p (a b c)"), ps[:, 6, 0:32]).then_inc(sem("gdn_col_done"), 1)
        for t in range(16):
            act.wait_ge(*after("gdn_silu", t // 4 + 1))
            if t >= 4:
                act.wait_ge(*after("gdn_sum", t - 3))
            act.activation(gsq[:, t % 4, :], proj[:, t, :], ACT.Square).then_inc(sem("gdn_sq"), 1)
            if t >= 3:
                gdn_root(act, t - 3)
        for t in range(13, 16):
            gdn_root(act, t)
        act.wait_ge(*after("gdn_col_done", 1))
        act.activation(gexp[:, 1, :], gcol[:, 0, 1, :], ACT.Exp).then_inc(sem("gdn_e1"), 1)
        for sg in range(2):
            for p in range(2):
                g = 2 * sg + p
                act.wait_ge(*after("gdn_bc", g + 1))
                if sg:
                    act.wait_ge(*after("gdn_ot", 2 * sg))
                for m in range(2):
                    act.activation(qg[:, 2 * p + m, :], ps[:, m, P:S], ACT.Exp).then_inc(sem("gdn_qe"), 1)
                act.wait_ge(*after("gdn_diff", g + 1))
                act.activation(flat(dec), flat(dec), ACT.Exp).then_inc(sem("gdn_dec"), 1)
                act.wait_ge(*after("gdn_nat", g + 1))
                act.wait_ge(*after("gdn_e0", 2 * (g + 1)))
                act.wait_ge(*after("gdn_e1", 2))
                link(act.activation(gexp[:, 0, 2 * g:2 * g + 2], gexp[:, 2, 2 * g:2 * g + 2], ACT.Exp))
                for m in range(2):
                    h = 2 * g + m
                    for c in range(2):
                        j = 2 * m + c
                        act.activation(kdg[p][:, j, :], ps[:, 2, j * P:(j + 1) * P], ACT.Copy,
                                       scale=gexp[:, c, h:h + 1]).then_inc(sem("gdn_kdg"), 1)
            for lv in range(1, LEVELS):
                for p in range(2):
                    act.wait_ge(*after("gdn_p", (sg * LEVELS + lv) * 2 + p + 1))
                    act.copy(flat(pm[p]), ps[:, 6 + p, :]).then_inc(sem("gdn_ps"), 1)
            act.wait_ge(*after("gdn_u0", sg + 1))
            act.copy(flat(u0), ps[:, 6, :]).then_inc(sem("gdn_u0s"), 1)
            act.wait_ge(*after("gdn_w", sg + 1))
            act.mul(flat(wn), ps[:, 7, :], -1.0).then_inc(sem("gdn_ws"), 1)
            for q in range(2):
                act.wait_ge(*after("gdn_ot", 2 * sg + q + 1))
                act.copy(flat(proj[:, 4 * sg + 2 * q:4 * sg + 2 * q + 2, :]), ps[:, 2 + q, :]).then_inc(sem("gdn_o"), 1)
        for h in range(8):
            act.wait_ge(*after("gdn_o", h // 2 + 1))
            if h >= 4:
                act.wait_ge(*after("gdn_osum", h - 3))
            act.activation(gsq[:, h % 4, :], proj[:, h, :], ACT.Square).then_inc(sem("gdn_osq"), 1)
            if h >= 3:
                gdn_out_root(act, h - 3)
        for h in range(5, 8):
            gdn_out_root(act, h)
        split("in3", KT, lambda k: proj[:, k, :], "gdn_gated", lambda k: k + 1)
        project("gdn_out", plain(proj))
        layer_norm("ln1", 1, False)

        act.wait_ge(*after("mem_in", 16))
        act.wait_ge(*after("ln1_x", KT))
        squares("mem", proj[:, 8:16, :])
        root("mem", EPS)
        split("in4", KT, lambda k: h_t[:, k, :], "mem_h", lambda k: k + 1)
        project("mem_kv", plain(memkv))
        act.wait_ge(*after("ln1_x", KT))
        squares("mix", x_t)
        root("mix", EPS)
        split("in5", KT, lambda k: h_t[:, k, :], "mix_h", lambda k: k + 1)
        natural("mem_v", 4, (4, 5), mem_vnat)
        act.wait_ge(*after("ml_pre", 2))
        link(act.activation(rows[:, 2, :], rows[:, 1, :], ACT.Abs))
        link(act.activation(rows[:, 2, :], rows[:, 2, :], ACT.Exp, scale=-1.0))
        act.activation(rows[:, 2, :], rows[:, 2, :], ACT.Ln, bias=1.0).then_inc(sem("ml_ln"), 1)
        project("w_in", plain(proj))
        act.wait_ge(taken, all_taken("w_in"))
        act.activation(proj[:, 12:16, :], proj[:, 12:16, :], ACT.Sigmoid).then_inc(sem("ml_o"), 1)
        for t in range(8):
            act.wait_ge(*after("ml_conv", t + 1))
            act.activation(proj[:, t, :], gsq[:, t % 4, :], ACT.Silu, bias=param("ml_conv_b", t)
                           ).then_inc(sem("ml_qk"), 1)
        act.wait_ge(*after("ml_cols", 1))
        for c in range(2):
            act.activation(mcol[:, 1, c, :], ps[:, 4, (2 + c) * 40:(2 + c) * 40 + ML_ROWS], ACT.Exp, scale=-1.0
                           ).then_inc(sem("ml_cols_taken"), 1)
        natural("ml_v", 4, (5, 6), vnat)
        for h in range(4):
            act.wait_ge(*after("ml_diff", h + 1))
            act.activation(flat(eb), flat(eb), ACT.Exp).then_inc(sem("ml_exp"), 1)
            act.wait_ge(*after("ml_turned_p", h + 1))
            if h >= 1:
                act.wait_ge(*after("ml_pv", h))
            act.copy(flat(pt), ps[:, 6, :]).then_inc(sem("ml_pt"), 1)
            act.wait_ge(*after("ml_pv", h + 1))
            act.copy(proj[:, h, :], half(7, 0)).then_inc(sem("ml_h"), 1)
            act.wait_ge(*after("ml_h", h + 1))
            act.activation(gsq[:, h, :], proj[:, h, :], ACT.Square).then_inc(sem("ml_hsq"), 1)
        for h in range(4):
            act.wait_ge(*after("ml_hsum", h + 1))
            act.activation(eb[:, h, :], half(h, 0), ACT.Sqrt, bias=eps_col(EPS), scale=1.0 / P
                           ).then_inc(sem("ml_root"), 1)
        split("in6m", 4, lambda k: proj[:, k, :], "ml_rms", lambda k: k + 1, base=8)

        def high_of(name, base, h, rows_):
            act.wait_ge(*after(f"{name}_pv", h + 1))
            p0 = rows_ * (h % 2) if rows_ == 64 else 0
            t = h // 2 if rows_ == 64 else h
            act.copy(in_hi[p0:p0 + rows_, base + t, :], ps[p0:p0 + rows_, 7, 0:S]).then_inc(sem(f"{name}_high"), 1)

        natural("na_v", 4, (4, 5), vnat)
        attention("na", 8, lambda h: high_of("na", 12, h, 64))
        attention("xa", 4, lambda h: high_of("xa", 16, h, P))

        def evac_gate(i, u):
            act.activation(proj[:, bass.ds(i * GROUP + u, 1), :], ps[:, u:u + 1, 0:S], ACT.Sigmoid,
                           bias=params[:, bass.ds(i * GROUP + (PCOL["merge_b"] + u), 1)]).then_inc(taken, 1)

        act.wait_ge(*after("in6m_lo", 4))
        project("merge", evac_gate)
        act.wait_ge(taken, all_taken("merge"))
        for n in range(COUNT["branch"]):
            high("branch", n + GROUP)
        split("in7", KT, lambda k: h_t[:, k, :], "merged", lambda k: 9 + k // 2)
        project("w_out", plain(proj))
        squares("ffn", x_t, "ffn_res")
        root("ffn", EPS)
        split("in8", KT, lambda k: h_t[:, k, :], "ffn_h", lambda k: k + 1)

        first = FIRST["ffn_up"]
        with act.Fori(0, COUNT["ffn_up"] // GROUP) as i:
            for m in range(2):
                act.wait_ge(unit_done, i * GROUP + (first + 2 * m + 1))
                act.wait_ge(*after("ffn_pair_free", i * 2 + (m + 1)))
                act.copy(cin[m][:, 1:1 + S], ps[:, 2 * m, 0:S]).then_inc(taken, 1)
                act.wait_ge(unit_done, i * GROUP + (first + 2 * m + 2))
                act.copy(fbuf[m][:, 1, :], ps[:, 2 * m + 1, 0:S]).then_inc(taken, 1)
                for u in (2 * m, 2 * m + 1):
                    high_part(LOADED["ffn_up"] + GROUP + u, u, i, GROUP)
                act.wait_ge(*after("ffn_conv", i * 6 + (3 * m + 3)))
                act.activation(fbuf[m][:, 0, :], fbuf[m][:, 0, :], ACT.Gelu_apprx_tanh,
                               bias=params[:, bass.ds(i * 2 + (PCOL["ffn_conv_b"] + m), 1)]).then_inc(sem("ffn_gelu"), 1)
        split("in9", FT, lambda k: proj[:, k, :], "ffn_pair_free", lambda k: 2 + k + 1)
        first = FIRST["ffn_down"]
        for n in range(COUNT["ffn_down"]):
            if n % 3 == 2:
                act.wait_ge(unit_done, first + n + 1)
                act.copy(proj[:, 22 + n // 3, :], ps[:, (n // 3) % 4, 0:S]).then_inc(taken, 1)
            if first + n + GROUP < UNITS:
                high("ffn_down", n + GROUP)
        squares("final", x_t, "final_res")
        root("final", EPS)

    @block.vector
    def _(dve):
        count = [0]

        def link(ins):
            count[0] += 1
            ins.then_inc(sem("dve_chain"), 1)
            dve.wait_ge(*after("dve_chain", count[0]))

        def unit_at(r, i=None, stride=0):
            c = slice((r % PAIR) * UNIT * P, (r % PAIR + 1) * UNIT * P)
            if i is None:
                return raw[:, (r // PAIR) % RAW, c]
            slot = (i * (stride // PAIR) + r // PAIR) % RAW
            return raw[:, bass.ds(slot, 1), c].rearrange("p a b -> p (a b)")

        def low_part(src, u):
            dve.tensor_tensor(w_lo[:, u, :], src, w_hi[:, u, :].bitcast(F32), ALU.subtract).then_inc(lo_done, 1)

        def low(name, n):
            dve.wait_ge(hi_done, FIRST[name] + n + 1)
            low_part(unit_at(LOADED[name] + n), n % GROUP)

        def low_in_loop(name, i, u):
            dve.wait_ge(hi_done, i * GROUP + (FIRST[name] + u + GROUP + 1))
            low_part(unit_at(LOADED[name] + STRIDE[name] + u, i, STRIDE[name]), u)

        def project(name, before=None, first_group=0, groups=None):
            groups = COUNT[name] // GROUP if groups is None else groups
            with dve.Fori(first_group, first_group + groups) as i:
                for u in range(GROUP):
                    if before:
                        before(i, u)
                    low_in_loop(name, i, u)

        def split(tag, tiles, src, base=0):
            for k in range(tiles):
                dve.wait_ge(*after(f"{tag}_hi", k + 1))
                dve.tensor_tensor(in_lo[:, base + k, :], src(k), in_hi[:, base + k, :].bitcast(F32), ALU.subtract
                                  ).then_inc(sem(f"{tag}_lo"), 1)

        def h_tile(k):
            return h_t[:, k, :]

        for m in range(GROUP):
            link(dve.memset(cin[m], 0.0))
        link(dve.memset(small[:, 1, 14:15], EPS))
        link(dve.memset(small[:, 1, 15:16], LN_EPS))
        dve.memset(rows[:], 0.0).then_inc(sem("rows_zero"), 1)
        dve.sem_inc(sem("conv_free"), GROUP)
        dve.wait_ge(*after("cs_ready", 1))
        for t in range(16):
            c, k = divmod(t, KT)
            dve.wait_ge(loaded, t // PAIR + 1)
            if k == 0:
                ins = dve.tensor_scalar(acc[:, c, :], unit_at(t), cs[:, 0:1], None, ALU.mult)
            else:
                dve.wait_ge(lo_done, t)
                ins = dve.scalar_tensor_tensor(acc[:, c, :], unit_at(t), cs[:, k:k + 1], acc[:, c, :],
                                               ALU.mult, ALU.add)
            ins.then_inc(lo_done, 1)
        for n in range(GROUP):
            low("moba_in", n)

        def modulation(at, chunks, name):
            flat_mod, one_plus = mod[:].rearrange("p a b -> p (a b)"), KT if at == 0 else 4 * KT
            dve.wait_ge(*after(name, 1))
            link(dve.tensor_tensor(flat_mod[:, KT * at:KT * (at + chunks)], ps[:, 7, 0:KT * chunks],
                                   param("ada_b", KT * at, KT * chunks), ALU.add))
            scale = flat_mod[:, one_plus:one_plus + KT]
            link(dve.tensor_scalar(scale, scale, 1.0, None, ALU.add))

        modulation(0, 2, "mod_first")
        dve.wait_ge(*after("x_in", 16))
        for k in range(KT):
            dve.tensor_scalar(h_t[:, k, :], x_t[:, k, :], mod[:, 0, 8 + k:9 + k], mod[:, 0, k:k + 1], ALU.mult, ALU.add
                              ).then_inc(sem("h0"), 1)
        split("in0", KT, h_tile)
        dve.tensor_scalar(x_t[:], x_t[:], ALPHA, None, ALU.mult).then_inc(sem("x_alpha"), 1)
        dve.wait_ge(*after("acc_zero", 1))
        with dve.Fori(0, 8) as i:
            for u in range(GROUP):
                r = LOADED["moba_in"] + GROUP + u
                dve.wait_ge(loaded, i * (8 // PAIR) + (r // PAIR + 1))
                dve.wait_ge(lo_done, i * 8 + r)
                a = acc[:, bass.ds(i // 2, 1), :].rearrange("p a b -> p (a b)")
                dve.scalar_tensor_tensor(a, unit_at(r, i, 8), cs[:, bass.ds((i % 2) * GROUP + u, 1)], a,
                                         ALU.mult, ALU.add).then_inc(lo_done, 1)
            for u in range(GROUP):
                low_in_loop("moba_in", i, u)
        modulation(2, 4, "mod_rest")
        dve.sem_inc(sem("mod_read"), 1)

        def attention(name, heads, logits, finish):
            for h in range(heads + 1):
                if h < heads:
                    dve.wait_ge(*after(f"{name}_scores", h + 1))
                    if h >= 2:
                        dve.wait_ge(*after(f"{name}_turned_p", h - 1))
                    logits(h)
                    dve.wait_ge(*after(f"{name}_logits", h + 1))
                    dve.tensor_reduce(small[:, 0, 4 * (h % 2):4 * (h % 2) + 2], lg[h % 2], X, ALU.max, negate=True
                                      ).then_inc(sem(f"{name}_max"), 1)
                    dve.wait_ge(*after(f"{name}_exp", 2 * h + 2))
                    a = small[:, 0, 4 * (h % 2) + 2:4 * (h % 2) + 4]
                    link(dve.reciprocal(a, a))
                    for qt in range(2):
                        ins = dve.tensor_scalar(lg[h % 2][:, qt, :], lg[h % 2][:, qt, :], a[:, qt:qt + 1], None, ALU.mult)
                    ins.then_inc(sem(f"{name}_probs"), 1)
                if h >= 1:
                    finish(h - 1)

        def low_of(name, base, h, rows_):
            dve.wait_ge(*after(f"{name}_high", h + 1))
            p0 = rows_ * (h % 2) if rows_ == 64 else 0
            t = h // 2 if rows_ == 64 else h
            dve.tensor_tensor(in_lo[p0:p0 + rows_, base + t, :], ps[p0:p0 + rows_, 7, 0:S],
                              in_hi[p0:p0 + rows_, base + t, :].bitcast(F32), ALU.subtract).then_inc(sem(f"{name}_out"), 1)

        def moba_logits(h):
            for qt in range(2):
                ins = dve.scalar_tensor_tensor(lg[h % 2][:, qt, :], half(4 + h % 2, qt), float(P) ** -0.5,
                                               strip("neg", qt), ALU.mult, ALU.add)
            ins.then_inc(sem("moba_logits"), 1)

        def moba_finish(h):
            dve.wait_ge(*after("moba_pv", h + 1))
            if h >= 2:
                dve.wait_ge(*after("in1_hi", h - 1))
            dve.tensor_tensor(gated[h % 2], half(7, 0), proj[:, 24 + h, :], ALU.mult).then_inc(sem("moba_out"), 1)
            dve.wait_ge(*after("in1_hi", h + 1))
            dve.tensor_tensor(in_lo[:, h, :], gated[h % 2], in_hi[:, h, :].bitcast(F32), ALU.subtract
                              ).then_inc(sem("in1_lo"), 1)

        dve.wait_ge(*after("moba_z", 1))
        attention("moba", 8, moba_logits, moba_finish)
        project("moba_out")

        def layer_norm(tag, layer, name):
            dve.wait_ge(taken, all_taken(name))
            for k in range(KT):
                dve.scalar_tensor_tensor(x_t[:, k, :], proj[:, k, :], mod[:, layer, 16 + k:17 + k], x_t[:, k, :],
                                         ALU.mult, ALU.add).then_inc(sem(f"{tag}_res"), 1)
            dve.wait_ge(*after(f"{tag}_sum", 1))
            link(dve.tensor_scalar(stat[:, 0, :], half(4, 0), 1.0 / D, None, ALU.mult))
            for k in range(KT):
                dve.tensor_tensor(x_t[:, k, :], x_t[:, k, :], stat[:, 0, :], ALU.subtract
                                  ).then_inc(sem(f"{tag}_centred"), 1)
            dve.wait_ge(*after(f"{tag}_root", 1))
            link(dve.reciprocal(stat[:, 1, :], stat[:, 1, :]))
            for k in range(KT):
                dve.scalar_tensor_tensor(sq[:, k, :], x_t[:, k, :], param("ln_g", 8 * layer + k), stat[:, 1, :],
                                         ALU.mult, ALU.mult).then_inc(sem(f"{tag}_scaled"), 1)

        def rms(tag, src, dst, gain, done):
            dve.wait_ge(*after(f"{tag}_root", 1))
            link(dve.reciprocal(stat[:, 1, :], stat[:, 1, :]))
            for k in range(KT):
                dve.scalar_tensor_tensor(dst[:, k, :], src[:, k, :], param(gain, k), stat[:, 1, :],
                                         ALU.mult, ALU.mult).then_inc(sem(done), 1)

        layer_norm("ln0", 0, "moba_out")
        split("in2", KT, h_tile)

        dve.wait_ge(*after("h1", KT))
        dve.tensor_scalar(x_t[:], x_t[:], ALPHA, None, ALU.mult).then_inc(sem("x_alpha"), 1)
        for m in range(GROUP):
            dve.memset(cin[m][:, 0:3], 0.0).then_inc(sem("edges"), 1)
        dve.wait_ge(*after("gdn_gates", 1))
        dve.tensor_scalar(rows[0:8, 0, :], ps[0:8, 6, 0:S], param("dt_bias", 0, 1, 8), None, ALU.add
                          ).then_inc(sem("gdn_z"), 1)
        dve.wait_ge(*after("gdn_ln", 1))
        link(dve.scalar_tensor_tensor(rows[0:8, 0, :], rows[0:8, 0, :], 0.0, rows[0:8, 1, :], ALU.max, ALU.add))
        dve.wait_ge(*after("gdn_a", 1))
        link(dve.tensor_scalar(rows[0:8, 0, :], rows[0:8, 0, :], gexp[0:8, 2, 0:1], -1.0, ALU.mult, ALU.mult))
        for c in range(2):
            ins = dve.tensor_tensor_scan(rows[0:8, 2, c * P:(c + 1) * P], rows[0:8, 4, c * P:(c + 1) * P],
                                         rows[0:8, 0, c * P:(c + 1) * P], 0.0, ALU.add, ALU.add)
        ins.then_inc(sem("gdn_rows"), 1)

        def conv(i, u):
            first = FIRST["gdn_in"]
            dve.wait_ge(taken, i * GROUP + (GROUP + first + u + 1))
            tile = proj[:, bass.ds(i * GROUP + u, 1), :]
            for n, tap in enumerate((2, 1, 0)):
                if n:
                    dve.wait_ge(*after("conv_tap", i * 8 + (2 * u + n)))
                ins = dve.scalar_tensor_tensor(tile, cin[u][:, tap:tap + S].rearrange("p (a b) -> p a b", a=1),
                                               params[:, bass.ds(i * GROUP + (PCOL["gdn_conv"] + 24 * tap + u), 1)],
                                               tile, ALU.mult, ALU.add)
                ins.then_inc(sem("conv_tap") if n < 2 else sem("conv_free"), 1)

        dve.wait_ge(*after("edges", GROUP))
        project("gdn_in", conv, groups=6)
        project("gdn_in", first_group=6, groups=2)
        for t in range(16):
            dve.wait_ge(*after("gdn_len", t + 1))
            link(dve.reciprocal(rb[:, t % 4, :], rb[:, t % 4, :]))
            dve.scalar_tensor_tensor(proj[:, t, :], proj[:, t, :], float(P) ** -0.5 if t < 8 else 1.0, rb[:, t % 4, :],
                                     ALU.mult, ALU.mult).then_inc(sem("gdn_unit"), 1)
        dve.wait_ge(*after("gdn_e1", 1))
        dve.tensor_tensor(gexp[:, 1, :], gexp[:, 1, :], gcol[:, 1, 1, :], ALU.mult).then_inc(sem("gdn_e1"), 1)
        dve.wait_ge(*after("gdn_unit", 16))
        one = ident.rearrange("p (a b) -> p a b", a=1).to_broadcast([P, 4, P])
        for sg in range(2):
            for p in range(2):
                g = 2 * sg + p
                dve.wait_ge(*after("gdn_bc", g + 1))
                dve.wait_ge(*after("gdn_qe", 2 * (g + 1)))
                if g:
                    dve.wait_ge(*after("gdn_gram", g))
                    dve.wait_ge(*after("gdn_a0", g))
                for m in range(2):
                    h = 2 * g + m
                    dve.tensor_tensor(kb[:, m, :], half(m, 1), proj[:, 8 + h, :], ALU.mult).then_inc(sem("gdn_kb"), 1)
                    dve.tensor_scalar(gexp[:, 2, h:h + 1], ps[:, m, P - 1:P], gcol[:, 0, 0, h:h + 1], None, ALU.subtract
                                      ).then_inc(sem("gdn_e0"), 1)
                    for c in range(2):
                        ins = dve.tensor_scalar(dec[:, 2 * m + c, :], ps[:, m, c * P:(c + 1) * P],
                                                gcol[:, 0, c, h:h + 1], 0.0, ALU.subtract, ALU.min)
                ins.then_inc(sem("gdn_diff"), 1)
                dve.wait_ge(*after("gdn_nat", g + 1))
                for m in range(2):
                    for c in range(2):
                        j = 2 * m + c
                        dve.tensor_scalar(vb[p][:, j, :], ps[:, 3, j * P:(j + 1) * P],
                                          gcol[:, 1, c, 2 * g + m:2 * g + m + 1], None, ALU.mult).then_inc(sem("gdn_vb"), 1)
                dve.wait_ge(*after("gdn_gram", g + 1))
                dve.wait_ge(*after("gdn_dec", g + 1))
                dve.tensor_tensor(flat(lt[p]), ps[:, 4, :], flat(dec), ALU.mult).then_inc(sem("gdn_lt"), 1)
                dve.tensor_tensor(flat(aqk[p]), ps[:, 5, :], flat(dec), ALU.mult).then_inc(sem("gdn_a0"), 1)
            for lv in range(LEVELS):
                for p in range(2):
                    n = (sg * LEVELS + lv) * 2 + p
                    t, tt = tri(8, 2 * sg + p), tri(16, 2 * sg + p)
                    if lv == 0:
                        dve.wait_ge(*after("gdn_p", n + 1))
                        dve.tensor_tensor(t, one, ps[:, 6 + p, :].rearrange("p (a b) -> p a b", a=4), ALU.subtract)
                        dve.tensor_tensor(tt, one, ctm[p], ALU.subtract).then_inc(sem("gdn_t"), 1)
                        continue
                    dve.wait_ge(*after("gdn_t", n - 1))
                    dve.wait_ge(*after("gdn_d", (sg * (LEVELS - 1) + lv - 1) * 2 + p + 1))
                    if lv < LEVELS - 1:
                        dve.tensor_tensor(t, t, ps[:, 2 * p, :].rearrange("p (a b) -> p a b", a=4), ALU.subtract)
                    dve.tensor_tensor(tt, tt, ps[:, 2 * p + 1, :].rearrange("p (a b) -> p a b", a=4), ALU.subtract
                                      ).then_inc(sem("gdn_t"), 1)
            dve.wait_ge(*after("gdn_s1", sg + 1))
            dve.tensor_copy(flat(s1), ps[:, 5, :]).then_inc(sem("gdn_s1s"), 1)
            dve.wait_ge(*after("gdn_v1", sg + 1))
            dve.tensor_copy(flat(v1), ps[:, 4, :]).then_inc(sem("gdn_v1s"), 1)
        for h in range(8):
            dve.wait_ge(*after("gdn_rms", h + 1))
            link(dve.reciprocal(rb[:, h % 4, :], rb[:, h % 4, :]))
            link(dve.scalar_tensor_tensor(proj[:, h, :], proj[:, h, :], param("gdn_norm"), rb[:, h % 4, :],
                                          ALU.mult, ALU.mult))
            dve.tensor_tensor(proj[:, h, :], proj[:, h, :], proj[:, 24 + h, :], ALU.mult).then_inc(sem("gdn_gated"), 1)
        split("in3", KT, lambda k: proj[:, k, :])
        project("gdn_out")
        layer_norm("ln1", 1, "gdn_out")

        rms("mem", proj[:, 8:16, :], h_t, "mem_norm", "mem_h")
        split("in4", KT, h_tile)
        project("mem_kv")
        rms("mix", x_t, h_t, "mix_norm", "mix_h")
        split("in5", KT, h_tile)
        dve.wait_ge(*after("ml_gates", 1))
        dve.tensor_scalar(rows[:, 0, :], ps[0:ML_ROWS, 6, 0:S], param("b_ig", 0, 1, ML_ROWS), None, ALU.add
                          ).then_inc(sem("ml_pre"), 1)
        dve.tensor_scalar(rows[:, 1, :], ps[0:ML_ROWS, 7, 0:S], param("b_fg", 0, 1, ML_ROWS), None, ALU.add
                          ).then_inc(sem("ml_pre"), 1)
        dve.wait_ge(*after("ml_ln", 1))
        link(dve.scalar_tensor_tensor(rows[:, 1, :], rows[:, 1, :], 0.0, rows[:, 2, :], ALU.min, ALU.subtract))
        link(dve.memset(rows[:, 4, :], 0.0))
        link(dve.tensor_tensor_scan(rows[:, 2, :], rows[:, 4, :], rows[:, 1, :], 0.0, ALU.add, ALU.add))
        link(dve.tensor_tensor(rows[32:36, 2, :], rows[32:36, 1, :], rows[32:36, 2, :], ALU.subtract))
        link(dve.tensor_tensor(rows[:, 3, :], rows[:, 0, :], rows[:, 2, :], ALU.subtract))
        link(dve.tensor_tensor_scan(rows[0:4, 4, :], rows[0:4, 3, :], rows[0:4, 3, :], NEG, ALU.max, ALU.max))
        link(dve.tensor_tensor_scan(rows[32:36, 4, ::-1], rows[32:36, 3, ::-1], rows[32:36, 3, ::-1], NEG, ALU.max, ALU.max))
        link(dve.tensor_tensor(rows[:, 5, :], rows[:, 2, :], rows[:, 4, :], ALU.add))
        dve.tensor_scalar(rows[:, 5, :], rows[:, 5, :], -88.0, None, ALU.max).then_inc(sem("ml_gate_rows"), 1)
        project("w_in")
        dve.wait_ge(taken, all_taken("w_in"))
        for t in range(8):
            if t >= 4:
                dve.wait_ge(*after("ml_qk", t - 3))
            out, src = gsq[:, t % 4, :], proj[:, t, :]
            link(dve.tensor_scalar(out, src, param("ml_conv", 8 + t), None, ALU.mult))
            link(dve.scalar_tensor_tensor(out[:, 1:S], src[:, 0:S - 1], param("ml_conv", t), out[:, 1:S], ALU.mult, ALU.add))
            dve.scalar_tensor_tensor(out[:, 0:S - 1], src[:, 1:S], param("ml_conv", 16 + t), out[:, 0:S - 1],
                                     ALU.mult, ALU.add).then_inc(sem("ml_conv"), 1)
        dve.wait_ge(*after("ml_cols", 1))
        dve.wait_ge(*after("ml_cols_taken", 2))
        for c in range(2):
            link(dve.tensor_copy(mcol[:, 0, c, :], ps[:, 4, c * 40:c * 40 + ML_ROWS]))
        dve.sem_inc(sem("ml_cols_taken"), 1)
        for h in range(4):
            dve.wait_ge(*after("ml_scores", h + 1))
            for d in range(2):
                for qt in range(2):
                    r = h + 32 * d
                    ins = dve.tensor_scalar(eb[:, 2 * d + qt, :], half(5, d), mcol[:, 0, qt, r:r + 1], 0.0,
                                            ALU.subtract, ALU.min)
            ins.then_inc(sem("ml_diff"), 1)
            dve.wait_ge(*after("ml_masked", 4 * (h + 1)))
            den = small[:, 1, 0:4]
            for d in range(2):
                for qt in range(2):
                    j = 2 * d + qt
                    link(dve.tensor_tensor_reduce(eb[:, j, :], eb[:, j, :], half(4, qt), float(P) ** -0.5, 0.0, ALU.mult,
                                                  ALU.add, den[:, j:j + 1]))
            link(dve.scalar_tensor_tensor(den, den, -1.0, den, ALU.mult, ALU.max))
            for d in range(2):
                r = h + 32 * d
                link(dve.tensor_tensor(den[:, 2 * d:2 * d + 2].rearrange("p (a b) -> p a b", b=1),
                                       den[:, 2 * d:2 * d + 2].rearrange("p (a b) -> p a b", b=1),
                                       mcol[:, 1, :, r:r + 1], ALU.max))
            link(dve.reciprocal(den, den))
            if h >= 1:
                dve.wait_ge(*after("ml_turned_p", h))
            for qt in range(2):
                link(dve.tensor_scalar(wsum[:, qt, :], eb[:, qt, :], den[:, qt:qt + 1], None, ALU.mult))
                dve.scalar_tensor_tensor(wsum[:, qt, :], eb[:, 2 + qt, :], den[:, 2 + qt:3 + qt], wsum[:, qt, :],
                                         ALU.mult, ALU.add).then_inc(sem("ml_w"), 1)
        dve.wait_ge(*after("ml_o", 1))
        for h in range(4):
            dve.wait_ge(*after("ml_root", h + 1))
            link(dve.reciprocal(eb[:, h, :], eb[:, h, :]))
            link(dve.scalar_tensor_tensor(proj[:, h, :], proj[:, h, :], param("ml_norm", h), eb[:, h, :],
                                          ALU.mult, ALU.mult))
            dve.tensor_tensor(proj[:, h, :], proj[:, h, :], proj[:, 12 + h, :], ALU.mult).then_inc(sem("ml_rms"), 1)
        split("in6m", 4, lambda k: proj[:, k, :], base=8)

        def na_logits(h):
            dve.wait_ge(*after("na_bias", h + 1))
            dve.scalar_tensor_tensor(flat(lg[h % 2]), ps[:, 4 + h % 2, :], 64.0 ** -0.5, flat(bias[h % 2]),
                                     ALU.mult, ALU.add).then_inc(sem("na_logits"), 1)

        def xa_logits(h):
            dve.tensor_scalar(flat(lg[h % 2]), ps[:, 4 + h % 2, :], float(P) ** -0.5, None, ALU.mult
                              ).then_inc(sem("xa_logits"), 1)

        attention("na", 8, na_logits, lambda h: low_of("na", 12, h, 64))
        attention("xa", 4, xa_logits, lambda h: low_of("xa", 16, h, P))
        project("merge")
        dve.wait_ge(taken, all_taken("merge"))
        first = FIRST["branch"]
        for n in range(COUNT["branch"]):
            b, u = divmod(n, GROUP)
            dve.wait_ge(unit_done, first + n + 1)
            out = ps[:, u, :].rearrange("p (a b) -> p a b", a=2)
            gate = proj[:, 8 * b + 2 * u:8 * b + 2 * u + 2, :]
            dst = h_t[:, 2 * u:2 * u + 2, :]
            if b == 0:
                ins = dve.tensor_tensor(dst, gate, out, ALU.mult)
            else:
                ins = dve.tensor_tensor(gate, gate, out, ALU.mult)
            ins.then_inc(taken, 1)
            if b:
                dve.wait_ge(taken, all_taken("branch", n + 1))
                ins = dve.tensor_tensor(dst, dst, gate, ALU.add).then_inc(sem("merged"), 1)
            else:
                dve.sem_inc(sem("merged"), 1)
            low("branch", n + GROUP)
        split("in7", KT, h_tile)
        project("w_out")
        dve.wait_ge(taken, all_taken("w_out"))
        for k in range(KT):
            dve.tensor_tensor(x_t[:, k, :], x_t[:, k, :], proj[:, k, :], ALU.add).then_inc(sem("ffn_res"), 1)
        rms("ffn", x_t, h_t, "ffn_norm", "ffn_h")
        split("in8", KT, h_tile)
        dve.wait_ge(*after("in8_lo", KT))
        for m in range(2):
            dve.memset(cin[m][:, 0:1], 0.0).then_inc(sem("edges"), 1)
            dve.memset(cin[m][:, 1 + S:2 + S], 0.0).then_inc(sem("edges"), 1)
        dve.wait_ge(*after("edges", GROUP + 4))
        dve.sem_inc(sem("ffn_pair_free"), 2)
        first = FIRST["ffn_up"]
        with dve.Fori(0, COUNT["ffn_up"] // GROUP) as i:
            for m in range(2):
                dve.wait_ge(taken, i * GROUP + (GROUP + first + 2 * m + 1))
                conved = fbuf[m][:, 0, :]

                def tap(t):
                    return params[:, bass.ds(i * 2 + (PCOL["ffn_conv"] + FT * t + m), 1)]

                dve.tensor_scalar(conved, cin[m][:, 0:S], tap(0), None, ALU.mult).then_inc(sem("ffn_conv"), 1)
                for t in (1, 2):
                    dve.wait_ge(*after("ffn_conv", i * 6 + (3 * m + t)))
                    dve.scalar_tensor_tensor(conved, cin[m][:, t:t + S], tap(t), conved, ALU.mult, ALU.add
                                             ).then_inc(sem("ffn_conv"), 1)
                for u in (2 * m, 2 * m + 1):
                    low_in_loop("ffn_up", i, u)
                dve.wait_ge(*after("ffn_gelu", i * 2 + (m + 1)))
                dve.wait_ge(taken, i * GROUP + (GROUP + first + 2 * m + 2))
                dve.tensor_tensor(proj[:, bass.ds(i * 2 + m, 1), :], fbuf[m][:, 0:1, :], fbuf[m][:, 1:2, :], ALU.mult
                                  ).then_inc(sem("ffn_pair_free"), 1)
        split("in9", FT, lambda k: proj[:, k, :])
        first = FIRST["ffn_down"]
        for n in range(COUNT["ffn_down"] - GROUP):
            low("ffn_down", n + GROUP)
        for k in range(KT):
            dve.wait_ge(taken, GROUP + first + k + 1)
            dve.tensor_tensor(x_t[:, k, :], x_t[:, k, :], proj[:, 22 + k, :], ALU.add).then_inc(sem("final_res"), 1)
        rms("final", x_t, proj, "final_norm", "final_done")

    @block.gpsimd
    def _(pool):
        pool.wait_ge(*after("in0_lo", KT))
        pool.memset(acc[:], 0.0).then_inc(sem("acc_zero"), 1)
        pool.wait_ge(*after("consts_in", 16))
        pool.wait_ge(*after("gdn_unit", 16))
        for sg in range(2):
            for p in range(2):
                g = 2 * sg + p
                for m in range(2):
                    pool.wait_ge(*after("gdn_qe", 2 * g + m + 1))
                    ins = pool.tensor_tensor(qg[:, 2 * p + m, :], qg[:, 2 * p + m, :], proj[:, 2 * g + m, P:S], ALU.mult)
                ins.then_inc(sem("gdn_qg"), 1)
            for lv in range(LEVELS):
                for p in range(2):
                    g, n = 2 * sg + p, (sg * LEVELS + lv) * 2 + p
                    if lv == 0:
                        pool.wait_ge(*after("gdn_lt", g + 1))
                        if sg:
                            pool.wait_ge(*after("gdn_ot", 2 * sg))
                    elif lv == 1:
                        pool.wait_ge(*after("gdn_t", n - 1))
                    else:
                        pool.wait_ge(*after("gdn_p", n - 1))
                    a = CCOL["level"] + lv * P
                    mask = consts[:, a:a + P].rearrange("p (a b) -> p a b", a=1).to_broadcast([P, 4, P])
                    pool.tensor_tensor(ctm[p], lt[p], mask, ALU.mult).then_inc(sem("gdn_ct"), 1)
                    if lv == 0:
                        pool.wait_ge(*after("gdn_a0", g + 1))
                        incl = consts[:, CCOL["bw"] + P:CCOL["bw"] + 2 * P].rearrange(
                            "p (a b) -> p a b", a=1).to_broadcast([P, 4, P])
                        pool.tensor_tensor(aqk[p], aqk[p], incl, ALU.mult).then_inc(sem("gdn_aqk"), 1)
        pool.wait_ge(*after("in3_lo", KT))
        pool.dma_start(proj[:, 8:16, :], io["mem_t"]).then_inc(sem("mem_in"), 16)
        for h in range(4):
            pool.wait_ge(*after("ml_exp", h + 1))
            for d, name in enumerate(("fw", "bw")):
                for qt in range(2):
                    pool.tensor_tensor(eb[:, 2 * d + qt, :], eb[:, 2 * d + qt, :], strip(name, qt), ALU.mult
                                       ).then_inc(sem("ml_masked"), 1)
        pool.wait_ge(*after("ml_hsum", 4))
        for h in range(8):
            if h >= 2:
                pool.wait_ge(*after("na_logits", h - 1))
            pool.dma_start(bias[h % 2], io["na_bias"][h]).then_inc(sem("na_bias_in"), 16)
            pool.wait_ge(*after("na_bias_in", 16 * (h + 1)))
            mask = consts[:, CCOL["colmask"]:CCOL["colmask"] + S].rearrange("p (a b) -> p a b", a=1).to_broadcast([P, 2, S])
            pool.tensor_tensor(bias[h % 2], bias[h % 2], mask, ALU.add).then_inc(sem("na_bias"), 1)


def _constants():
    i, j = np.meshgrid(np.arange(P), np.arange(P), indexing="ij")
    one, zero = np.ones((P, P)), np.zeros((P, P))
    out = {
        "ident": np.eye(P),
        "fw": np.hstack([one, j <= i, zero]),
        "bw": np.hstack([zero, j >= i, one]),
        "neg": np.hstack([zero, np.where(j <= i, 0.0, NEG), NEG * one]),
        "level": np.hstack([(i // (2 * s) == j // (2 * s)) & ((i // s) % 2 == 0) & ((j // s) % 2 == 1)
                            for s in (2 ** n for n in range(LEVELS))]),
    }
    c, w = np.arange(64), 16
    start = np.clip(c - w // 2, 0, 64 - w)
    ok = (c[None, :] >= start[:, None]) & (c[None, :] < start[:, None] + w)
    out["colmask"] = np.tile(np.where(ok, 0.0, NEG), (2, 4))
    return np.ascontiguousarray(np.hstack([out[n] for n, _ in CONSTS]).astype(np.float32))


def _pairs(blocks):
    u = blocks.shape[0]
    return np.ascontiguousarray(blocks.reshape(u // PAIR, PAIR * UNIT, P, P).transpose(0, 2, 1, 3)
                                .reshape(u // PAIR, P, PAIR * UNIT * P))


def _by_output(w):
    n = w.shape[1] // P
    return w.reshape(KT, P, n, P).transpose(2, 0, 1, 3)


def _tiles(a):
    return np.ascontiguousarray(a.T.reshape(-1, P, S).transpose(1, 0, 2))


def _columns(v):
    return np.asarray(v).reshape(-1, P).T


def _rows(v, at):
    out = np.zeros((P, 1), np.float32)
    for part, a in zip(v, at):
        out[a:a + len(part), 0] = part
    return out


def kernel(**inputs):
    import concourse.bacc as bacc
    from concourse.bass_utils import run_bass_kernel_spmd

    t = {k: np.asarray(v) for k, v in inputs.items()}
    a = {}
    w_in = t["w_in_2"][0]
    gdn = t["gdn_w_in"][0]
    a["ada"] = np.ascontiguousarray(t["ada_w"].reshape(2, KT, P, 3, D).transpose(0, 3, 1, 2, 4)
                                    .reshape(ADA // PAIR, PAIR, P, D).transpose(0, 2, 1, 3)
                                    .reshape(ADA // PAIR, P, PAIR * D))
    a["moba_in"] = _pairs(_by_output(t["moba_w_in"][0]))
    a["moba_out"] = _pairs(_by_output(t["moba_w_out"][0]))
    a["gdn_in"] = _pairs(_by_output(gdn[:, :4096]))
    a["gdn_out"] = _pairs(_by_output(t["gdn_w_out"][0]))
    a["mem_kv"] = _pairs(_by_output(t["w_mem_kv_2"][0]))
    a["w_in"] = _pairs(_by_output(np.concatenate([w_in[:, :2048], w_in[:, 2064:4112]], 1)))
    a["merge"] = _pairs(_by_output(w_in[:, 4112:]))
    a["branch"] = _pairs(np.concatenate([
        t[n][0].reshape(4, P, 8, P).transpose(2, 0, 1, 3).reshape(4, 8, P, P)
        for n in ("w_br_ml_2", "w_br_na_2", "w_br_xa_2")]))
    a["w_out"] = _pairs(_by_output(t["w_out_2"][0]))
    up = _by_output(t["w_ffn_up_2"][0])
    a["ffn_up"] = _pairs(np.stack([up[:FT], up[FT:]], 1).reshape(2 * FT, KT, P, P))
    down = t["w_ffn_down_2"][0].reshape(FT, P, KT, P).transpose(2, 0, 1, 3)
    a["ffn_down"] = _pairs(np.concatenate([down, np.zeros((KT, 2, P, P), np.float32)], 1).reshape(24, UNIT, P, P))
    a["x_t"] = _tiles(t["x"][0])
    a["mem_t"] = _tiles(t["mem_2"][0])
    a["gdn_wg"] = np.ascontiguousarray(gdn[:, 4096:].reshape(KT, P, 16).transpose(1, 0, 2))
    gates = w_in[:, 2048:2064]
    wide = np.zeros((D, 2 * ML_ROWS), np.float32)
    wide[:, 0:4], wide[:, 32:36] = gates[:, 0:4], gates[:, 8:12]
    wide[:, ML_ROWS:ML_ROWS + 4], wide[:, ML_ROWS + 32:ML_ROWS + 36] = gates[:, 4:8], gates[:, 12:16]
    a["ml_wg"] = np.ascontiguousarray(wide.reshape(KT, P, 2 * ML_ROWS).transpose(1, 0, 2))
    rpb = t["na_rpb_2"][0]
    q = np.arange(S)
    r, c = q // 64, q % 64
    dr = r[None, :] - r[:, None] + 7
    dc = np.clip(c[None, :] - c[:, None] + 15, 0, 30)
    a["na_bias"] = np.ascontiguousarray(rpb[:, dr, dc].reshape(8, 2, P, S).transpose(0, 2, 1, 3))
    named = {
        "c": t["c"], "ada_b": t["ada_b"], "ln_g": t["ln_g"], "ln_b": t["ln_b"], "gdn_conv": t["gdn_conv_w"][0],
        "gdn_norm": t["gdn_norm_w"], "ml_conv": t["w_ml_conv_2"][0], "ml_conv_b": t["b_ml_conv_2"],
        "ml_norm": t["ml_norm_g_2"], "mix_norm": t["mix_norm_g_2"], "mem_norm": t["mem_norm_g_2"],
        "merge_b": t["b_merge_gate_2"], "ffn_norm": t["ffn_norm_g_2"], "ffn_conv": t["w_ffn_conv_2"][0],
        "ffn_conv_b": t["b_ffn_conv_2"], "final_norm": t["final_norm_g_2"],
    }
    rows_ = {"a_log": _rows([t["gdn_a_log"][0]], [0]), "dt_bias": _rows([t["gdn_dt_bias"][0]], [0]),
             "b_ig": _rows(t["b_ml_igate_2"][0], [0, 32]), "b_fg": _rows(t["b_ml_fgate_2"][0], [0, 32])}
    a["params"] = np.ascontiguousarray(np.hstack([_columns(named[n]) if n in named else rows_[n] for n, _ in PARAMS]))
    a["consts"] = _constants()

    nc = bacc.Bacc("TRN2", target_bir_lowering=False, num_devices=1)
    io = {n: nc.dram_tensor(f"in_{n}", v.shape, F32, kind="ExternalInput").ap() for n, v in a.items()}
    io["out"] = nc.dram_tensor("out_t", (P, KT, S), F32, kind="ExternalOutput").ap()
    build(nc, io)
    r = run_bass_kernel_spmd(nc, [{f"in_{n}": v for n, v in a.items()}], core_ids=[0])
    out = r.results[0]["out_t"]
    return np.ascontiguousarray(out.transpose(1, 0, 2).reshape(D, S).T)[None]
```

```python
from contextlib import ExitStack

import numpy as np
import concourse.bass as bass
from concourse import mybir

F32 = mybir.dt.float32
F32R = mybir.dt.float32r
ALU = mybir.AluOpType
ACT = mybir.ActivationFunctionType
X = mybir.AxisListType.X

P = 128
D = 1024
KT = D // P
S = 256
NEG = -1e30
DEPTH = 2
ALPHA = (2.0 * DEPTH) ** 0.25
LN_EPS = 1e-5
EPS = 1e-6
FF = 2816
FT = FF // P
UNIT = 8
GROUP = 4
PAIR = 2
RAW = 4
ADA = 48
LEVELS = 7

STAGES = [("moba_in", 32), ("moba_out", 8), ("gdn_in", 32), ("gdn_out", 8),
          ("mem_kv", 8), ("w_in", 32), ("merge", 24), ("branch", 12), ("w_out", 8), ("ffn_up", 44),
          ("ffn_down", 24)]
FIRST = {}
_n = 0
for _name, _count in STAGES:
    FIRST[_name] = _n
    _n += _count
UNITS = _n
LOADED = {n: 16 + f + (32 if f else 0) for n, f in FIRST.items()}
STRIDE = {n: 8 if n == "moba_in" else 4 for n in FIRST}
COUNT = dict(STAGES)


def place(name, n):
    return LOADED[name] + STRIDE[name] * (n // GROUP) + n % GROUP



PARAMS = [("c", 8), ("ada_b", 48), ("ln_g", 16), ("ln_b", 16), ("gdn_conv", 96), ("gdn_norm", 1),
          ("ml_conv", 24), ("ml_conv_b", 8), ("ml_norm", 4), ("mix_norm", 8), ("mem_norm", 8),
          ("merge_b", 24), ("ffn_norm", 8), ("ffn_conv", 66), ("ffn_conv_b", 22), ("final_norm", 8),
          ("a_log", 1), ("dt_bias", 1), ("b_ig", 1), ("b_fg", 1)]
PCOL = {}
_n = 0
for _name, _count in PARAMS:
    PCOL[_name] = _n
    _n += _count
NPARAM = _n

CONSTS = [("ident", P), ("fw", 3 * P), ("bw", 3 * P), ("neg", 3 * P), ("level", LEVELS * P), ("colmask", S),
          ("pick", 31)]
CCOL = {}
_n = 0
for _name, _count in CONSTS:
    CCOL[_name] = _n
    _n += _count
NCONST = _n
ML_ROWS = 36


def build(nc, io):
    ctx = ExitStack()
    with ctx:
        _program(nc, io, ctx)


def _program(nc, io, ctx):
    def sb(name, shape, dt=F32):
        return ctx.enter_context(nc.sbuf_tensor(name, shape, dt))

    turns = {
        ("_total",): [(n, KT - 1) for n in ("ln0", "ln1", "ffn", "final")],
        ("_sum",): [("ln0", 1), ("ln1", 1)],
        ("_root", "_sumsq"): [("ln0", 1), ("mem", 1), ("ln1", 1), ("mix", 1), ("ffn", 1), ("final", 1)],
        ("_sq",): [(n, KT) for n in ("ln0", "mem", "ln1", "mix", "ffn", "final")],
        ("_centred", "_scaled", "_x"): [("ln0", KT), ("ln1", KT)],
        ("_scores", "_logits", "_max", "_probs", "_turned_p", "_pt", "_pv", "_out"):
            [("moba", 8), ("na", 8), ("xa", 4)],
        ("_exp",): [("moba", 16), ("na", 16), ("xa", 8)],
        ("_high",): [("na", 8), ("xa", 4)],
        ("_turned", "_natural"): [("moba_v", 8), ("mem_v", 2), ("ml_v", 2), ("na_v", 2)],
        ("_hi", "_lo"): [(f"in{n}", KT) for n in range(6)] + [("in6m", 4), ("in7", KT), ("in8", KT), ("in9", FT)],
    }
    shared, start = {}, {}
    for kinds, order in turns.items():
        for kind in kinds:
            at = 0
            for tag, n in order:
                shared[tag + kind], start[tag + kind] = "turn" + kind, at
                at += n

    sems = {}

    def sem(name):
        name = shared.get(name, name)
        if name not in sems:
            sems[name] = ctx.enter_context(nc.semaphore(name))
        return sems[name]

    def after(name, n):
        return sem(name), n + start.get(name, 0)

    raw = sb("raw", [P, RAW, PAIR * UNIT * P])
    w_hi = sb("w_hi", [P, GROUP, UNIT * P], F32R)
    w_lo = sb("w_lo", [P, GROUP, UNIT * P], F32R)
    in_hi = sb("in_hi", [P, FT, S], F32R)
    in_lo = sb("in_lo", [P, FT, S], F32R)
    x_t = sb("x_t", [P, KT, S])
    proj = sb("proj", [P, 32, S])
    params = sb("params", [P, NPARAM])
    consts = sb("consts", [P, NCONST])
    gdn_wg = sb("gdn_wg", [P, KT, 40])
    ml_wg = sb("ml_wg", [P, KT, 64 + ML_ROWS])
    cs = sb("cs", [P, KT])
    mod = sb("mod", [P, 2, 24])
    stat = sb("stat", [P, 2, S])
    ln_bias = sb("ln_bias", [P, 2, KT])
    rows = sb("rows", [ML_ROWS, 6, S])
    gcol = sb("gcol", [P, 2, 2, 8])
    gexp = sb("gexp", [P, 3, 8])
    mcol = sb("mcol", [P, 2, 2, ML_ROWS])
    small = sb("small", [P, 2, 16])
    work = sb("work", [P, 5 * 1024])
    memkv = sb("memkv", [P, 8, S])
    mem_vnat = sb("mem_vnat", [P, 2, 4 * P])

    ps = ctx.enter_context(nc.psum_tensor("ps", [P, 8, 512], F32))

    def area(at, *shape, of=work):
        v = of[:, at:at + int(np.prod(shape))]
        return v.rearrange("p (a b) -> p a b", a=shape[0]) if len(shape) == 2 else v

    acc = area(0, 4, D)
    sq = area(0, KT, S)
    h_t = area(2048, KT, S)
    vnat = area(0, 2, D)
    lg = {n: [area(2048, 2, S), area(2560, 2, S)] for n in ("na", "xa")}
    pt = {n: area(3072, 2, S) for n in ("ml", "na", "xa")}
    bias = [area(4096, 2, S), area(4608, 2, S)]
    cin = [area((S + 3) * u, S + 3) for u in range(GROUP)]
    fbuf = [area(2048 + 512 * u, 2, S) for u in range(2)]
    eb = [area(2048, 4, S), area(1024, 4, S)]
    ml_vnat = area(0, 2, 4 * P)
    wsum = area(3584, 2, S)
    gsq = area(4096, 4, S)
    lsq = area(2048, 12, S)
    osq = [area(1024, 4, S), area(2048, 4, S)]
    ctm, pm, lt, aqk = ([area(1024 * n + 512 * p, 4, P) for p in range(2)] for n in range(4))
    dec, kb = area(4096, 4, P), area(4608, 2, S)
    kv_flat = memkv[:].rearrange("p a b -> p (a b)")
    vnat_flat = mem_vnat[:].rearrange("p a b -> p (a b)")
    moba_vnat = area(0, 2, D, of=kv_flat)
    lg["moba"] = [area(512 * n, 2, S, of=vnat_flat) for n in range(2)]
    pt["moba"] = area(4096, 2, S)
    gated = [area(4608, S), area(4864, S)]
    kdg, vb = ([area(1024 * n + 512 * p, 4, P, of=kv_flat) for p in range(2)] for n in range(2))
    qg = area(0, 4, P, of=vnat_flat)
    u0, wn, s1, v1 = area(4096, 4, P), area(4608, 4, P), ctm[0], ctm[1]

    def tri(base, gg):
        return proj[:, base + 2 * gg:base + 2 * gg + 2, :].rearrange("p a (c b) -> p (a c) b", c=2)


    ident = consts[:, CCOL["ident"]:CCOL["ident"] + P]
    ones = consts[:, CCOL["fw"]:CCOL["fw"] + P]

    def pick(t, n):
        a = CCOL["pick"] + 15 - t
        return consts[:, a:a + n]

    def param(name, k=0, n=1, rows_=P):
        return params[0:rows_, PCOL[name] + k:PCOL[name] + k + n]

    def strip(name, qt):
        a = CCOL[name] + P * (1 - qt)
        return consts[:, a:a + S]

    def half(bank, k):
        return ps[:, bank, k * S:(k + 1) * S]

    def flat(t):
        return t.rearrange("p a b -> p (a b)")

    loaded, hi_done, lo_done, unit_done, taken = (sem(n) for n in
        ("pair_loaded", "unit_hi", "unit_lo", "unit_multiplied", "bank_taken"))

    def all_taken(name, n=None):
        return GROUP + FIRST[name] + (COUNT[name] if n is None else n)

    block = ctx.enter_context(nc.Block())

    @block.sync
    def _(sp):
        sp.dma_start(params[:], io["params"]).then_inc(sem("params_in"), 16)
        early = CCOL["neg"]
        sp.dma_start(consts[:, 0:early], io["consts"][:, 0:early]).then_inc(sem("consts_in"), 16)
        sp.dma_start(x_t[:], io["x_t"]).then_inc(sem("x_in"), 16)

        def load(g, src, i=None):
            at = 0 if i is None else i
            if i is not None or g >= RAW:
                sp.wait_ge(lo_done, at * RAW * PAIR + PAIR * (g - RAW + 1))
            sp.dma_start(raw[:, g % RAW, :], src).then_inc(sem(f"slot_in{g % RAW}"), 16)
            if i is not None or g >= 2:
                sp.wait_ge(sem(f"slot_in{(g - 2) % RAW}"), at * 16 + 16 * ((g - 2) // RAW + 1))
                sp.sem_inc(loaded, 1)

        def load_stage(name, first, count):
            g = LOADED[name] // PAIR + first
            if count % RAW == 0 and g % RAW == 0 and count > RAW:
                with sp.Fori(0, count // RAW) as i:
                    for c in range(RAW):
                        load(g + c, io[name][bass.ds(i * RAW + (first + c), 1)].rearrange("a p n -> (a p) n"), i)
            else:
                for c in range(count):
                    load(g + c, io[name][first + c])

        for g in range(8):
            load(g, io["ada"][g])
        for start in (0, 4):
            with sp.Fori(start, start + 4) as i:
                for c in range(RAW):
                    src, first = (io["moba_in"], c) if c < 2 else (io["ada"], 6 + c)
                    load(8 + c, src[bass.ds(i * 2 + first, 1)].rearrange("a p n -> (a p) n"), i)
            if start == 0:
                sp.dma_start(consts[:, early:], io["consts"][:, early:]).then_inc(sem("masks_in"), 16)
                sp.dma_start(gdn_wg[:], io["gdn_wg"]).then_inc(sem("gate_w_in"), 16)
                sp.dma_start(ml_wg[:], io["ml_wg"]).then_inc(sem("gate_w_in"), 16)
        for name, units in STAGES[1:]:
            pairs = units // PAIR
            head = -(LOADED[name] // PAIR) % RAW if pairs > 2 * RAW else 0
            load_stage(name, 0, head)
            load_stage(name, head, (pairs - head) // RAW * RAW)
            done = head + (pairs - head) // RAW * RAW
            load_stage(name, done, pairs - done)
        for g in (138, 139):
            sp.wait_ge(sem(f"slot_in{g % RAW}"), 16 * (g // RAW + 1))
            sp.sem_inc(loaded, 1)
        sp.wait_ge(*after("final_done", KT))
        sp.dma_start(io["out"], proj[:, 0:KT, :]).then_inc(sem("out_stored"), 16)
        sp.wait_ge(*after("out_stored", 16))

    @block.tensor
    def _(pe):
        def unit(u, tag=None, base=0):
            for n, (w, a) in enumerate(((w_hi, in_hi), (w_hi, in_lo), (w_lo, in_hi))):
                for k in range(UNIT):
                    if tag and n < 2:
                        pe.wait_ge(*after(f"{tag}_{('hi', 'lo')[n]}", k + 1))
                    mm = pe.matmul(half(u, 0), w[:, u, k * P:(k + 1) * P], a[:, base + k, :],
                                   start=(n == 0 and k == 0), stop=(n == 2 and k == UNIT - 1))
            mm.then_inc(unit_done, 1)

        def project(name, tag, first_group=0, groups=None, base=0):
            first = FIRST[name]
            groups = COUNT[name] // GROUP if groups is None else groups
            with pe.Fori(first_group, first_group + groups) as i:
                for u in range(GROUP):
                    pe.wait_ge(lo_done, i * STRIDE[name] + (LOADED[name] + u + 1))
                    pe.wait_ge(taken, i * GROUP + (first + u + 1))
                    unit(u, tag if u == 0 else None, base)

        def project_short(name, tag, base=0, between={}):
            for n in range(COUNT[name]):
                pe.wait_ge(lo_done, LOADED[name] + n + 1)
                pe.wait_ge(taken, FIRST[name] + n + 1)
                unit(n % GROUP, tag if n == 0 else None, base)
                if n in between:
                    between[n]()

        def split_mm(out, u, blocks, start, stop):
            last = len(blocks) - 1
            for n, (w, a) in enumerate(((w_hi, in_hi), (w_hi, in_lo), (w_lo, in_hi))):
                for m, (b, k) in enumerate(blocks):
                    mm = pe.matmul(out, w[:, u, b * P:(b + 1) * P], a[:, k, :],
                                   start=start and n == 0 and m == 0, stop=stop and n == 2 and m == last)
            return mm

        def keep_warm(n, bank):
            for _ in range(n):
                pe.matmul(half(bank, 0), ident, consts[:, 0:S], start=True, stop=True)

        def sum_tiles(out, src, ready, name, tiles=KT):
            for k in range(tiles):
                pe.wait_ge(*after(ready, k + 1))
                mm = pe.matmul(out, ones, src[:, k, :], start=(k == 0), stop=(k == tiles - 1))
            mm.then_inc(sem(name), 1)

        def transposes(src, tiles, banks, name, per_bank=2):
            for t in range(tiles):
                bank = banks[(t // 2) % len(banks)]
                if t % 2 == 0 and t // 2 >= len(banks):
                    pe.wait_ge(*after(f"{name}_natural", t // 2 - len(banks) + 1))
                for c in range(2):
                    mm = pe.transpose(ps[:, bank, (t % 2) * S + c * P:(t % 2) * S + (c + 1) * P],
                                      src[:, t, c * P:(c + 1) * P], ident)
                if t % 2 == 1:
                    mm.then_inc(sem(f"{name}_turned"), 1)

        def stream(name, n):
            pe.wait_ge(lo_done, place(name, n) + 1)
            pe.wait_ge(taken, FIRST[name] + n + 1)
            unit(n % GROUP)

        def attention(name, heads, q, k, v, beside=None):
            def scores(h):
                if h >= 2:
                    pe.wait_ge(*after(f"{name}_logits", h - 1))
                    if name == "moba":
                        pe.wait_ge(*after("moba_v_natural", h))
                for qt in range(2):
                    qh = q(h)
                    mm = pe.matmul(half(4 + h % 2, qt), qh[:, qt * P:(qt + 1) * P], k(h), start=True, stop=True)
                mm.then_inc(sem(f"{name}_scores"), 1)

            scores(0)
            for h in range(heads):
                if h + 1 < heads:
                    scores(h + 1)
                if beside:
                    beside(2 * h)
                pe.wait_ge(*after(f"{name}_probs", h + 1))
                if h >= 1:
                    pe.wait_ge(*after(f"{name}_pt", h))
                for qt in range(2):
                    for kt in range(2):
                        mm = pe.transpose(ps[:, 6, kt * S + qt * P:kt * S + (qt + 1) * P],
                                          lg[name][h % 2][:, qt, kt * P:(kt + 1) * P], ident)
                mm.then_inc(sem(f"{name}_turned_p"), 1)
                if beside:
                    beside(2 * h + 1)
                if name == "moba":
                    pe.wait_ge(*after("moba_v_natural", h + 1))
                pe.wait_ge(*after(f"{name}_pt", h + 1))
                if h >= 1:
                    pe.wait_ge(*after(f"{name}_out", h))
                for kt in range(2):
                    vh = v(h, kt)
                    m = vh.shape[-1]
                    p0 = 64 * (h % 2) if m == 64 else 0
                    mm = pe.matmul(ps[p0:p0 + m, 7, 0:S], vh, pt[name][:, kt, :], start=(kt == 0), stop=(kt == 1))
                mm.then_inc(sem(f"{name}_pv"), 1)

        def add_partitions(chunks, name):
            for c in chunks:
                for n in range(KT):
                    mm = pe.matmul(ps[:, 7, c * KT + n:c * KT + n + 1], acc[:, c, n * P:(n + 1) * P], ones[:, 0:1],
                                   start=True, stop=True)
            mm.then_inc(sem(name), 1)

        pe.wait_ge(*after("consts_in", 16))
        pe.wait_ge(lo_done, 14)
        keep_warm(10, 6)
        pe.wait_ge(lo_done, 16)
        add_partitions(range(2), "mod_first")
        keep_warm(6, 6)
        project("moba_in", "in0", groups=6)

        stream("moba_in", 24)
        pe.wait_ge(lo_done, place("moba_in", 12))
        add_partitions(range(0, 1), "mod_gate")
        pe.wait_ge(*after("mod_read", 1))

        def turn_v(t, bank):
            pe.wait_ge(taken, all_taken("moba_in", 25 + t))
            for c in range(2):
                mm = pe.transpose(ps[:, bank, c * P:(c + 1) * P], proj[:, 24 + t, c * P:(c + 1) * P], ident)
            mm.then_inc(sem("moba_v_turned"), 1)

        turn_v(0, 6)
        stream("moba_in", 25)
        pe.wait_ge(*after("moba_v_natural", 1))

        def beside_moba(n):
            h = n // 2
            if n % 2 == 0 and h < 6:
                stream("moba_in", 26 + h)
            if n % 2 and h < 7:
                turn_v(h + 1, 4 + h % 2)

        attention("moba", 8, lambda h: proj[:, h, :], lambda h: proj[:, 8 + h, :],
                  lambda h, kt: moba_vnat[:, kt, h * P:(h + 1) * P], beside=beside_moba)
        pe.wait_ge(lo_done, LOADED["moba_out"])
        pe.wait_ge(*after("moba_out", 8))
        project_short("moba_out", "in1", base=8, between={
            2: lambda: add_partitions(range(1, 2), "mod_rest"), 3: lambda: add_partitions(range(2, 3), "mod_rest")})

        def sum_total(bank, tag, name):
            pe.wait_ge(*after(f"{tag}_total", KT - 1))
            pe.matmul(half(bank, 0), ones, stat[:, 0, :], start=True, stop=True).then_inc(sem(name), 1)

        def sum_squares(tag):
            sum_tiles(half(5, 0), sq, f"{tag}_sq", f"{tag}_sumsq")

        sum_total(4, "ln0", "ln0_sum")
        add_partitions(range(3, 4), "mod_last")
        sum_squares("ln0")
        keep_warm(8, 6)

        project("gdn_in", "in2", groups=1)
        pe.wait_ge(*after("gate_w_in", 32))
        for k in range(KT):
            mm = pe.matmul(ps[0:40, 6, 0:S], gdn_wg[:, k, :], h_t[:, k, :], start=(k == 0), stop=(k == KT - 1))
        mm.then_inc(sem("gdn_gates"), 1)
        project("gdn_in", None, first_group=1, groups=5)
        pe.wait_ge(*after("gdn_rows", 2))
        for n, r in enumerate((2, 3)):
            for c in range(2):
                mm = pe.transpose(ps[:, 6, (2 * n + c) * 8:(2 * n + c) * 8 + 8], rows[0:8, r, c * P:(c + 1) * P],
                                  ident[0:8, 0:8])
        mm.then_inc(sem("gdn_cols"), 1)

        def spread(src, tiles, rows_in, banks, name):
            for t in tiles:
                if t % 2 == 0 and t // 2 >= len(banks):
                    pe.wait_ge(*after(name, t // 2 - len(banks) + 1))
                sel = ident[0:rows_in, t:t + 1].to_broadcast([rows_in, P])
                mm = pe.matmul(half(banks[t // 2 % len(banks)], t % 2), sel, src, start=True, stop=True)
                if t % 2:
                    mm.then_inc(sem(f"{name}_bc"), 1)

        def length_sums(b):
            pe.wait_ge(*after("gdn_sq", b + 1))
            for t in range(4 * b, 4 * b + 4):
                mm = pe.matmul(ps[0:16, 7, 0:S], pick(t, 16), lsq[:, t % 12, :], start=(t == 0), stop=(t == 15))
            mm.then_inc(sem("gdn_sum"), 1)

        for n in range(8):
            u = n % GROUP
            pe.wait_ge(lo_done, LOADED["gdn_in"] + 24 + n + 1)
            pe.wait_ge(taken, FIRST["gdn_in"] + 24 + n + 1)
            unit(u)
            if 2 <= n <= 5:
                length_sums(n - 2)
        keep_warm(10, 4)
        pe.wait_ge(*after("gdn_len", 2))
        pe.wait_ge(taken, all_taken("gdn_in"))
        spread(rows[0:16, 5, :], range(16), 16, (4, 5, 7, 3), "gdn_unit")
        pe.wait_ge(*after("gdn_unit", 8))
        pe.wait_ge(*after("gdn_silu", 6))
        pe.wait_ge(taken, all_taken("gdn_in"))
        for sg in range(2):
            for p in range(2):
                g = 2 * sg + p
                if g >= 1:
                    pe.wait_ge(*after("gdn_a0", g))
                    pe.wait_ge(*after("gdn_kdg", 4 * g))
                if sg and not p:
                    pe.wait_ge(*after("gdn_o", 2 * sg))
                for m in range(2):
                    h = 2 * g + m
                    sel = ident[0:8, h:h + 1].to_broadcast([8, P])
                    pe.matmul(half(m, 0), sel, rows[0:8, 2, :], start=True, stop=True)
                    mm = pe.matmul(half(m, 1), sel, rows[0:8, 3, :], start=True, stop=True)
                mm.then_inc(sem("gdn_bc"), 1)
                for m in range(2):
                    h = 2 * g + m
                    for c in range(2):
                        j = 2 * m + c
                        pe.transpose(ps[:, 2, j * P:(j + 1) * P], proj[:, 8 + h, c * P:(c + 1) * P], ident)
                        mm = pe.transpose(ps[:, 3, j * P:(j + 1) * P], proj[:, 16 + h, c * P:(c + 1) * P], ident)
                mm.then_inc(sem("gdn_nat"), 1)
                pe.wait_ge(*after("gdn_kb", 2 * (g + 1)))
                for m in range(2):
                    h = 2 * g + m
                    for c in range(2):
                        kk = proj[:, 8 + h, c * P:(c + 1) * P]
                        j = 2 * m + c
                        pe.matmul(ps[:, 4, j * P:(j + 1) * P], kk, kb[:, m, c * P:(c + 1) * P], start=True, stop=True)
                        mm = pe.matmul(ps[:, 5, j * P:(j + 1) * P], kk, proj[:, h, c * P:(c + 1) * P], start=True, stop=True)
                mm.then_inc(sem("gdn_gram"), 1)
            for lv in range(LEVELS):
                for p in range(2):
                    n = (sg * LEVELS + lv) * 2 + p
                    t, tt = tri(8, 2 * sg + p), tri(16, 2 * sg + p)
                    pe.wait_ge(*after("gdn_ct", n + 1))
                    if lv == 0:
                        for j in range(4):
                            mm = pe.matmul(ps[:, 6 + p, j * P:(j + 1) * P], ctm[p][:, j, :], ident, start=True, stop=True)
                        mm.then_inc(sem("gdn_p"), 1)
                        continue
                    pe.wait_ge(*after("gdn_t", n - 1))
                    for j in range(4):
                        mm = pe.matmul(ps[:, 6 + p, j * P:(j + 1) * P], ctm[p][:, j, :], t[:, j, :], start=True, stop=True)
                    mm.then_inc(sem("gdn_p"), 1)
                for p in range(2):
                    if lv == 0:
                        continue
                    n = (sg * (LEVELS - 1) + lv - 1) * 2 + p
                    t, tt = tri(8, 2 * sg + p), tri(16, 2 * sg + p)
                    pe.wait_ge(*after("gdn_ps", n + 1))
                    if lv < LEVELS - 1:
                        for j in range(4):
                            pe.matmul(ps[:, 2 * p, j * P:(j + 1) * P], tt[:, j, :], pm[p][:, j, :], start=True, stop=True)
                    for j in range(4):
                        mm = pe.matmul(ps[:, 2 * p + 1, j * P:(j + 1) * P], pm[p][:, j, :], tt[:, j, :], start=True, stop=True)
                    mm.then_inc(sem("gdn_d"), 1)
            pe.wait_ge(*after("gdn_t", 2 * (sg + 1) * LEVELS))
            pe.wait_ge(*after("gdn_kdg", 8 * (sg + 1)))
            pe.wait_ge(*after("gdn_vb", 8 * (sg + 1)))
            pe.wait_ge(*after("gdn_aqk", 2 * (sg + 1)))
            pe.wait_ge(*after("gdn_qg", 2 * (sg + 1)))

            def each():
                for q in range(4):
                    p, m = divmod(q, 2)
                    tt = tri(16, 2 * sg + p)
                    yield q, slice(q * P, (q + 1) * P), p, 2 * m, tt[:, 2 * m, :], tt[:, 2 * m + 1, :]

            def out_sums(g):
                pe.wait_ge(*after("gdn_osq", 2 * (g + 1)))
                for h in range(4 * g, 4 * g + 4):
                    mm = pe.matmul(ps[0:8, 0, 0:S], pick(h, 8), osq[g][:, h % 4, :], start=(h == 0), stop=(h == 7))
                mm.then_inc(sem("gdn_osum"), 1)

            for q, c, p, j, t0, t1 in each():
                mm = pe.matmul(ps[:, 6, c], t0, vb[p][:, j, :], start=True, stop=True)
            mm.then_inc(sem("gdn_u0"), 1)
            for q, c, p, j, t0, t1 in each():
                mm = pe.matmul(ps[:, 7, c], kdg[p][:, j + 1, :], t1, start=True, stop=True)
            mm.then_inc(sem("gdn_w"), 1)
            pe.wait_ge(*after("gdn_u0s", sg + 1))
            for q, c, p, j, t0, t1 in each():
                mm = pe.matmul(ps[:, 5, c], kdg[p][:, j, :], u0[:, q, :], start=True, stop=True)
            mm.then_inc(sem("gdn_s1"), 1)
            pe.wait_ge(*after("gdn_s1s", sg + 1))
            pe.wait_ge(*after("gdn_ws", sg + 1))
            for q, c, p, j, t0, t1 in each():
                pe.matmul(ps[:, 4, c], t1, vb[p][:, j + 1, :], start=True, stop=False)
                mm = pe.matmul(ps[:, 4, c], wn[:, q, :], s1[:, q, :], start=False, stop=True)
            mm.then_inc(sem("gdn_v1"), 1)
            pe.wait_ge(*after("gdn_v1s", sg + 1))
            if sg:
                out_sums(0)
            for q, c, p, j, t0, t1 in each():
                out = half(2 + q // 2, q % 2)
                pe.matmul(out[:, 0:P], u0[:, q, :], aqk[p][:, j, :], start=True, stop=True)
                pe.matmul(out[:, P:S], v1[:, q, :], aqk[p][:, j + 1, :], start=True, stop=False)
                mm = pe.matmul(out[:, P:S], s1[:, q, :], qg[:, q, :], start=False, stop=True)
                if q % 2:
                    mm.then_inc(sem("gdn_ot"), 1)
        out_sums(1)
        keep_warm(5, 1)
        pe.wait_ge(*after("gdn_rms", 2))
        spread(rows[0:8, 5, :], range(8), 8, (4, 5, 6, 7), "gdn_gated")
        project_short("gdn_out", "in3", between={2: lambda: sum_squares("mem")})
        keep_warm(3, 6)
        sum_total(4, "ln1", "ln1_sum")
        project_short("mem_kv", "in4", base=8, between={1: lambda: sum_squares("ln1"), 4: lambda: sum_squares("mix")})
        pe.wait_ge(taken, all_taken("mem_kv"))
        transposes(memkv[:, 4:8, :], 4, (4, 5), "mem_v")
        project("w_in", "in5", groups=1)
        for k in range(KT):
            mm = pe.matmul(ps[0:64 + ML_ROWS, 6, 0:S], ml_wg[:, k, :], h_t[:, k, :], start=(k == 0), stop=(k == KT - 1))
        mm.then_inc(sem("ml_gates"), 1)
        project("w_in", None, first_group=1, groups=3)
        pe.wait_ge(taken, all_taken("w_in", 16))

        pe.wait_ge(*after("mem_v_natural", 2))
        pe.wait_ge(*after("ml_gate_rows", 1))
        for n in range(2):
            for c in range(2):
                a = (2 * n + c) * 40
                mm = pe.transpose(ps[:, 4, a:a + ML_ROWS], rows[0:ML_ROWS, 4 + n, c * P:(c + 1) * P],
                                  ident[0:ML_ROWS, 0:ML_ROWS])
        mm.then_inc(sem("ml_cols"), 1)
        transposes(proj[:, 8:12, :], 4, (5, 6), "ml_v")
        stream("w_in", 16)
        pe.wait_ge(*after("ml_v_natural", 2))
        pe.wait_ge(*after("ml_cols_taken", 3))
        stream("w_in", 17)

        def ml_scores(h):
            pe.wait_ge(*after("ml_qk", 2 * h + 2))
            if h >= 1:
                pe.wait_ge(*after("ml_diff", h))
            if h >= 2:
                pe.wait_ge(*after("ml_w", 2 * (h - 1)))
            for qt in range(2):
                pe.matmul(half(4 + h % 2, qt), proj[:, h, qt * P:(qt + 1) * P], proj[:, 4 + h, :], start=True, stop=True)
            for d in range(2):
                r = h + 32 * d
                sel = ident[0:ML_ROWS, r:r + 1].to_broadcast([ML_ROWS, P])
                mm = pe.matmul(half(6, d), sel, rows[0:ML_ROWS, 3, :], start=True, stop=True)
            mm.then_inc(sem("ml_scores"), 1)

        ml_scores(0)
        stream("w_in", 18)
        stream("w_in", 19)
        for h in range(4):
            if h < 3:
                ml_scores(h + 1)
            stream("w_in", 20 + 3 * h)
            stream("w_in", 21 + 3 * h)
            pe.wait_ge(*after("ml_w", 2 * (h + 1)))
            if h >= 1:
                pe.wait_ge(*after("ml_h", h))
                pe.wait_ge(*after("ml_hsq", h))
            for qt in range(2):
                for kt in range(2):
                    mm = pe.transpose(ps[:, 7, kt * S + qt * P:kt * S + (qt + 1) * P],
                                      wsum[:, qt, kt * P:(kt + 1) * P], ident)
            mm.then_inc(sem("ml_turned_p"), 1)
            if h < 3:
                stream("w_in", 22 + 3 * h)
            pe.wait_ge(*after("ml_pt", h + 1))
            for kt in range(2):
                mm = pe.matmul(half(7, 0), ml_vnat[:, kt, h * P:(h + 1) * P], pt["ml"][:, kt, :],
                               start=(kt == 0), stop=(kt == 1))
            mm.then_inc(sem("ml_pv"), 1)
        pe.wait_ge(taken, all_taken("w_in", 28))
        transposes(proj[:, 24:28, :], 4, (4, 5), "na_v")
        pe.wait_ge(*after("ml_hsq", 4))
        for h in range(4):
            mm = pe.matmul(ps[0:4, 6, 0:S], pick(h, 4), gsq[:, h, :], start=(h == 0), stop=(h == 3))
        mm.then_inc(sem("ml_hsum"), 1)
        stream("w_in", 31)
        pe.wait_ge(*after("ml_root", 2))
        pe.wait_ge(*after("na_v_natural", 2))
        spread(rows[0:4, 0, :], range(4), 4, (6, 7), "ml_rms")

        pe.wait_ge(*after("ml_rms", 2))
        attention("na", 8, lambda h: proj[64 * (h % 2):64 * (h % 2) + 64, 16 + h // 2, :],
                  lambda h: proj[64 * (h % 2):64 * (h % 2) + 64, 20 + h // 2, :],
                  lambda h, kt: vnat[:, kt, h * 64:(h + 1) * 64], beside=lambda n: stream("merge", n))
        pe.wait_ge(*after("na_out", 8))
        pe.wait_ge(taken, all_taken("w_in"))
        attention("xa", 4, lambda h: proj[:, 28 + h, :], lambda h: memkv[:, h, :],
                  lambda h, kt: mem_vnat[:, kt, h * P:(h + 1) * P], beside=lambda n: stream("merge", 16 + n))

        pe.wait_ge(*after("in6m_lo", 4))
        pe.wait_ge(*after("na_out", 8))
        pe.wait_ge(*after("xa_out", 4))
        first = FIRST["branch"]
        for i in range(3):
            for u in range(GROUP):
                n = first + GROUP * i + u
                pe.wait_ge(lo_done, LOADED["branch"] + GROUP * i + u + 1)
                pe.wait_ge(taken, n + 1)
                for t in range(2):
                    mm = split_mm(half(u, t), u, [(4 * t + k, 8 + 4 * i + k) for k in range(4)], True, True)
                mm.then_inc(unit_done, 1)
        project("w_out", "in7")
        keep_warm(4, 6)
        sum_total(5, "ffn", "ffn_sumsq")
        keep_warm(7, 6)
        project("ffn_up", "in8")
        first = FIRST["ffn_down"]
        with pe.Fori(0, 2) as i:
            for u in range(12):
                pe.wait_ge(lo_done, i * 12 + (LOADED["ffn_down"] + u + 1))
                if u % 3 == 0:
                    pe.wait_ge(taken, i * 4 + (first + u // 3 + 1))
                blocks = [(b, (8 * (u % 3) + b + 8) % FT) for b in range(UNIT if u % 3 < 2 else FT - 2 * UNIT)]
                if u < 3:
                    pe.wait_ge(*after("in9_lo", 8 * u + len(blocks)))
                split_mm(ps[:, u // 3, 0:S], u % GROUP, blocks, u % 3 == 0, u % 3 == 2).then_inc(unit_done, 1)
        sum_total(5, "final", "final_sumsq")

    @block.scalar
    def _(act):
        act_in = [0]

        def link(ins):
            act_in[0] += 1
            ins.then_inc(sem("act_chain"), 1)
            act.wait_ge(*after("act_chain", act_in[0]))

        def high_part(r, u, i=None, stride=0):
            c = slice((r % PAIR) * UNIT * P, (r % PAIR + 1) * UNIT * P)
            if i is None:
                act.wait_ge(loaded, r // PAIR + 1)
                src = raw[:, (r // PAIR) % RAW, c]
            else:
                act.wait_ge(loaded, i * (stride // PAIR) + (r // PAIR + 1))
                slot = (i * (stride // PAIR) + r // PAIR) % RAW
                src = raw[:, bass.ds(slot, 1), c].rearrange("p a b -> p (a b)")
            act.copy(w_hi[:, u, :], src).then_inc(hi_done, 1)

        def high(name, n):
            if FIRST[name] + n >= GROUP:
                act.wait_ge(unit_done, FIRST[name] + n - GROUP + 1)
            high_part(place(name, n), n % GROUP)

        def project(name, evac, first_group=0, groups=None):
            first = FIRST[name]
            groups = COUNT[name] // GROUP if groups is None else groups
            with act.Fori(first_group, first_group + groups) as i:
                for u in range(GROUP):
                    act.wait_ge(unit_done, i * GROUP + (first + u + 1))
                    evac(i, u)
                    high_part(LOADED[name] + STRIDE[name] + u, u, i, STRIDE[name])

        def plain(dst):
            def evac(i, u):
                act.copy(dst[:, bass.ds(i * GROUP + u, 1), :], ps[:, u:u + 1, 0:S]).then_inc(taken, 1)
            return evac

        def split(tag, tiles, src, ready, ready_at, base=0):
            for k in range(tiles):
                act.wait_ge(*after(ready, ready_at(k)))
                act.copy(in_hi[:, base + k, :], src(k)).then_inc(sem(f"{tag}_hi"), 1)

        def square(tag, src, k):
            act.activation(sq[:, k, :], src[:, k, :], ACT.Square).then_inc(sem(f"{tag}_sq"), 1)

        def squares(tag, src, ready=None):
            for k in range(KT):
                if ready:
                    act.wait_ge(*after(ready, k + 1))
                square(tag, src, k)

        def root_table():
            link(act.activation(small[:, 1, 13:14], eps_col(EPS), ACT.Sqrt))

        def root(tag, eps):
            act.wait_ge(*after(f"{tag}_sumsq", 1))
            act.activation(stat[:, 1, :], half(5, 0), ACT.Sqrt, bias=eps_col(eps), scale=1.0 / D
                           ).then_inc(sem(f"{tag}_root"), 1)

        def eps_col(eps):
            return small[:, 1, 15:16] if eps == LN_EPS else small[:, 1, 14:15]

        act.sem_inc(taken, GROUP)
        act.wait_ge(*after("params_in", 16))
        act.activation(cs[:], param("c", 0, 8), ACT.Silu).then_inc(sem("cs_ready"), 1)
        act.wait_ge(*after("cs_ready", 1))
        for n in range(GROUP):
            high("moba_in", n)
        split("in0", KT, lambda k: h_t[:, k, :], "h0", lambda k: k + 1)
        project("moba_in", plain(proj), groups=6)

        def copy_out(name, n, dst):
            act.wait_ge(unit_done, FIRST[name] + n + 1)
            act.copy(dst, half(n % GROUP, 0)).then_inc(taken, 1)

        def stream(name, n, dst):
            copy_out(name, n, dst)
            high(name, n + GROUP)

        def natural(name, tiles, banks, dst):
            for g in range(tiles // 2):
                act.wait_ge(*after(f"{name}_turned", g + 1))
                act.copy(dst[:, :, 2 * g * P:2 * (g + 1) * P].rearrange("p c (t d) -> p t c d", t=2),
                         ps[:, banks[g % len(banks)], :].rearrange("p (t c d) -> p t c d", t=2, c=2)
                         ).then_inc(sem(f"{name}_natural"), 1)

        def attention(name, heads, finish, beside=None, round_next=None):
            for h in range(heads + 1):
                if h < heads:
                    act.wait_ge(*after(f"{name}_max", h + 1))
                    for qt in range(2):
                        act.activation(lg[name][h % 2][:, qt, :], lg[name][h % 2][:, qt, :], ACT.Exp,
                                       bias=small[:, 0, 4 * (h % 2) + qt:4 * (h % 2) + qt + 1],
                                       accum_out=small[:, 0, 4 * (h % 2) + 2 + qt:4 * (h % 2) + 3 + qt]
                                       ).then_inc(sem(f"{name}_exp"), 1)
                if beside and h >= 1:
                    beside(2 * h - 1)
                if h >= 1:
                    finish(h - 1)
                if beside and h < heads:
                    beside(2 * h)
                if h < heads:
                    act.wait_ge(*after(f"{name}_turned_p", h + 1))
                    if h >= 1:
                        act.wait_ge(*after(f"{name}_pv", h))
                    act.copy(flat(pt[name]), ps[:, 6, :]).then_inc(sem(f"{name}_pt"), 1)
                if round_next and h < heads:
                    round_next(2 * h)

        act.wait_ge(taken, all_taken("moba_in", 24))
        act.activation(proj[:, 16:24, :], proj[:, 16:24, :], ACT.Silu).then_inc(sem("moba_z"), 1)
        copy_out("moba_in", 24, proj[:, 24, :])

        def natural_v(t, bank):
            act.wait_ge(*after("moba_v_turned", t + 1))
            act.copy(moba_vnat[:, :, t * P:(t + 1) * P], half(bank, 0).rearrange("p (c d) -> p c d", c=2)
                     ).then_inc(sem("moba_v_natural"), 1)

        def beside_moba(n):
            h = n // 2
            if n % 2 == 0 and h < 6:
                copy_out("moba_in", 26 + h, proj[:, 26 + h, :])

        def after_pt(n):
            h = n // 2
            if h < 7:
                natural_v(h + 1, 4 + h % 2)
            for m in {0: (30,), 1: (31,), 5: (32,), 6: (33, 34), 7: (35,)}.get(h, ()):
                high("moba_in", m)

        natural_v(0, 6)
        copy_out("moba_in", 25, proj[:, 25, :])
        high("moba_in", 28)
        high("moba_in", 29)

        def moba_finish(h):
            act.wait_ge(*after("moba_out", h + 1))
            act.copy(in_hi[:, 8 + h, :], gated[h % 2]).then_inc(sem("in1_hi"), 1)

        attention("moba", 8, moba_finish, beside=beside_moba,
                  round_next=after_pt)
        root_table()
        for n in range(KT):
            high("moba_out", n + GROUP)
        squares("ln0", x_t, "ln0_centred")
        root("ln0", LN_EPS)
        for k in range(KT + 1):
            if k < KT:
                act.wait_ge(*after("ln0_scaled", k + 1))
                act.activation(h_t[:, k, :], sq[:, k, :], ACT.Identity, bias=ln_bias[:, 0, k:k + 1],
                               scale=mod[:, 1, 8 + k:9 + k]).then_inc(sem("h1"), 1)
            if k >= 1:
                act.wait_ge(*after("h1", k))
                act.copy(in_hi[:, k - 1, :], h_t[:, k - 1, :]).then_inc(sem("in2_hi"), 1)

        def evac_conv(i, u):
            act.wait_ge(*after("conv_free", i * GROUP + (u + 1)))
            act.copy(cin[u][:, 3:3 + S], ps[:, u, 0:S])
            act.activation(proj[:, bass.ds(i * GROUP + u, 1), :], ps[:, u:u + 1, 0:S], ACT.Copy,
                           scale=params[:, bass.ds(i * GROUP + (PCOL["gdn_conv"] + 72 + u), 1)]).then_inc(taken, 1)

        act.wait_ge(*after("ln0_x", KT))
        project("gdn_in", evac_conv, groups=1)
        act.activation(gexp[0:8, 2, 0:1], param("a_log", 0, 1, 8), ACT.Exp).then_inc(sem("gdn_a"), 1)
        act.wait_ge(*after("gdn_gates", 1))
        act.activation(rows[0:8, 3, :], ps[32:40, 6, 0:S], ACT.Sigmoid).then_inc(sem("gdn_rows"), 1)
        act.wait_ge(*after("gdn_z", 1))
        link(act.activation(rows[0:8, 1, :], rows[0:8, 0, :], ACT.Abs))
        link(act.activation(rows[0:8, 1, :], rows[0:8, 1, :], ACT.Exp, scale=-1.0))
        act.activation(rows[0:8, 1, :], rows[0:8, 1, :], ACT.Ln, bias=1.0).then_inc(sem("gdn_ln"), 1)
        project("gdn_in", evac_conv, first_group=1, groups=5)
        for n in range(8):
            act.wait_ge(unit_done, FIRST["gdn_in"] + 24 + n + 1)
            act.copy(proj[:, 24 + n, :], half(n % GROUP, 0)).then_inc(taken, 1)
            high("gdn_in", 24 + n + GROUP)
            if n < 6:
                act.wait_ge(*after("conv_free", GROUP + 4 * (n + 1)))
                act.activation(proj[:, 4 * n:4 * n + 4, :], proj[:, 4 * n:4 * n + 4, :], ACT.Silu
                               ).then_inc(sem("gdn_silu"), 1)
            if n == 6:
                act.wait_ge(*after("gdn_sum", 4))
                act.activation(rows[0:16, 5, :], ps[0:16, 7, 0:S], ACT.Sqrt, bias=small[0:16, 1, 14:15]
                               ).then_inc(sem("gdn_len"), 1)
        act.wait_ge(taken, all_taken("gdn_in"))
        act.activation(proj[:, 24:32, :], proj[:, 24:32, :], ACT.Silu).then_inc(sem("gdn_silu"), 1)
        act.wait_ge(*after("gdn_cols", 1))
        act.copy(gcol[:].rearrange("p a b c -> p (a b c)"), ps[:, 6, 0:32]).then_inc(sem("gdn_col_done"), 1)
        act.wait_ge(*after("gdn_col_done", 1))
        act.activation(gexp[:, 1, :], gcol[:, 0, 1, :], ACT.Exp).then_inc(sem("gdn_e1"), 1)
        for sg in range(2):
            for p in range(2):
                g = 2 * sg + p
                act.wait_ge(*after("gdn_bc", g + 1))
                if sg:
                    act.wait_ge(*after("gdn_ot", 2 * sg))
                for m in range(2):
                    act.activation(qg[:, 2 * p + m, :], ps[:, m, P:S], ACT.Exp).then_inc(sem("gdn_qe"), 1)
                act.wait_ge(*after("gdn_diff", g + 1))
                act.activation(flat(dec), flat(dec), ACT.Exp).then_inc(sem("gdn_dec"), 1)
                act.wait_ge(*after("gdn_nat", g + 1))
                act.wait_ge(*after("gdn_e0", 2 * (g + 1)))
                act.wait_ge(*after("gdn_e1", 2))
                link(act.activation(gexp[:, 0, 2 * g:2 * g + 2], gexp[:, 2, 2 * g:2 * g + 2], ACT.Exp))
                for m in range(2):
                    h = 2 * g + m
                    for c in range(2):
                        j = 2 * m + c
                        act.activation(kdg[p][:, j, :], ps[:, 2, j * P:(j + 1) * P], ACT.Copy,
                                       scale=gexp[:, c, h:h + 1]).then_inc(sem("gdn_kdg"), 1)
            for lv in range(1, LEVELS):
                for p in range(2):
                    act.wait_ge(*after("gdn_p", (sg * LEVELS + lv) * 2 + p + 1))
                    act.copy(flat(pm[p]), ps[:, 6 + p, :]).then_inc(sem("gdn_ps"), 1)
            act.wait_ge(*after("gdn_u0", sg + 1))
            act.copy(flat(u0), ps[:, 6, :]).then_inc(sem("gdn_u0s"), 1)
            act.wait_ge(*after("gdn_w", sg + 1))
            act.mul(flat(wn), ps[:, 7, :], -1.0).then_inc(sem("gdn_ws"), 1)
            if sg:
                for q in range(2):
                    act.activation(osq[0][:, 2 * q:2 * q + 2, :], proj[:, 2 * q:2 * q + 2, :], ACT.Square
                                   ).then_inc(sem("gdn_osq"), 1)
                root_table()
                for q in range(2):
                    act.wait_ge(*after("gdn_ot", 3 + q))
                    act.activation(flat(osq[1][:, 2 * q:2 * q + 2, :]), ps[:, 2 + q, :], ACT.Square
                                   ).then_inc(sem("gdn_osq"), 1)
                continue
            for q in range(2):
                act.wait_ge(*after("gdn_ot", 2 * sg + q + 1))
                act.copy(flat(proj[:, 4 * sg + 2 * q:4 * sg + 2 * q + 2, :]), ps[:, 2 + q, :]).then_inc(sem("gdn_o"), 1)
        act.wait_ge(*after("gdn_osum", 2))
        act.activation(rows[0:8, 5, :], ps[0:8, 0, 0:S], ACT.Sqrt, bias=small[0:8, 1, 14:15], scale=1.0 / P
                       ).then_inc(sem("gdn_rms"), 1)
        split("in3", KT, lambda k: proj[:, k, :], "gdn_gated", lambda k: k // 2 + 1)

        act.wait_ge(*after("mem_in", 16))
        squares("mem", proj[:, 8:16, :])
        for n in range(KT):
            high("gdn_out", n + GROUP)
            if n == 3:
                root("mem", EPS)
            if n in (4, 5):
                for k in range(4 * (n - 4), 4 * (n - 3)):
                    act.wait_ge(*after("mem_h", k + 1))
                    act.copy(in_hi[:, 8 + k, :], h_t[:, k, :]).then_inc(sem("in4_hi"), 1)
        squares("ln1", x_t, "ln1_centred")
        for n in range(KT):
            act.wait_ge(unit_done, FIRST["mem_kv"] + n + 1)
            act.copy(memkv[:, n, :], half(n % GROUP, 0)).then_inc(taken, 1)
            high("mem_kv", n + GROUP)
            if n == 1:
                root("ln1", LN_EPS)
                for k in range(KT + 1):
                    if k < KT:
                        act.wait_ge(*after("ln1_scaled", k + 1))
                        act.activation(x_t[:, k, :], sq[:, k, :], ACT.Identity, bias=param("ln_b", 8 + k)
                                       ).then_inc(sem("ln1_x"), 1)
                    if k >= 1:
                        act.wait_ge(*after("ln1_x", k))
                        square("mix", x_t, k - 1)
            if n == 4:
                root("mix", EPS)
            if n in (5, 6):
                for k in range(4 * (n - 5), 4 * (n - 4)):
                    act.wait_ge(*after("mix_h", k + 1))
                    act.copy(in_hi[:, k, :], h_t[:, k, :]).then_inc(sem("in5_hi"), 1)
        natural("mem_v", 4, (4, 5), mem_vnat)
        project("w_in", plain(proj), groups=1)
        act.wait_ge(*after("ml_pre", 2))
        link(act.activation(rows[:, 2, :], rows[:, 1, :], ACT.Abs))
        link(act.activation(rows[:, 2, :], rows[:, 2, :], ACT.Exp, scale=-1.0))
        act.activation(rows[:, 2, :], rows[:, 2, :], ACT.Ln, bias=1.0).then_inc(sem("ml_ln"), 1)
        project("w_in", plain(proj), first_group=1, groups=3)
        act.wait_ge(taken, all_taken("w_in", 16))
        act.wait_ge(*after("ml_cols", 1))
        for c in range(2):
            act.activation(mcol[:, 1, c, :], ps[:, 4, (2 + c) * 40:(2 + c) * 40 + ML_ROWS], ACT.Exp, scale=-1.0
                           ).then_inc(sem("ml_cols_taken"), 1)
        natural("ml_v", 4, (5, 6), ml_vnat)
        act.activation(proj[:, 12:16, :], proj[:, 12:16, :], ACT.Sigmoid).then_inc(sem("ml_o"), 1)
        for n in range(4):
            stream("w_in", 16 + n, proj[:, 16 + n, :])
            for t in (n, 4 + n):
                act.wait_ge(*after("ml_conv", 2 * n + 1 + t // 4))
                act.activation(proj[:, t, :], gsq[:, (2 * n + t // 4) % 4, :], ACT.Silu, bias=param("ml_conv_b", t)
                               ).then_inc(sem("ml_qk"), 1)

        def ml_exp(h):
            act.wait_ge(*after("ml_diff", h + 1))
            act.activation(flat(eb[h % 2]), flat(eb[h % 2]), ACT.Exp).then_inc(sem("ml_exp"), 1)

        ml_exp(0)
        for h in range(4):
            if h < 3:
                ml_exp(h + 1)
            for n in (20 + 3 * h, 21 + 3 * h):
                stream("w_in", n, proj[:, n, :])
            act.wait_ge(*after("ml_turned_p", h + 1))
            if h >= 1:
                act.wait_ge(*after("ml_pv", h))
            act.copy(flat(pt["ml"]), ps[:, 7, :]).then_inc(sem("ml_pt"), 1)
            if h < 3:
                stream("w_in", 22 + 3 * h, proj[:, 22 + 3 * h, :])
            act.wait_ge(*after("ml_pv", h + 1))
            act.activation(gsq[:, h, :], half(7, 0), ACT.Square).then_inc(sem("ml_hsq"), 1)
        natural("na_v", 4, (4, 5), vnat)
        act.wait_ge(*after("ml_hsum", 1))
        act.activation(rows[0:4, 0, :], ps[0:4, 6, 0:S], ACT.Sqrt, bias=small[0:4, 1, 14:15], scale=1.0 / P
                       ).then_inc(sem("ml_root"), 1)
        stream("w_in", 31, proj[:, 31, :])
        split("in6m", 4, lambda k: proj[:, k, :], "ml_rms", lambda k: k // 2 + 1, base=8)

        def high_of(name, base, h, rows_):
            act.wait_ge(*after(f"{name}_pv", h + 1))
            p0 = rows_ * (h % 2) if rows_ == 64 else 0
            t = h // 2 if rows_ == 64 else h
            act.copy(in_hi[p0:p0 + rows_, base + t, :], ps[p0:p0 + rows_, 7, 0:S]).then_inc(sem(f"{name}_high"), 1)

        def gate(n):
            act.wait_ge(unit_done, FIRST["merge"] + n + 1)
            act.activation(proj[:, n, :], half(n % GROUP, 0), ACT.Identity, bias=param("merge_b", n)).then_inc(taken, 1)
            if n % 2:
                high("merge", n + GROUP)

        act.wait_ge(*after("in6m_lo", 4))
        attention("na", 8, lambda h: high_of("na", 12, h, 64), beside=gate,
                  round_next=lambda n: high("merge", n + GROUP))
        attention("xa", 4, lambda h: high_of("xa", 16, h, P), beside=lambda n: gate(16 + n),
                  round_next=lambda n: high("merge", 16 + n + GROUP))
        act.wait_ge(taken, all_taken("merge"))
        for b in range(3):
            act.activation(proj[:, 8 * b:8 * b + 8, :], proj[:, 8 * b:8 * b + 8, :], ACT.Sigmoid).then_inc(sem("gates"), 1)
        act.wait_ge(taken, all_taken("merge"))
        for n in range(COUNT["branch"]):
            high("branch", n + GROUP)
        split("in7", KT, lambda k: h_t[:, k, :], "merged", lambda k: 9 + k // 2)
        root_table()
        for n in range(KT):
            high("w_out", n + GROUP)
            act.wait_ge(taken, all_taken("w_out", n + 1))
            square("ffn", x_t, n)
        root("ffn", EPS)
        split("in8", KT, lambda k: h_t[:, k, :], "ffn_h", lambda k: k + 1)

        def ffn(i, base):
            first = FIRST["ffn_up"] + GROUP * base
            for m in range(2):
                act.wait_ge(unit_done, i * GROUP + (first + 2 * m + 1))
                act.wait_ge(*after("ffn_pair_free", i * 2 + (2 * base + m + 1)))
                act.copy(cin[m][:, 1:1 + S], ps[:, 2 * m, 0:S]).then_inc(taken, 1)
                act.wait_ge(unit_done, i * GROUP + (first + 2 * m + 2))
                act.copy(fbuf[m][:, 1, :], ps[:, 2 * m + 1, 0:S]).then_inc(taken, 1)
                for u in (2 * m, 2 * m + 1):
                    high_part(LOADED["ffn_up"] + GROUP * (base + 1) + u, u, i, GROUP)
                if base:
                    act.wait_ge(*after("ffn_pair_free", i * 2 + (3 + m)))
                    act.copy(in_hi[:, bass.ds(i * 2 + (8 + m), 1), :], proj[:, bass.ds(i * 2 + m, 1), :]
                             ).then_inc(sem("in9_hi"), 1)
                act.wait_ge(*after("ffn_conv", i * 6 + (6 * base + 3 * m + 3)))
                act.activation(fbuf[m][:, 0, :], fbuf[m][:, 0, :], ACT.Gelu_apprx_tanh,
                               bias=params[:, bass.ds(i * 2 + (PCOL["ffn_conv_b"] + 2 * base + m), 1)]
                               ).then_inc(sem("ffn_gelu"), 1)

        with act.Fori(0, 4) as i:
            ffn(i, 0)
        with act.Fori(0, 7) as i:
            ffn(i, 4)
        act.wait_ge(unit_done, FIRST["ffn_down"])
        for k in range(14, FT):
            act.wait_ge(*after("ffn_pair_free", 2 + k + 1))
            act.copy(in_hi[:, k - 14, :], proj[:, k, :]).then_inc(sem("in9_hi"), 1)
        first = FIRST["ffn_down"]
        for n in range(COUNT["ffn_down"]):
            if first + n + GROUP < UNITS:
                high("ffn_down", n + GROUP)
            if n == 2:
                root_table()
            if n % 3 == 2:
                act.wait_ge(taken, all_taken("ffn_down", n // 3 + 1))
                square("final", x_t, n // 3)
        root("final", EPS)

    @block.vector
    def _(dve):
        count = [0]

        def link(ins):
            count[0] += 1
            ins.then_inc(sem("dve_chain"), 1)
            dve.wait_ge(*after("dve_chain", count[0]))

        def unit_at(r, i=None, stride=0):
            c = slice((r % PAIR) * UNIT * P, (r % PAIR + 1) * UNIT * P)
            if i is None:
                return raw[:, (r // PAIR) % RAW, c]
            slot = (i * (stride // PAIR) + r // PAIR) % RAW
            return raw[:, bass.ds(slot, 1), c].rearrange("p a b -> p (a b)")

        def low_part(src, u):
            dve.tensor_tensor(w_lo[:, u, :], src, w_hi[:, u, :].bitcast(F32), ALU.subtract).then_inc(lo_done, 1)

        def low(name, n):
            dve.wait_ge(hi_done, FIRST[name] + n + 1)
            low_part(unit_at(place(name, n)), n % GROUP)

        def low_in_loop(name, i, u):
            dve.wait_ge(hi_done, i * GROUP + (FIRST[name] + u + GROUP + 1))
            low_part(unit_at(LOADED[name] + STRIDE[name] + u, i, STRIDE[name]), u)

        def project(name, before=None, first_group=0, groups=None):
            groups = COUNT[name] // GROUP if groups is None else groups
            with dve.Fori(first_group, first_group + groups) as i:
                for u in range(GROUP):
                    if before:
                        before(i, u)
                    low_in_loop(name, i, u)

        def split(tag, tiles, src, base=0):
            for k in range(tiles):
                dve.wait_ge(*after(f"{tag}_hi", k + 1))
                dve.tensor_tensor(in_lo[:, base + k, :], src(k), in_hi[:, base + k, :].bitcast(F32), ALU.subtract
                                  ).then_inc(sem(f"{tag}_lo"), 1)

        def h_tile(k):
            return h_t[:, k, :]

        for m in range(GROUP):
            link(dve.memset(cin[m], 0.0))
        link(dve.memset(small[:, 1, 14:15], EPS))
        link(dve.memset(small[:, 1, 15:16], LN_EPS))
        dve.memset(rows[:], 0.0).then_inc(sem("rows_zero"), 1)
        dve.sem_inc(sem("conv_free"), GROUP)
        dve.wait_ge(*after("cs_ready", 1))
        for t in range(16):
            c, k = divmod(t, KT)
            dve.wait_ge(loaded, t // PAIR + 1)
            if k == 0:
                ins = dve.tensor_scalar(acc[:, c, :], unit_at(t), cs[:, 0:1], None, ALU.mult)
            else:
                dve.wait_ge(lo_done, t)
                ins = dve.scalar_tensor_tensor(acc[:, c, :], unit_at(t), cs[:, k:k + 1], acc[:, c, :],
                                               ALU.mult, ALU.add)
            ins.then_inc(lo_done, 1)
        for n in range(GROUP):
            low("moba_in", n)

        flat_mod = mod[:].rearrange("p a b -> p (a b)")

        def modulation(at, chunks, column, one_plus=None):
            link(dve.tensor_tensor(flat_mod[:, KT * at:KT * (at + chunks)], ps[:, 7, column:column + KT * chunks],
                                   param("ada_b", KT * at, KT * chunks), ALU.add))
            if one_plus is not None:
                scale = flat_mod[:, one_plus * KT:one_plus * KT + KT]
                link(dve.tensor_scalar(scale, scale, 1.0, None, ALU.add))

        dve.wait_ge(*after("mod_first", 1))
        modulation(0, 2, 0, one_plus=1)
        dve.wait_ge(*after("x_in", 16))
        for k in range(KT):
            dve.tensor_scalar(h_t[:, k, :], x_t[:, k, :], mod[:, 0, 8 + k:9 + k], mod[:, 0, k:k + 1], ALU.mult, ALU.add
                              ).then_inc(sem("h0"), 1)
        split("in0", KT, h_tile)
        dve.wait_ge(*after("acc_zero", 1))
        with dve.Fori(0, 6) as i:
            for u in range(GROUP):
                r = LOADED["moba_in"] + GROUP + u
                dve.wait_ge(loaded, i * (8 // PAIR) + (r // PAIR + 1))
                dve.wait_ge(lo_done, i * 8 + r)
                a = acc[:, bass.ds(i // 2, 1), :].rearrange("p a b -> p (a b)")
                dve.scalar_tensor_tensor(a, unit_at(r, i, 8), cs[:, bass.ds((i % 2) * GROUP + u, 1)], a,
                                         ALU.mult, ALU.add).then_inc(lo_done, 1)
            for u in range(GROUP):
                low_in_loop("moba_in", i, u)

        def add_modulation(g, u):
            r = LOADED["moba_in"] + 8 * g + GROUP + u
            k = (g % 2) * GROUP + u
            dve.wait_ge(loaded, r // PAIR + 1)
            dve.wait_ge(lo_done, r)
            dve.scalar_tensor_tensor(acc[:, g // 2, :], unit_at(r), cs[:, k:k + 1], acc[:, g // 2, :],
                                     ALU.mult, ALU.add).then_inc(lo_done, 1)


        def attention(name, heads, logits, finish, beside=None):
            for h in range(heads + 1):
                if h < heads:
                    dve.wait_ge(*after(f"{name}_scores", h + 1))
                    if h >= 2:
                        dve.wait_ge(*after(f"{name}_turned_p", h - 1))
                    logits(h)
                    dve.wait_ge(*after(f"{name}_logits", h + 1))
                    dve.tensor_reduce(small[:, 0, 4 * (h % 2):4 * (h % 2) + 2], lg[name][h % 2], X, ALU.max, negate=True
                                      ).then_inc(sem(f"{name}_max"), 1)
                if beside and h >= 1:
                    beside(2 * h - 2)
                if h < heads:
                    dve.wait_ge(*after(f"{name}_exp", 2 * h + 2))
                    a = small[:, 0, 4 * (h % 2) + 2:4 * (h % 2) + 4]
                    link(dve.reciprocal(a, a))
                    for qt in range(2):
                        ins = dve.tensor_scalar(lg[name][h % 2][:, qt, :], lg[name][h % 2][:, qt, :], a[:, qt:qt + 1], None, ALU.mult)
                    ins.then_inc(sem(f"{name}_probs"), 1)
                if h >= 1:
                    finish(h - 1)
                if beside and h >= 1:
                    beside(2 * h - 1)

        def low_of(name, base, h, rows_):
            dve.wait_ge(*after(f"{name}_high", h + 1))
            p0 = rows_ * (h % 2) if rows_ == 64 else 0
            t = h // 2 if rows_ == 64 else h
            dve.tensor_tensor(in_lo[p0:p0 + rows_, base + t, :], ps[p0:p0 + rows_, 7, 0:S],
                              in_hi[p0:p0 + rows_, base + t, :].bitcast(F32), ALU.subtract).then_inc(sem(f"{name}_out"), 1)

        def moba_logits(h):
            for qt in range(2):
                ins = dve.scalar_tensor_tensor(lg["moba"][h % 2][:, qt, :], half(4 + h % 2, qt), float(P) ** -0.5,
                                               strip("neg", qt), ALU.mult, ALU.add)
            ins.then_inc(sem("moba_logits"), 1)

        def moba_finish(h):
            dve.wait_ge(*after("moba_pv", h + 1))
            if h >= 2:
                dve.wait_ge(*after("in1_hi", h - 1))
            dve.tensor_tensor(gated[h % 2], half(7, 0), proj[:, 16 + h, :], ALU.mult).then_inc(sem("moba_out"), 1)
            dve.wait_ge(*after("in1_hi", h + 1))
            dve.tensor_tensor(in_lo[:, 8 + h, :], gated[h % 2], in_hi[:, 8 + h, :].bitcast(F32), ALU.subtract
                              ).then_inc(sem("in1_lo"), 1)

        dve.wait_ge(*after("moba_z", 1))
        dve.wait_ge(*after("mod_gate", 1))
        modulation(2, 1, 0)
        dve.sem_inc(sem("mod_read"), 1)
        for u in range(2):
            add_modulation(6, u)

        def beside_moba(n):
            if n == 0:
                add_modulation(6, 2)
                add_modulation(6, 3)
            if n in (1, 2, 3, 4):
                low("moba_in", 27 + n)
            if n in (5, 6, 7, 8):
                add_modulation(7, n - 5)
            if n in (11, 13, 14, 15):
                low("moba_in", {11: 32, 13: 33, 14: 34, 15: 35}[n])

        dve.wait_ge(*after("masks_in", 16))
        attention("moba", 8, moba_logits, moba_finish, beside=beside_moba)
        def residual(name, n, gate=None, unit=None):
            y = half(n % GROUP, 0)
            dve.wait_ge(unit_done, FIRST[name] + (n if unit is None else unit) + 1)
            if gate is None:
                dve.tensor_tensor(x_t[:, n, :], x_t[:, n, :], y, ALU.add).then_inc(taken, 1)
            else:
                dve.scalar_tensor_tensor(x_t[:, n, :], y, gate, x_t[:, n, :], ALU.mult, ALU.add).then_inc(taken, 1)

        def centre(tag):
            dve.wait_ge(*after(f"{tag}_sum", 1))
            for k in range(KT):
                dve.scalar_tensor_tensor(x_t[:, k, :], half(4, 0), -1.0 / D, x_t[:, k, :], ALU.mult, ALU.add
                                         ).then_inc(sem(f"{tag}_centred"), 1)

        def invert(tag):
            dve.wait_ge(*after(f"{tag}_root", 1))
            link(dve.reciprocal(stat[:, 1, :], stat[:, 1, :]))

        def scaled(src, dst, gain, k, done):
            dve.scalar_tensor_tensor(dst[:, k, :], src[:, k, :], param(gain[0], gain[1] + k),
                                     stat[:, 1, :], ALU.mult, ALU.mult).then_inc(sem(done), 1)

        def low_input(tag, k, src, base=0):
            dve.wait_ge(*after(f"{tag}_hi", k + 1))
            dve.tensor_tensor(in_lo[:, base + k, :], src, in_hi[:, base + k, :].bitcast(F32), ALU.subtract
                              ).then_inc(sem(f"{tag}_lo"), 1)

        dve.wait_ge(*after("x_alpha", 1))
        for n in range(KT):
            residual("moba_out", n, mod[:, 0, 16 + n:17 + n])
            low("moba_out", n + GROUP)
            if n == 5:
                dve.wait_ge(*after("mod_rest", 2))
                modulation(3, 2, KT, one_plus=4)
                link(dve.tensor_tensor(ln_bias[:, 0, :], param("ln_b", 0, KT), mod[:, 1, 8:16], ALU.mult))
                link(dve.tensor_tensor(ln_bias[:, 0, :], ln_bias[:, 0, :], mod[:, 1, 0:8], ALU.add))
                link(dve.tensor_scalar(ln_bias[:, 1, :], param("ln_b", 0, KT), ALPHA, None, ALU.mult))
        centre("ln0")
        invert("ln0")
        for k in range(KT + 2):
            if k < KT:
                scaled(x_t, sq, ("ln_g", 0), k, "ln0_scaled")
            if k >= 2:
                low_input("in2", k - 2, h_tile(k - 2))

        dve.wait_ge(*after("mod_last", 1))
        modulation(5, 1, 3 * KT)
        dve.wait_ge(*after("ln0_scaled", KT))
        for k in range(KT):
            dve.tensor_scalar(x_t[:, k, :], sq[:, k, :], ALPHA, ln_bias[:, 1, k:k + 1], ALU.mult, ALU.add
                              ).then_inc(sem("ln0_x"), 1)
        dve.wait_ge(*after("ln0_x", KT))
        for m in range(GROUP):
            dve.memset(cin[m][:, 0:3], 0.0).then_inc(sem("edges"), 1)
        def conv(i, u):
            first = FIRST["gdn_in"]
            dve.wait_ge(taken, i * GROUP + (GROUP + first + u + 1))
            tile = proj[:, bass.ds(i * GROUP + u, 1), :]
            for n, tap in enumerate((2, 1, 0)):
                if n:
                    dve.wait_ge(*after("conv_tap", i * 8 + (2 * u + n)))
                ins = dve.scalar_tensor_tensor(tile, cin[u][:, tap:tap + S].rearrange("p (a b) -> p a b", a=1),
                                               params[:, bass.ds(i * GROUP + (PCOL["gdn_conv"] + 24 * tap + u), 1)],
                                               tile, ALU.mult, ALU.add)
                ins.then_inc(sem("conv_tap") if n < 2 else sem("conv_free"), 1)

        dve.wait_ge(*after("edges", GROUP))
        project("gdn_in", conv, groups=1)
        dve.wait_ge(*after("gdn_gates", 1))
        dve.tensor_scalar(rows[0:8, 0, :], ps[0:8, 6, 0:S], param("dt_bias", 0, 1, 8), None, ALU.add
                          ).then_inc(sem("gdn_z"), 1)
        dve.wait_ge(*after("gdn_ln", 1))
        link(dve.scalar_tensor_tensor(rows[0:8, 0, :], rows[0:8, 0, :], 0.0, rows[0:8, 1, :], ALU.max, ALU.add))
        dve.wait_ge(*after("gdn_a", 1))
        link(dve.tensor_scalar(rows[0:8, 0, :], rows[0:8, 0, :], gexp[0:8, 2, 0:1], -1.0, ALU.mult, ALU.mult))
        for c in range(2):
            ins = dve.tensor_tensor_scan(rows[0:8, 2, c * P:(c + 1) * P], rows[0:8, 4, c * P:(c + 1) * P],
                                         rows[0:8, 0, c * P:(c + 1) * P], 0.0, ALU.add, ALU.add)
        ins.then_inc(sem("gdn_rows"), 1)
        project("gdn_in", conv, first_group=1, groups=5)
        def unit_length(t):
            two = proj[:, 2 * t:2 * t + 2, :]
            dve.wait_ge(*after("gdn_unit_bc", t + 1))
            dve.scalar_tensor_tensor(two, two, float(P) ** -0.5 if t < 4 else 1.0,
                                     ps[:, (4, 5, 7, 3)[t % 4], :].rearrange("p (a b) -> p a b", a=2),
                                     ALU.mult, ALU.mult).then_inc(sem("gdn_unit"), 1)

        for n in range(8):
            low("gdn_in", 24 + n + GROUP)
            if n < 4:
                dve.wait_ge(*after("gdn_silu", n + 1))
                if n == 3:
                    dve.wait_ge(*after("gdn_sum", 1))
                dve.tensor_tensor(lsq[:, 4 * n % 12:4 * n % 12 + 4, :], proj[:, 4 * n:4 * n + 4, :],
                                  proj[:, 4 * n:4 * n + 4, :], ALU.mult).then_inc(sem("gdn_sq"), 1)
            if n == 6:
                dve.wait_ge(*after("gdn_len", 1))
                dve.reciprocal(rows[0:16, 5, :], rows[0:16, 5, :]).then_inc(sem("gdn_len"), 1)
        for t in range(8):
            unit_length(t)
        dve.wait_ge(*after("gdn_e1", 1))
        dve.tensor_tensor(gexp[:, 1, :], gexp[:, 1, :], gcol[:, 1, 1, :], ALU.mult).then_inc(sem("gdn_e1"), 1)
        dve.wait_ge(*after("gdn_unit", 8))
        one = ident.rearrange("p (a b) -> p a b", a=1).to_broadcast([P, 4, P])
        for sg in range(2):
            for p in range(2):
                g = 2 * sg + p
                dve.wait_ge(*after("gdn_bc", g + 1))
                dve.wait_ge(*after("gdn_qe", 2 * (g + 1)))
                if g:
                    dve.wait_ge(*after("gdn_gram", g))
                    dve.wait_ge(*after("gdn_a0", g))
                for m in range(2):
                    h = 2 * g + m
                    dve.tensor_tensor(kb[:, m, :], half(m, 1), proj[:, 8 + h, :], ALU.mult).then_inc(sem("gdn_kb"), 1)
                    dve.tensor_scalar(gexp[:, 2, h:h + 1], ps[:, m, P - 1:P], gcol[:, 0, 0, h:h + 1], None, ALU.subtract
                                      ).then_inc(sem("gdn_e0"), 1)
                    for c in range(2):
                        ins = dve.tensor_scalar(dec[:, 2 * m + c, :], ps[:, m, c * P:(c + 1) * P],
                                                gcol[:, 0, c, h:h + 1], 0.0, ALU.subtract, ALU.min)
                ins.then_inc(sem("gdn_diff"), 1)
                dve.wait_ge(*after("gdn_nat", g + 1))
                for m in range(2):
                    for c in range(2):
                        j = 2 * m + c
                        dve.tensor_scalar(vb[p][:, j, :], ps[:, 3, j * P:(j + 1) * P],
                                          gcol[:, 1, c, 2 * g + m:2 * g + m + 1], None, ALU.mult).then_inc(sem("gdn_vb"), 1)
                dve.wait_ge(*after("gdn_gram", g + 1))
                dve.wait_ge(*after("gdn_dec", g + 1))
                dve.tensor_tensor(flat(lt[p]), ps[:, 4, :], flat(dec), ALU.mult).then_inc(sem("gdn_lt"), 1)
                dve.tensor_tensor(flat(aqk[p]), ps[:, 5, :], flat(dec), ALU.mult).then_inc(sem("gdn_a0"), 1)
            for lv in range(LEVELS):
                for p in range(2):
                    n = (sg * LEVELS + lv) * 2 + p
                    t, tt = tri(8, 2 * sg + p), tri(16, 2 * sg + p)
                    if lv == 0:
                        dve.wait_ge(*after("gdn_p", n + 1))
                        dve.tensor_tensor(t, one, ps[:, 6 + p, :].rearrange("p (a b) -> p a b", a=4), ALU.subtract)
                        dve.tensor_tensor(tt, one, ctm[p], ALU.subtract).then_inc(sem("gdn_t"), 1)
                        continue
                    dve.wait_ge(*after("gdn_t", n - 1))
                    dve.wait_ge(*after("gdn_d", (sg * (LEVELS - 1) + lv - 1) * 2 + p + 1))
                    if lv < LEVELS - 1:
                        dve.tensor_tensor(t, t, ps[:, 2 * p, :].rearrange("p (a b) -> p a b", a=4), ALU.subtract)
                    dve.tensor_tensor(tt, tt, ps[:, 2 * p + 1, :].rearrange("p (a b) -> p a b", a=4), ALU.subtract
                                      ).then_inc(sem("gdn_t"), 1)
            dve.wait_ge(*after("gdn_s1", sg + 1))
            dve.tensor_copy(flat(s1), ps[:, 5, :]).then_inc(sem("gdn_s1s"), 1)
            dve.wait_ge(*after("gdn_v1", sg + 1))
            dve.tensor_copy(flat(v1), ps[:, 4, :]).then_inc(sem("gdn_v1s"), 1)
        for t in range(4):
            two = proj[:, 2 * t:2 * t + 2, :]
            if t < 2:
                dve.wait_ge(*after("gdn_osq", t + 1))
                src = two
            else:
                dve.wait_ge(*after("gdn_osq", t + 1))
                src = ps[:, t, :].rearrange("p (a b) -> p a b", a=2)
            dve.scalar_tensor_tensor(two, src, param("gdn_norm"), proj[:, 24 + 2 * t:26 + 2 * t, :],
                                     ALU.mult, ALU.mult).then_inc(sem("gdn_weighted"), 1)
        dve.wait_ge(*after("gdn_rms", 1))
        dve.reciprocal(rows[0:8, 5, :], rows[0:8, 5, :]).then_inc(sem("gdn_rms"), 1)
        dve.wait_ge(*after("gdn_weighted", 4))
        for t in range(KT // 2 + 1):
            if t < KT // 2:
                two = proj[:, 2 * t:2 * t + 2, :]
                dve.wait_ge(*after("gdn_gated_bc", t + 1))
                dve.tensor_tensor(two, two, ps[:, 4 + t, :].rearrange("p (a b) -> p a b", a=2), ALU.mult
                                  ).then_inc(sem("gdn_gated"), 1)
            if t >= 1:
                for k in (2 * t - 2, 2 * t - 1):
                    low_input("in3", k, proj[:, k, :])

        for n in range(KT):
            residual("gdn_out", n, mod[:, 1, 16 + n:17 + n])
            if n == 7:
                for k in range(4, 8):
                    low_input("in4", k, h_tile(k), base=8)
            low("gdn_out", n + GROUP)
            if n == 3:
                invert("mem")
            if n in (3, 4):
                for k in range(4 * (n - 3), 4 * (n - 2)):
                    scaled(proj[:, 8:16, :], h_t, ("mem_norm", 0), k, "mem_h")
            if n == 5:
                for k in range(4):
                    low_input("in4", k, h_tile(k), base=8)
        centre("ln1")
        for n in range(KT):
            low("mem_kv", n + GROUP)
            if n == 1:
                invert("ln1")
                for k in range(KT):
                    scaled(x_t, sq, ("ln_g", 8), k, "ln1_scaled")
            if n == 4:
                invert("mix")
                for k in range(KT):
                    scaled(x_t, h_t, ("mix_norm", 0), k, "mix_h")
            if n in (5, 6):
                for k in range(4 * (n - 5), 4 * (n - 4)):
                    low_input("in5", k, h_tile(k))
        project("w_in", groups=1)
        dve.wait_ge(*after("ml_gates", 1))
        dve.tensor_scalar(rows[:, 0, :], ps[0:ML_ROWS, 6, 0:S], param("b_ig", 0, 1, ML_ROWS), None, ALU.add
                          ).then_inc(sem("ml_pre"), 1)
        dve.tensor_scalar(rows[:, 1, :], ps[64:64 + ML_ROWS, 6, 0:S], param("b_fg", 0, 1, ML_ROWS), None, ALU.add
                          ).then_inc(sem("ml_pre"), 1)
        dve.wait_ge(*after("ml_ln", 1))
        link(dve.scalar_tensor_tensor(rows[:, 1, :], rows[:, 1, :], 0.0, rows[:, 2, :], ALU.min, ALU.subtract))
        link(dve.memset(rows[:, 4, :], 0.0))
        link(dve.tensor_tensor_scan(rows[:, 2, :], rows[:, 4, :], rows[:, 1, :], 0.0, ALU.add, ALU.add))
        link(dve.tensor_tensor(rows[32:36, 2, :], rows[32:36, 1, :], rows[32:36, 2, :], ALU.subtract))
        link(dve.tensor_tensor(rows[:, 3, :], rows[:, 0, :], rows[:, 2, :], ALU.subtract))
        link(dve.tensor_tensor_scan(rows[0:4, 4, :], rows[0:4, 3, :], rows[0:4, 3, :], NEG, ALU.max, ALU.max))
        link(dve.tensor_tensor_scan(rows[32:36, 4, ::-1], rows[32:36, 3, ::-1], rows[32:36, 3, ::-1], NEG, ALU.max, ALU.max))
        link(dve.tensor_tensor(rows[:, 5, :], rows[:, 2, :], rows[:, 4, :], ALU.add))
        dve.tensor_scalar(rows[:, 5, :], rows[:, 5, :], -88.0, None, ALU.max).then_inc(sem("ml_gate_rows"), 1)
        project("w_in", first_group=1, groups=3)
        dve.wait_ge(taken, all_taken("w_in", 16))
        dve.wait_ge(*after("ml_cols", 1))
        dve.wait_ge(*after("ml_cols_taken", 2))
        for c in range(2):
            link(dve.tensor_copy(mcol[:, 0, c, :], ps[:, 4, c * 40:c * 40 + ML_ROWS]))
        dve.sem_inc(sem("ml_cols_taken"), 1)

        def ml_diff(h):
            dve.wait_ge(*after("ml_scores", h + 1))
            if h >= 2:
                dve.wait_ge(*after("ml_w", 2 * (h - 1)))
            for d in range(2):
                for qt in range(2):
                    r = h + 32 * d
                    ins = dve.tensor_scalar(eb[h % 2][:, 2 * d + qt, :], half(6, d), mcol[:, 0, qt, r:r + 1], 0.0,
                                            ALU.subtract, ALU.min)
            ins.then_inc(sem("ml_diff"), 1)

        for m in range(8):
            if m == 6:
                ml_diff(0)
            n, t = m // 2, m // 2 + 4 * (m % 2)
            if m >= 4:
                dve.wait_ge(*after("ml_qk", m - 3))
            out, src = gsq[:, m % 4, :], proj[:, t, :]
            link(dve.tensor_scalar(out, src, param("ml_conv", 8 + t), None, ALU.mult))
            link(dve.scalar_tensor_tensor(out[:, 1:S], src[:, 0:S - 1], param("ml_conv", t), out[:, 1:S], ALU.mult, ALU.add))
            dve.scalar_tensor_tensor(out[:, 0:S - 1], src[:, 1:S], param("ml_conv", 16 + t), out[:, 0:S - 1],
                                     ALU.mult, ALU.add).then_inc(sem("ml_conv"), 1)
            if m % 2:
                low("w_in", 16 + n + GROUP)

        for h in range(4):
            if h < 3:
                ml_diff(h + 1)
            dve.wait_ge(*after("ml_masked", 4 * (h + 1)))
            den, e = small[:, 1, 0:4], eb[h % 2]
            for d in range(2):
                for qt in range(2):
                    j = 2 * d + qt
                    ins = dve.tensor_tensor_reduce(e[:, j, :], e[:, j, :], half(4 + h % 2, qt), float(P) ** -0.5, 0.0,
                                                   ALU.mult, ALU.add, den[:, j:j + 1])
            link(ins)
            link(dve.scalar_tensor_tensor(den, den, -1.0, den, ALU.mult, ALU.max))
            for d in range(2):
                r = h + 32 * d
                ins = dve.tensor_tensor(den[:, 2 * d:2 * d + 2].rearrange("p (a b) -> p a b", b=1),
                                        den[:, 2 * d:2 * d + 2].rearrange("p (a b) -> p a b", b=1),
                                        mcol[:, 1, :, r:r + 1], ALU.max)
            link(ins)
            link(dve.reciprocal(den, den))
            if h >= 1:
                dve.wait_ge(*after("ml_turned_p", h))
            for qt in range(2):
                ins = dve.tensor_scalar(wsum[:, qt, :], e[:, qt, :], den[:, qt:qt + 1], None, ALU.mult)
            link(ins)
            for qt in range(2):
                dve.scalar_tensor_tensor(wsum[:, qt, :], e[:, 2 + qt, :], den[:, 2 + qt:3 + qt], wsum[:, qt, :],
                                         ALU.mult, ALU.add).then_inc(sem("ml_w"), 1)
            for n in range(3 if h < 3 else 2):
                low("w_in", 20 + 3 * h + n + GROUP)
            dve.wait_ge(*after("ml_o", 1))
            dve.wait_ge(*after("ml_hsq", h + 1))
            dve.scalar_tensor_tensor(proj[:, h, :], half(7, 0), param("ml_norm", h), proj[:, 12 + h, :],
                                     ALU.mult, ALU.mult).then_inc(sem("ml_h"), 1)
        dve.wait_ge(*after("ml_root", 1))
        dve.reciprocal(rows[0:4, 0, :], rows[0:4, 0, :]).then_inc(sem("ml_root"), 1)
        dve.wait_ge(*after("ml_h", 4))
        for t in range(2):
            two = proj[:, 2 * t:2 * t + 2, :]
            dve.wait_ge(*after("ml_rms_bc", t + 1))
            dve.tensor_tensor(two, two, ps[:, 6 + t, :].rearrange("p (a b) -> p a b", a=2), ALU.mult
                              ).then_inc(sem("ml_rms"), 1)
        split("in6m", 4, lambda k: proj[:, k, :], base=8)
        low("w_in", 35)

        def na_logits(h):
            dve.wait_ge(*after("na_bias", h + 1))
            dve.scalar_tensor_tensor(flat(lg["na"][h % 2]), ps[:, 4 + h % 2, :], 64.0 ** -0.5, flat(bias[h % 2]),
                                     ALU.mult, ALU.add).then_inc(sem("na_logits"), 1)

        def xa_logits(h):
            dve.tensor_scalar(flat(lg["xa"][h % 2]), ps[:, 4 + h % 2, :], float(P) ** -0.5, None, ALU.mult
                              ).then_inc(sem("xa_logits"), 1)

        attention("na", 8, na_logits, lambda h: low_of("na", 12, h, 64), beside=lambda n: low("merge", n + GROUP))
        attention("xa", 4, xa_logits, lambda h: low_of("xa", 16, h, P), beside=lambda n: low("merge", 16 + n + GROUP))
        first = FIRST["branch"]
        for n in range(COUNT["branch"]):
            b, u = divmod(n, GROUP)
            dve.wait_ge(unit_done, first + n + 1)
            out = ps[:, u, :].rearrange("p (a b) -> p a b", a=2)
            dve.wait_ge(*after("gates", b + 1))
            gate = proj[:, 8 * b + 2 * u:8 * b + 2 * u + 2, :]
            dst = h_t[:, 2 * u:2 * u + 2, :]
            if b == 0:
                ins = dve.tensor_tensor(dst, gate, out, ALU.mult)
            else:
                ins = dve.tensor_tensor(gate, gate, out, ALU.mult)
            ins.then_inc(taken, 1)
            if b:
                dve.wait_ge(taken, all_taken("branch", n + 1))
                ins = dve.tensor_tensor(dst, dst, gate, ALU.add).then_inc(sem("merged"), 1)
            else:
                dve.sem_inc(sem("merged"), 1)
            low("branch", n + GROUP)
        split("in7", KT, h_tile)
        for n in range(KT):
            residual("w_out", n)
            low("w_out", n + GROUP)
        invert("ffn")
        for k in range(KT + 2):
            if k < KT:
                scaled(x_t, h_t, ("ffn_norm", 0), k, "ffn_h")
            if k >= 2:
                low_input("in8", k - 2, h_tile(k - 2))
        dve.wait_ge(*after("in8_lo", KT))
        for m in range(2):
            dve.memset(cin[m][:, 0:1], 0.0).then_inc(sem("edges"), 1)
            dve.memset(cin[m][:, 1 + S:2 + S], 0.0).then_inc(sem("edges"), 1)
        dve.wait_ge(*after("edges", GROUP + 4))
        dve.sem_inc(sem("ffn_pair_free"), 2)
        def ffn(i, base):
            first = FIRST["ffn_up"] + GROUP * base
            for m in range(2):
                dve.wait_ge(taken, i * GROUP + (GROUP + first + 2 * m + 1))
                conved = fbuf[m][:, 0, :]

                def tap(t):
                    return params[:, bass.ds(i * 2 + (PCOL["ffn_conv"] + FT * t + 2 * base + m), 1)]

                dve.tensor_scalar(conved, cin[m][:, 0:S], tap(0), None, ALU.mult).then_inc(sem("ffn_conv"), 1)
                for t in (1, 2):
                    dve.wait_ge(*after("ffn_conv", i * 6 + (6 * base + 3 * m + t)))
                    dve.scalar_tensor_tensor(conved, cin[m][:, t:t + S], tap(t), conved, ALU.mult, ALU.add
                                             ).then_inc(sem("ffn_conv"), 1)
                for u in (2 * m, 2 * m + 1):
                    dve.wait_ge(hi_done, i * GROUP + (first + u + GROUP + 1))
                    low_part(unit_at(LOADED["ffn_up"] + GROUP * (base + 1) + u, i, GROUP), u)
                if base:
                    dve.wait_ge(*after("in9_hi", i * 2 + (m + 1)))
                    at = bass.ds(i * 2 + (8 + m), 1)
                    dve.tensor_tensor(in_lo[:, at, :], proj[:, bass.ds(i * 2 + m, 1), :], in_hi[:, at, :].bitcast(F32),
                                      ALU.subtract).then_inc(sem("in9_lo"), 1)
                dve.wait_ge(*after("ffn_gelu", i * 2 + (2 * base + m + 1)))
                dve.wait_ge(taken, i * GROUP + (GROUP + first + 2 * m + 2))
                dve.tensor_tensor(proj[:, bass.ds(i * 2 + (2 * base + m), 1), :], fbuf[m][:, 0:1, :], fbuf[m][:, 1:2, :],
                                  ALU.mult).then_inc(sem("ffn_pair_free"), 1)

        with dve.Fori(0, 4) as i:
            ffn(i, 0)
        with dve.Fori(0, 7) as i:
            ffn(i, 4)
        for k in range(14, FT):
            dve.wait_ge(*after("in9_hi", k + 1))
            dve.tensor_tensor(in_lo[:, k - 14, :], proj[:, k, :], in_hi[:, k - 14, :].bitcast(F32), ALU.subtract
                              ).then_inc(sem("in9_lo"), 1)
        first = FIRST["ffn_down"]
        for n in range(COUNT["ffn_down"]):
            if n % 3 == 2:
                residual("ffn_down", n // 3, unit=n)
            if first + n + GROUP < UNITS:
                low("ffn_down", n + GROUP)
        invert("final")
        for k in range(KT):
            scaled(x_t, proj, ("final_norm", 0), k, "final_done")

    @block.gpsimd
    def _(pool):
        pool.wait_ge(*after("in0_lo", KT))
        pool.memset(acc[:], 0.0).then_inc(sem("acc_zero"), 1)
        pool.wait_ge(*after("h0", KT))
        pool.tensor_scalar(x_t[:], x_t[:], ALPHA, None, ALU.mult).then_inc(sem("x_alpha"), 1)

        def total(tag, src, ready):
            for k in range(1, KT):
                pool.wait_ge(*ready(k))
                if k == 1:
                    ins = pool.tensor_tensor(stat[:, 0, :], src[:, 0, :], src[:, 1, :], ALU.add)
                else:
                    pool.wait_ge(*after(f"{tag}_total", k - 1))
                    ins = pool.tensor_tensor(stat[:, 0, :], stat[:, 0, :], src[:, k, :], ALU.add)
                ins.then_inc(sem(f"{tag}_total"), 1)

        pool.wait_ge(*after("masks_in", 16))
        total("ln0", x_t, lambda k: (taken, all_taken("moba_out", k + 1)))
        pool.wait_ge(*after("gdn_unit", 8))
        for sg in range(2):
            for p in range(2):
                g = 2 * sg + p
                for m in range(2):
                    pool.wait_ge(*after("gdn_qe", 2 * g + m + 1))
                    ins = pool.tensor_tensor(qg[:, 2 * p + m, :], qg[:, 2 * p + m, :], proj[:, 2 * g + m, P:S], ALU.mult)
                ins.then_inc(sem("gdn_qg"), 1)
            for lv in range(LEVELS):
                for p in range(2):
                    g, n = 2 * sg + p, (sg * LEVELS + lv) * 2 + p
                    if lv == 0:
                        pool.wait_ge(*after("gdn_lt", g + 1))
                        if sg:
                            pool.wait_ge(*after("gdn_ot", 2 * sg))
                    elif lv == 1:
                        pool.wait_ge(*after("gdn_t", n - 1))
                    else:
                        pool.wait_ge(*after("gdn_p", n - 1))
                    a = CCOL["level"] + lv * P
                    mask = consts[:, a:a + P].rearrange("p (a b) -> p a b", a=1).to_broadcast([P, 4, P])
                    pool.tensor_tensor(ctm[p], lt[p], mask, ALU.mult).then_inc(sem("gdn_ct"), 1)
                    if lv == 0:
                        pool.wait_ge(*after("gdn_a0", g + 1))
                        incl = consts[:, CCOL["bw"] + P:CCOL["bw"] + 2 * P].rearrange(
                            "p (a b) -> p a b", a=1).to_broadcast([P, 4, P])
                        pool.tensor_tensor(aqk[p], aqk[p], incl, ALU.mult).then_inc(sem("gdn_aqk"), 1)
        pool.wait_ge(*after("gdn_p", 4 * LEVELS))
        pool.dma_start(proj[:, 8:16, :], io["mem_t"]).then_inc(sem("mem_in"), 16)
        total("ln1", x_t, lambda k: (taken, all_taken("gdn_out", k + 1)))
        for h in range(4):
            pool.wait_ge(*after("ml_exp", h + 1))
            for d, name in enumerate(("fw", "bw")):
                for qt in range(2):
                    e = eb[h % 2][:, 2 * d + qt, :]
                    pool.tensor_tensor(e, e, strip(name, qt), ALU.mult
                                       ).then_inc(sem("ml_masked"), 1)
        pool.wait_ge(*after("ml_hsum", 1))
        for h in range(8):
            if h >= 2:
                pool.wait_ge(*after("na_logits", h - 1))
            pool.dma_start(bias[h % 2], io["na_bias"][h]).then_inc(sem("na_bias_in"), 16)
            pool.wait_ge(*after("na_bias_in", 16 * (h + 1)))
            mask = consts[:, CCOL["colmask"]:CCOL["colmask"] + S].rearrange("p (a b) -> p a b", a=1).to_broadcast([P, 2, S])
            pool.tensor_tensor(bias[h % 2], bias[h % 2], mask, ALU.add).then_inc(sem("na_bias"), 1)
        total("ffn", sq, lambda k: after("ffn_sq", k + 1))
        total("final", sq, lambda k: after("final_sq", k + 1))


def _constants():
    i, j = np.meshgrid(np.arange(P), np.arange(P), indexing="ij")
    one, zero = np.ones((P, P)), np.zeros((P, P))
    out = {
        "ident": np.eye(P),
        "fw": np.hstack([one, j <= i, zero]),
        "bw": np.hstack([zero, j >= i, one]),
        "neg": np.hstack([zero, np.where(j <= i, 0.0, NEG), NEG * one]),
        "pick": np.tile(np.arange(31) == 15, (P, 1)),
        "level": np.hstack([(i // (2 * s) == j // (2 * s)) & ((i // s) % 2 == 0) & ((j // s) % 2 == 1)
                            for s in (2 ** n for n in range(LEVELS))]),
    }
    c, w = np.arange(64), 16
    start = np.clip(c - w // 2, 0, 64 - w)
    ok = (c[None, :] >= start[:, None]) & (c[None, :] < start[:, None] + w)
    out["colmask"] = np.tile(np.where(ok, 0.0, NEG), (2, 4))
    return np.ascontiguousarray(np.hstack([out[n] for n, _ in CONSTS]).astype(np.float32))


def _pairs(blocks):
    u = blocks.shape[0]
    return np.ascontiguousarray(blocks.reshape(u // PAIR, PAIR * UNIT, P, P).transpose(0, 2, 1, 3)
                                .reshape(u // PAIR, P, PAIR * UNIT * P))


def _by_output(w):
    n = w.shape[1] // P
    return w.reshape(KT, P, n, P).transpose(2, 0, 1, 3)


def _tiles(a):
    return np.ascontiguousarray(a.T.reshape(-1, P, S).transpose(1, 0, 2))


def _columns(v):
    return np.asarray(v).reshape(-1, P).T


def _rows(v, at):
    out = np.zeros((P, 1), np.float32)
    for part, a in zip(v, at):
        out[a:a + len(part), 0] = part
    return out


def kernel(**inputs):
    import concourse.bacc as bacc
    from concourse.bass_utils import run_bass_kernel_spmd

    t = {k: np.asarray(v) for k, v in inputs.items()}
    a = {}
    w_in = t["w_in_2"][0]
    gdn = t["gdn_w_in"][0]
    a["ada"] = np.ascontiguousarray(t["ada_w"].reshape(2, KT, P, 3, D).transpose(0, 3, 1, 2, 4)
                                    .reshape(ADA // PAIR, PAIR, P, D).transpose(0, 2, 1, 3)
                                    .reshape(ADA // PAIR, P, PAIR * D))
    moba = t["moba_w_in"][0]
    a["moba_in"] = _pairs(_by_output(np.concatenate([moba[:, :2048], moba[:, 3072:], moba[:, 2048:3072]], 1)))
    a["moba_out"] = _pairs(_by_output(t["moba_w_out"][0]))
    a["gdn_in"] = _pairs(_by_output(gdn[:, :4096]))
    a["gdn_out"] = _pairs(_by_output(t["gdn_w_out"][0]))
    a["mem_kv"] = _pairs(_by_output(t["w_mem_kv_2"][0]))
    a["w_in"] = _pairs(_by_output(np.concatenate([w_in[:, :2048], w_in[:, 2064:4112]], 1)))
    a["merge"] = _pairs(_by_output(w_in[:, 4112:]))
    a["branch"] = _pairs(np.concatenate([
        t[n][0].reshape(4, P, 8, P).transpose(2, 0, 1, 3).reshape(4, 8, P, P)
        for n in ("w_br_ml_2", "w_br_na_2", "w_br_xa_2")]))
    a["w_out"] = _pairs(_by_output(t["w_out_2"][0]))
    up = _by_output(t["w_ffn_up_2"][0])
    a["ffn_up"] = _pairs(np.stack([up[:FT], up[FT:]], 1).reshape(2 * FT, KT, P, P))
    down = t["w_ffn_down_2"][0].reshape(FT, P, KT, P).transpose(2, 0, 1, 3)
    a["ffn_down"] = _pairs(np.concatenate([down, np.zeros((KT, 2, P, P), np.float32)], 1).reshape(24, UNIT, P, P))
    a["x_t"] = _tiles(t["x"][0])
    a["mem_t"] = _tiles(t["mem_2"][0])
    wide = np.zeros((D, 40), np.float32)
    wide[:, 0:8], wide[:, 32:40] = gdn[:, 4096:4104], gdn[:, 4104:4112]
    a["gdn_wg"] = np.ascontiguousarray(wide.reshape(KT, P, 40).transpose(1, 0, 2))
    gates = w_in[:, 2048:2064]
    wide = np.zeros((D, 64 + ML_ROWS), np.float32)
    wide[:, 0:4], wide[:, 32:36] = gates[:, 0:4], gates[:, 8:12]
    wide[:, 64:68], wide[:, 96:100] = gates[:, 4:8], gates[:, 12:16]
    a["ml_wg"] = np.ascontiguousarray(wide.reshape(KT, P, 64 + ML_ROWS).transpose(1, 0, 2))
    rpb = t["na_rpb_2"][0]
    q = np.arange(S)
    r, c = q // 64, q % 64
    dr = r[None, :] - r[:, None] + 7
    dc = np.clip(c[None, :] - c[:, None] + 15, 0, 30)
    a["na_bias"] = np.ascontiguousarray(rpb[:, dr, dc].reshape(8, 2, P, S).transpose(0, 2, 1, 3))
    named = {
        "c": t["c"], "ada_b": t["ada_b"], "ln_g": t["ln_g"], "ln_b": t["ln_b"], "gdn_conv": t["gdn_conv_w"][0],
        "gdn_norm": t["gdn_norm_w"], "ml_conv": t["w_ml_conv_2"][0], "ml_conv_b": t["b_ml_conv_2"],
        "ml_norm": t["ml_norm_g_2"], "mix_norm": t["mix_norm_g_2"], "mem_norm": t["mem_norm_g_2"],
        "merge_b": t["b_merge_gate_2"], "ffn_norm": t["ffn_norm_g_2"], "ffn_conv": t["w_ffn_conv_2"][0],
        "ffn_conv_b": t["b_ffn_conv_2"], "final_norm": t["final_norm_g_2"],
    }
    rows_ = {"a_log": _rows([t["gdn_a_log"][0]], [0]), "dt_bias": _rows([t["gdn_dt_bias"][0]], [0]),
             "b_ig": _rows(t["b_ml_igate_2"][0], [0, 32]), "b_fg": _rows(t["b_ml_fgate_2"][0], [0, 32])}
    a["params"] = np.ascontiguousarray(np.hstack([_columns(named[n]) if n in named else rows_[n] for n, _ in PARAMS]))
    a["consts"] = _constants()

    nc = bacc.Bacc("TRN2", target_bir_lowering=False, num_devices=1)
    io = {n: nc.dram_tensor(f"in_{n}", v.shape, F32, kind="ExternalInput").ap() for n, v in a.items()}
    io["out"] = nc.dram_tensor("out_t", (P, KT, S), F32, kind="ExternalOutput").ap()
    build(nc, io)
    r = run_bass_kernel_spmd(nc, [{f"in_{n}": v for n, v in a.items()}], core_ids=[0])
    out = r.results[0]["out_t"]
    return np.ascontiguousarray(out.transpose(1, 0, 2).reshape(D, S).T)[None]
```
